# Optimizing a Trainium2 kernel written in Bass

```python
import math
import jax
import jax.numpy as jnp
from jax import lax
import numpy as np
import jax, jax.numpy as jnp

D_MODEL = 1024
BATCH = 1
SEQ = 512
DEPTH = 1

EPS = 1e-6
NEG_INF = -1e30
DN_HEADS = 4
DN_DK = 128
DN_DV = 128
DN_KEY_W = DN_HEADS * DN_DK
DN_VAL_W = DN_HEADS * DN_DV
DN_CONV = 4
DN_CHUNK = 64
N_DIR = 2
DA_GROUPS = ((128, 1), (512, 4), (2048, 16))
DA_HEADS = 4
DA_HD = 128
DA_W = len(DA_GROUPS) * DA_HEADS * DA_HD
RP_BUCKETS = 32
RP_MAX_DIST = 1024
PEER_HEADS = 8
PEER_NKEYS = 128
PEER_QDIM = 256
PEER_TOPK = 16
PEER_EXPERTS = PEER_NKEYS * PEER_NKEYS
PEER_TOKEN_BLOCK = 128

IN_WIDTHS = (DN_KEY_W, DN_KEY_W, DN_VAL_W, DN_VAL_W, N_DIR * DN_HEADS, N_DIR * DN_HEADS,
             DA_W, DA_W, DA_W, D_MODEL, D_MODEL)


def rmsnorm(x, g):
    xf = x.astype(jnp.float32)
    y = xf * lax.rsqrt(jnp.mean(xf * xf, axis=-1, keepdims=True) + EPS)
    return (y * g.astype(jnp.float32)).astype(x.dtype)

def l2norm(x):
    return x * lax.rsqrt(jnp.sum(x * x, axis=-1, keepdims=True) + EPS)

def split_columns(t, widths):
    out, start = [], 0
    for w in widths:
        out.append(t[..., start:start + w])
        start += w
    return out

def centred_depthwise_conv(x, w):
    k, c = w.shape
    left = k // 2
    return lax.conv_general_dilated(x, w[:, None, :], window_strides=(1,), padding=[(left, k - 1 - left)],
                                    dimension_numbers=('NWC', 'WIO', 'NWC'), feature_group_count=c)

def gated_delta_rule(q, k, v, g, beta):
    r, s, dk = q.shape
    dv = v.shape[-1]
    c = DN_CHUNK
    n = s // c
    q = (q * (dk ** -0.5)).reshape(r, n, c, dk)
    k = k.reshape(r, n, c, dk)
    v = v.reshape(r, n, c, dv)
    beta = beta.reshape(r, n, c)
    gcum = jnp.cumsum(g.reshape(r, n, c), axis=-1)
    diff = gcum[..., :, None] - gcum[..., None, :]
    lower = jnp.tril(jnp.ones((c, c), dtype=bool))
    strict = jnp.tril(jnp.ones((c, c), dtype=bool), -1)
    decay = jnp.where(lower, jnp.exp(jnp.where(lower, diff, 0.0)), 0.0)
    kb = k * beta[..., None]
    lmat = jnp.where(strict, jnp.einsum('rnid,rnjd->rnij', kb, k) * decay, 0.0)
    amat = jnp.eye(c, dtype=jnp.float32) + lmat
    rhs = jnp.concatenate([v * beta[..., None], kb * jnp.exp(gcum)[..., None]], axis=-1)
    sol = lax.linalg.triangular_solve(amat, rhs, left_side=True, lower=True, unit_diagonal=True)
    u, w = sol[..., :dv], sol[..., dv:]
    intra = jnp.einsum('rnid,rnjd->rnij', q, k) * decay
    q_dec = q * jnp.exp(gcum)[..., None]
    k_dec = k * jnp.exp(gcum[..., -1:] - gcum)[..., None]
    g_last = jnp.exp(gcum[..., -1])

    def step(state, inp):
        u_i, w_i, intra_i, qd_i, kd_i, gl_i = inp
        v_new = u_i - jnp.einsum('rcd,rde->rce', w_i, state)
        out = jnp.einsum('rcd,rde->rce', qd_i, state) + jnp.einsum('rij,rje->rie', intra_i, v_new)
        state = state * gl_i[:, None, None] + jnp.einsum('rcd,rce->rde', kd_i, v_new)
        return state, out

    xs = tuple(jnp.moveaxis(a, 1, 0) for a in (u, w, intra, q_dec, k_dec, g_last))
    _, out = lax.scan(step, jnp.zeros((r, dk, dv), jnp.float32), xs)
    return jnp.moveaxis(out, 0, 1).reshape(r, s, dv)

def deltanet_branch(q, k, v, z, a, b, conv_w, a_log, dt_bias, out_norm):
    bsz, s, _ = q.shape
    f32 = jnp.float32
    qkv = jax.nn.silu(centred_depthwise_conv(jnp.concatenate([q, k, v], axis=-1), conv_w))
    q, k, v = split_columns(qkv, (DN_KEY_W, DN_KEY_W, DN_VAL_W))

    def heads(t, d):
        return t.reshape(bsz, s, DN_HEADS, d).transpose(0, 2, 1, 3).astype(f32)

    def per_dir(t):
        return t.reshape(bsz, s, N_DIR, DN_HEADS).transpose(2, 0, 3, 1).astype(f32)

    q, k, v = l2norm(heads(q, DN_DK)), l2norm(heads(k, DN_DK)), heads(v, DN_DV)
    g = -jnp.exp(a_log.astype(f32))[:, None, :, None] * jax.nn.softplus(per_dir(a) + dt_bias.astype(f32)[:, None, :, None])
    beta = jax.nn.sigmoid(per_dir(b))
    qs = jnp.stack([q, jnp.flip(q, 2)])
    ks = jnp.stack([k, jnp.flip(k, 2)])
    vs = jnp.stack([v, jnp.flip(v, 2)])
    gs = jnp.stack([g[0], jnp.flip(g[1], -1)])
    bs = jnp.stack([beta[0], jnp.flip(beta[1], -1)])
    rows = N_DIR * bsz * DN_HEADS
    o = gated_delta_rule(qs.reshape(rows, s, DN_DK), ks.reshape(rows, s, DN_DK), vs.reshape(rows, s, DN_DV),
                         gs.reshape(rows, s), bs.reshape(rows, s)).reshape(N_DIR, bsz, DN_HEADS, s, DN_DV)
    o = (o[0] + jnp.flip(o[1], 2)).transpose(0, 2, 1, 3)
    o = rmsnorm(o, out_norm) * jax.nn.silu(z.reshape(bsz, s, DN_HEADS, DN_DV).astype(f32))
    return o.reshape(bsz, s, DN_VAL_W)

def t5_bucket(rel):
    half = RP_BUCKETS // 2
    max_exact = half // 2
    n = np.abs(rel)
    large = max_exact + (np.log(np.maximum(n, 1) / max_exact) / math.log(RP_MAX_DIST / max_exact)
                         * (half - max_exact)).astype(np.int64)
    large = np.minimum(large, half - 1)
    return np.where(rel > 0, half, 0) + np.where(n < max_exact, n, large)

def dilated_group_attention(q, k, v, bias_table, window, dil):
    bsz, h, s, hd = q.shape
    side = window // (2 * dil)
    length = s // dil
    nb = -(-length // side)
    padded = nb * side

    def residue_blocks(t):
        t = t.reshape(bsz, h, length, dil, hd).transpose(0, 1, 3, 2, 4)
        t = jnp.pad(t, ((0, 0), (0, 0), (0, 0), (0, padded - length), (0, 0)))
        return t.reshape(bsz, h, dil, nb, side, hd)

    def with_neighbours(t):
        tp = jnp.pad(t, ((0, 0), (0, 0), (0, 0), (1, 1), (0, 0), (0, 0)))
        return jnp.concatenate([tp[:, :, :, :-2], tp[:, :, :, 1:-1], tp[:, :, :, 2:]], axis=4)

    qb = residue_blocks(q)
    kn = with_neighbours(residue_blocks(k))
    vn = with_neighbours(residue_blocks(v)).astype(jnp.float32)
    rel = np.arange(3 * side)[None, :] - side - np.arange(side)[:, None]
    key_idx = np.arange(nb)[:, None, None] * side + np.arange(3 * side)[None, None, :] - side
    valid = (np.abs(rel) <= side)[None] & (key_idx >= 0) & (key_idx < length)
    bias = bias_table.astype(jnp.float32)[:, t5_bucket(rel * dil)]
    scores = jnp.einsum('bhrnqd,bhrnkd->bhrnqk', qb, kn, preferred_element_type=jnp.float32) * (hd ** -0.5)
    scores = jnp.where(valid, scores + bias[None, :, None, None], NEG_INF)
    m = jnp.max(scores, axis=-1, keepdims=True)
    p = jnp.exp(scores - m)
    l = jnp.sum(p, axis=-1)
    o = jnp.einsum('bhrnqk,bhrnkd->bhrnqd', p, vn) / l[..., None]
    lse = m[..., 0] + jnp.log(l)
    o = o.reshape(bsz, h, dil, padded, hd)[:, :, :, :length].transpose(0, 1, 3, 2, 4).reshape(bsz, h, s, hd)
    lse = lse.reshape(bsz, h, dil, padded)[..., :length].transpose(0, 1, 3, 2).reshape(bsz, h, s)
    return o, lse

def dilated_attention_branch(q, k, v, rel_bias):
    bsz, s, _ = q.shape

    def groups(t):
        return t.reshape(bsz, s, len(DA_GROUPS), DA_HEADS, DA_HD).transpose(2, 0, 3, 1, 4)

    qg, kg, vg = groups(q), groups(k), groups(v)
    outs, lses = [], []
    for gi, (window, dil) in enumerate(DA_GROUPS):
        table = rel_bias[:, gi * DA_HEADS:(gi + 1) * DA_HEADS].T
        o, lse = dilated_group_attention(qg[gi], kg[gi], vg[gi], table, window, dil)
        outs.append(o)
        lses.append(lse)
    wts = jax.nn.softmax(jnp.stack(lses), axis=0)
    o = jnp.einsum('gbhs,gbhsd->bhsd', wts, jnp.stack(outs))
    return o.transpose(0, 2, 1, 3).reshape(bsz, s, DA_HEADS * DA_HD)

def peer_ffn(xn, w_q, sub_keys, expert_u, expert_v):
    bsz, s, d = xn.shape
    t = bsz * s
    x2 = xn.reshape(t, d)
    qh = (x2 @ w_q).reshape(t, PEER_HEADS, 2, PEER_QDIM // 2)
    scores = jnp.einsum('thcd,hckd->thck', qh, sub_keys, preferred_element_type=jnp.float32)
    sv, si = lax.top_k(scores, PEER_TOPK)
    cand = sv[..., 0, :, None] + sv[..., 1, None, :]
    cv, ci = lax.top_k(cand.reshape(t, PEER_HEADS, PEER_TOPK * PEER_TOPK), PEER_TOPK)
    i1 = jnp.take_along_axis(si[..., 0, :], ci // PEER_TOPK, axis=-1)
    i2 = jnp.take_along_axis(si[..., 1, :], ci % PEER_TOPK, axis=-1)
    experts = (i1 * PEER_NKEYS + i2).reshape(t, PEER_HEADS * PEER_TOPK)
    gates = jax.nn.softmax(cv, axis=-1).reshape(t, PEER_HEADS * PEER_TOPK)

    def token_block(args):
        xb, eb, gb = args
        act = jax.nn.gelu(jnp.einsum('tkd,td->tk', expert_u[eb], xb, preferred_element_type=jnp.float32))
        return jnp.einsum('tk,tkd->td', act * gb, expert_v[eb].astype(jnp.float32)).astype(xb.dtype)

    nblk = t // PEER_TOKEN_BLOCK
    out = lax.map(token_block, (x2.reshape(nblk, PEER_TOKEN_BLOCK, d),
                                experts.reshape(nblk, PEER_TOKEN_BLOCK, -1),
                                gates.reshape(nblk, PEER_TOKEN_BLOCK, -1)))
    return out.reshape(bsz, s, d)

def first_inputs(seed: int = 0) -> dict:
    key = jax.random.key(seed)
    ks = jax.random.split(key, 18)
    f32 = jnp.float32

    def normal(k, shape, scale):
        return jax.random.normal(k, shape, f32) * scale

    dt = jnp.exp(jax.random.uniform(ks[5], (DEPTH, N_DIR, DN_HEADS), f32, math.log(1e-3), math.log(1e-1)))
    return {
        'x': normal(ks[0], (BATCH, SEQ, D_MODEL), 1.0),
        'norm_mix': 1.0 + normal(ks[1], (DEPTH, D_MODEL), 0.02),
        'w_in': normal(ks[2], (DEPTH, D_MODEL, sum(IN_WIDTHS)), D_MODEL ** -0.5),
        'dn_conv': normal(ks[3], (DEPTH, DN_CONV, 2 * DN_KEY_W + DN_VAL_W), DN_CONV ** -0.5),
        'dn_a_log': jnp.log(jax.random.uniform(ks[4], (DEPTH, N_DIR, DN_HEADS), f32, 1.0, 16.0)),
        'dn_dt_bias': dt + jnp.log(-jnp.expm1(-dt)),
        'dn_out_norm': 1.0 + normal(ks[6], (DEPTH, DN_DV), 0.02),
        'rel_bias': normal(ks[7], (RP_BUCKETS, len(DA_GROUPS) * DA_HEADS), 0.2),
        'w_branch_dn': normal(ks[8], (DEPTH, DN_VAL_W, D_MODEL), DN_VAL_W ** -0.5),
        'w_branch_da': normal(ks[9], (DEPTH, DA_HEADS * DA_HD, D_MODEL), (DA_HEADS * DA_HD) ** -0.5),
        'w_out': normal(ks[10], (DEPTH, D_MODEL, D_MODEL), D_MODEL ** -0.5),
        'norm_ffn': 1.0 + normal(ks[11], (DEPTH, D_MODEL), 0.02),
        'peer_wq': normal(ks[12], (DEPTH, D_MODEL, PEER_HEADS * PEER_QDIM), D_MODEL ** -0.5),
        'peer_sub_keys': normal(ks[13], (DEPTH, PEER_HEADS, 2, PEER_NKEYS, PEER_QDIM // 2), (PEER_QDIM // 2) ** -0.5),
        'peer_u': normal(ks[14], (DEPTH, PEER_EXPERTS, D_MODEL), D_MODEL ** -0.5),
        'peer_v': normal(ks[15], (DEPTH, PEER_EXPERTS, D_MODEL), PEER_HEADS ** -0.5),
        'norm_final': 1.0 + normal(ks[16], (D_MODEL,), 0.02),
    }

def first_block(x, norm_mix, w_in, dn_conv, dn_a_log, dn_dt_bias, dn_out_norm, rel_bias, w_branch_dn,
              w_branch_da, w_out, norm_ffn, peer_wq, peer_sub_keys, peer_u, peer_v, norm_final):
    h = x
    for layer in range(DEPTH):
        xn = rmsnorm(h, norm_mix[layer])
        (dq, dk, dv, dz, da, db, aq, ak, av, gate_dn, gate_da) = split_columns(xn @ w_in[layer], IN_WIDTHS)
        o_dn = deltanet_branch(dq, dk, dv, dz, da, db, dn_conv[layer], dn_a_log[layer], dn_dt_bias[layer],
                               dn_out_norm[layer]).astype(h.dtype)
        o_da = dilated_attention_branch(aq, ak, av, rel_bias).astype(h.dtype)
        merged = (jax.nn.sigmoid(gate_dn) * (o_dn @ w_branch_dn[layer])
                  + jax.nn.sigmoid(gate_da) * (o_da @ w_branch_da[layer]))
        h = h + merged @ w_out[layer]
        h = h + peer_ffn(rmsnorm(h, norm_ffn[layer]), peer_wq[layer], peer_sub_keys[layer],
                         peer_u[layer], peer_v[layer])
    return rmsnorm(h, norm_final)


DEPTH_2 = 2

BLOCK = 128
ROPE_BASE = 10000.0

MLA_HEADS = 8
MLA_NOPE = 64
MLA_ROPE = 32
MLA_V = 64
MLA_Q_RANK = 384
MLA_KV_RANK = 256
SB_HEADS = 8
SB_DIM = 64
RET_HEADS = 8
RET_DK = 64
RET_DV = 64

BRANCH_WIDTH = 512
N_BRANCH = 3
D_FF = 4 * D_MODEL

IN_SIZES = (MLA_Q_RANK, MLA_KV_RANK, MLA_ROPE,
            SB_HEADS * SB_DIM, SB_HEADS * SB_DIM, SB_HEADS * SB_DIM,
            RET_HEADS * RET_DK, RET_HEADS * RET_DK, RET_HEADS * RET_DV, RET_HEADS * RET_DV,
            N_BRANCH * D_MODEL)
D_IN = sum(IN_SIZES)


def rmsnorm_2(x, g):
    xf = x.astype(jnp.float32)
    y = xf * lax.rsqrt(jnp.mean(xf * xf, axis=-1, keepdims=True) + EPS)
    return (y * g.astype(jnp.float32)).astype(x.dtype)

def head_group_norm(y, g):
    yf = y.astype(jnp.float32)
    mu = jnp.mean(yf, axis=-1, keepdims=True)
    var = jnp.mean(jnp.square(yf - mu), axis=-1, keepdims=True)
    yn = ((yf - mu) * lax.rsqrt(var + EPS)).reshape(y.shape[0], y.shape[1], -1)
    return (yn * g.astype(jnp.float32)).astype(y.dtype)

def rope_tables(positions, dim):
    inv_freq = ROPE_BASE ** (-jnp.arange(0, dim, 2, dtype=jnp.float32) / dim)
    ang = positions.astype(jnp.float32)[..., None] * inv_freq
    return jnp.cos(ang)[:, :, None, :], jnp.sin(ang)[:, :, None, :]

def apply_rope(x, cos, sin):
    half = x.shape[-1] // 2
    xf = x.astype(jnp.float32)
    x1, x2 = xf[..., :half], xf[..., half:]
    return jnp.concatenate([x1 * cos - x2 * sin, x2 * cos + x1 * sin], axis=-1).astype(x.dtype)

def causal_softmax_attention(q, k, v, scale):
    S = q.shape[1]
    outs = []
    for start in range(0, S, BLOCK):
        end = start + BLOCK
        s = jnp.einsum('bqhd,bkhd->bhqk', q[:, start:end], k[:, :end]).astype(jnp.float32) * scale
        t_idx = start + jnp.arange(BLOCK)[:, None]
        s_idx = jnp.arange(end)[None, :]
        s = jnp.where(s_idx <= t_idx, s, -jnp.inf)
        p = jax.nn.softmax(s, axis=-1)
        outs.append(jnp.einsum('bhqk,bkhd->bqhd', p.astype(v.dtype), v[:, :end]))
    return jnp.concatenate(outs, axis=1)

def stick_breaking_attention(q, k, v):
    S = q.shape[1]
    scale = SB_DIM ** -0.5
    outs = []
    for start in range(0, S, BLOCK):
        end = start + BLOCK
        z = jnp.einsum('bqhd,bkhd->bhqk', q[:, start:end], k[:, :end]).astype(jnp.float32) * scale
        t_idx = start + jnp.arange(BLOCK)[:, None]
        s_idx = jnp.arange(end)[None, :]
        before = s_idx < t_idx
        log_not = jnp.where(before, jax.nn.log_sigmoid(-z), 0.0)
        between = lax.cumsum(log_not, axis=3, reverse=True) - log_not
        a = jnp.where(before, jnp.exp(jax.nn.log_sigmoid(z) + between), 0.0)
        outs.append(jnp.einsum('bhqk,bkhd->bqhd', a.astype(v.dtype), v[:, :end]))
    return jnp.concatenate(outs, axis=1)

def retention(q, k, v, log_gamma):
    B, S, H, dk = q.shape
    dv = v.shape[-1]
    C = BLOCK
    N = S // C
    qc = q.astype(jnp.float32).reshape(B, N, C, H, dk)
    kc = (k.astype(jnp.float32) * dk ** -0.5).reshape(B, N, C, H, dk)
    vc = v.astype(jnp.float32).reshape(B, N, C, H, dv)
    idx = jnp.arange(C, dtype=jnp.float32)
    diff = idx[:, None] - idx[None, :]
    intra_decay = jnp.where(diff[None] >= 0,
                            jnp.exp(jnp.maximum(diff, 0.0)[None] * log_gamma[:, None, None]), 0.0)
    scores = jnp.einsum('bnchd,bnmhd->bnhcm', qc, kc) * intra_decay
    y_intra = jnp.einsum('bnhcm,bnmhe->bnche', scores, vc)
    zeta = jnp.exp((C - 1 - idx)[:, None] * log_gamma[None, :])
    kv = jnp.einsum('bnchd,bnche->nbhde', kc * zeta[None, None, :, :, None], vc)
    chunk_decay = jnp.exp(C * log_gamma)[None, :, None, None]

    def step(state, kv_n):
        return state * chunk_decay + kv_n, state

    _, prev = lax.scan(step, jnp.zeros((B, H, dk, dv), jnp.float32), kv)
    xi = jnp.exp((idx + 1.0)[:, None] * log_gamma[None, :])
    y_cross = jnp.einsum('bnchd,nbhde->bnche', qc, prev) * xi[None, None, :, :, None]
    return (y_intra + y_cross).reshape(B, S, H, dv).astype(v.dtype)

def second_inputs(seed: int = 0) -> dict:
    key = jax.random.key(seed)
    ks = jax.random.split(key, 16)
    f32 = jnp.float32

    def dense(k, shape, fan_in):
        return jax.random.normal(k, shape, f32) * fan_in ** -0.5

    def gain(k, shape):
        return 1.0 + 0.02 * jax.random.normal(k, shape, f32)

    x = jax.random.normal(ks[0], (BATCH, SEQ, D_MODEL), f32)
    offset = jax.random.randint(ks[1], (BATCH, 1), 0, 1024, dtype=jnp.int32)
    positions = offset + jnp.arange(SEQ, dtype=jnp.int32)[None, :]
    return {
        "x": x,
        "positions": positions,
        "norm_mix_g": gain(ks[2], (DEPTH_2, D_MODEL)),
        "w_in": dense(ks[3], (DEPTH_2, D_MODEL, D_IN), D_MODEL),
        "mla_q_norm_g": gain(ks[4], (DEPTH_2, MLA_Q_RANK)),
        "mla_w_uq": dense(ks[5], (DEPTH_2, MLA_Q_RANK, MLA_HEADS * (MLA_NOPE + MLA_ROPE)), MLA_Q_RANK),
        "mla_kv_norm_g": gain(ks[6], (DEPTH_2, MLA_KV_RANK)),
        "mla_w_ukv": dense(ks[7], (DEPTH_2, MLA_KV_RANK, MLA_HEADS * (MLA_NOPE + MLA_V)), MLA_KV_RANK),
        "ret_norm_g": gain(ks[8], (DEPTH_2, RET_HEADS * RET_DV)),
        "w_branch": dense(ks[9], (DEPTH_2, N_BRANCH, BRANCH_WIDTH, D_MODEL), BRANCH_WIDTH),
        "w_out": dense(ks[10], (DEPTH_2, D_MODEL, D_MODEL), D_MODEL),
        "norm_mlp_g": gain(ks[11], (DEPTH_2, D_MODEL)),
        "w_up": dense(ks[12], (DEPTH_2, D_MODEL, D_FF), D_MODEL),
        "w_down": dense(ks[13], (DEPTH_2, D_FF, D_MODEL), D_FF),
        "final_norm_g": gain(ks[14], (D_MODEL,)),
    }

def second_block(x, positions, norm_mix_g, w_in, mla_q_norm_g, mla_w_uq, mla_kv_norm_g, mla_w_ukv,
              ret_norm_g, w_branch, w_out, norm_mlp_g, w_up, w_down, final_norm_g):
    B, S, _ = x.shape
    cos_m, sin_m = rope_tables(positions, MLA_ROPE)
    cos_r, sin_r = rope_tables(positions, RET_DK)
    log_gamma = jnp.log1p(-jnp.exp2(-5.0 - jnp.arange(RET_HEADS, dtype=jnp.float32)))
    splits = [int(v) for v in np.cumsum(IN_SIZES)[:-1]]

    for l in range(DEPTH_2):
        h = rmsnorm_2(x, norm_mix_g[l])
        proj = h @ w_in[l]
        (c_q, c_kv, k_pe, sb_q, sb_k, sb_v, r_q, r_k, r_v, r_g, gate_logits) = jnp.split(proj, splits, axis=-1)

        q = (rmsnorm_2(c_q, mla_q_norm_g[l]) @ mla_w_uq[l]).reshape(B, S, MLA_HEADS, MLA_NOPE + MLA_ROPE)
        kv = (rmsnorm_2(c_kv, mla_kv_norm_g[l]) @ mla_w_ukv[l]).reshape(B, S, MLA_HEADS, MLA_NOPE + MLA_V)
        k_rot = jnp.broadcast_to(apply_rope(k_pe[:, :, None, :], cos_m, sin_m), (B, S, MLA_HEADS, MLA_ROPE))
        q_a = jnp.concatenate([q[..., :MLA_NOPE], apply_rope(q[..., MLA_NOPE:], cos_m, sin_m)], axis=-1)
        k_a = jnp.concatenate([kv[..., :MLA_NOPE], k_rot], axis=-1)
        y_a = causal_softmax_attention(q_a, k_a, kv[..., MLA_NOPE:], (MLA_NOPE + MLA_ROPE) ** -0.5).reshape(B, S, -1)

        y_b = stick_breaking_attention(sb_q.reshape(B, S, SB_HEADS, SB_DIM),
                                       sb_k.reshape(B, S, SB_HEADS, SB_DIM),
                                       sb_v.reshape(B, S, SB_HEADS, SB_DIM)).reshape(B, S, -1)

        y_c = retention(apply_rope(r_q.reshape(B, S, RET_HEADS, RET_DK), cos_r, sin_r),
                        apply_rope(r_k.reshape(B, S, RET_HEADS, RET_DK), cos_r, sin_r),
                        r_v.reshape(B, S, RET_HEADS, RET_DV), log_gamma)
        y_c = jax.nn.silu(r_g) * head_group_norm(y_c, ret_norm_g[l])

        branches = jnp.stack([y_a, y_b, y_c], axis=2)
        up = jnp.einsum('bsnw,nwd->bsnd', branches, w_branch[l])
        gates = jax.nn.sigmoid(gate_logits.reshape(B, S, N_BRANCH, D_MODEL))
        x = x + jnp.einsum('bsnd,bsnd->bsd', gates, up) @ w_out[l]

        h = rmsnorm_2(x, norm_mlp_g[l])
        x = x + jnp.square(jax.nn.relu(h @ w_up[l])) @ w_down[l]

    return rmsnorm_2(x, final_norm_g)


def setup_inputs(seed=0):
    out = dict(first_inputs(seed))
    for name, value in second_inputs(seed + 1).items():
        if name != "x":
            out[name + "_2"] = value
    return out


def reference(
    x, norm_mix, w_in, dn_conv, dn_a_log, dn_dt_bias, dn_out_norm, rel_bias, w_branch_dn,
    w_branch_da, w_out, norm_ffn, peer_wq, peer_sub_keys, peer_u, peer_v, norm_final,
    positions_2, norm_mix_g_2, w_in_2, mla_q_norm_g_2, mla_w_uq_2, mla_kv_norm_g_2, mla_w_ukv_2,
    ret_norm_g_2, w_branch_2, w_out_2, norm_mlp_g_2, w_up_2, w_down_2, final_norm_g_2,
):
    x = first_block(
        x, norm_mix, w_in, dn_conv, dn_a_log, dn_dt_bias, dn_out_norm, rel_bias, w_branch_dn,
        w_branch_da, w_out, norm_ffn, peer_wq, peer_sub_keys, peer_u, peer_v, norm_final,
    )
    return second_block(
        x, positions_2, norm_mix_g_2, w_in_2, mla_q_norm_g_2, mla_w_uq_2, mla_kv_norm_g_2,
        mla_w_ukv_2, ret_norm_g_2, w_branch_2, w_out_2, norm_mlp_g_2, w_up_2, w_down_2,
        final_norm_g_2,
    )


_drawn_inputs = setup_inputs


def setup_inputs(seed=0):
    import zlib

    import numpy as np

    out = dict(_drawn_inputs(seed))
    spreads = {}
    factors = {'norm_mix_g_2': 2.714,
     'mla_q_norm_g_2': 8.0,
     'mla_kv_norm_g_2': 8.0,
     'ret_norm_g_2': 6.437,
     'final_norm_g_2': 8.139,
     'norm_mlp_g_2': 4.458}
    for name, (base, spread) in spreads.items():
        noise = np.random.default_rng([zlib.crc32(name.encode()), seed]).standard_normal(out[name].shape)
        drawn = base * np.exp(spread * noise) if base else spread * noise
        out[name] = jnp.asarray(drawn.astype(out[name].dtype))
    for name, factor in factors.items():
        out[name] = (out[name] * factor).astype(out[name].dtype)
    return out
```

```python
import math
from contextlib import ExitStack

import numpy as np

import concourse.bass as bass
from concourse import mybir

ALU = mybir.AluOpType
ACT = mybir.ActivationFunctionType
AX = mybir.AxisListType
F32 = mybir.dt.float32
F32R = mybir.dt.float32r
BF16 = mybir.dt.bfloat16
I32 = mybir.dt.int32
U32 = mybir.dt.uint32

P = 128
T = 512
D = 1024
NT = T // P
NC_D = D // P
GW = 512
EPS = 1e-6
NEG = -1e30

DH = 4
DHD = 128
CH = 64
NCHUNK = T // CH
GROUPS = ((128, 1), (512, 4), (2048, 16))
NG = len(GROUPS)
AH = 4
BUCKETS = 32
PH = 8
NKEY = 128
TOPK = 16
MH, M_NOPE, M_ROPE, M_V, M_QR, M_KVR = 8, 64, 32, 64, 384, 256
SBH, SBD = 8, 64
RH, RD = 8, 64
FF = 4096


class Chain:

    def __init__(self, eng, sem):
        self.eng, self.sem, self.n = eng, sem, 0

    def __call__(self, ins):
        ins.then_inc(self.sem, 1)
        self.n += 1
        self.eng.wait_ge(self.sem, self.n)


class Kernel:

    def __init__(self, nc, ctx):
        self.nc, self.ctx, self.live = nc, ctx, []

    def sem(self, name):
        s = self.nc.alloc_semaphore(name)
        self.live.append(s)
        return s

    def gather_sem(self, name):
        return self.nc.alloc_semaphore(name)

    def recycle(self):
        numbers = sorted(s.num for s in self.live)
        with self.nc.Block() as block:
            @block.gpsimd
            def _(pool):
                first = last = numbers[0]
                for n in numbers[1:] + [None]:
                    if n is not None and n == last + 1:
                        last = n
                        continue
                    pool.sem_clear(range(first, last + 1))
                    first = last = n
        for s in self.live:
            self.nc.release_semaphore(s)
        self.live = []


def load_constants(k, pairs, name="constants"):
    landed = k.sem(name + "_landed")
    with k.nc.Block() as block:
        @block.sync
        def _(sp):
            for dst, src in pairs:
                sp.dma_start(dst, src).then_inc(landed, 16)
            sp.wait_ge(landed, 16 * len(pairs))


def load_residual(k, name, x):
    nc = k.nc
    landed, turned, copied = k.sem(name + "_x_landed"), k.sem(name + "_turned"), k.sem(name + "_copied")
    with nc.sbuf_tensor(name + "_tok", [P, NT, D], F32) as tok, nc.Block() as block:
        @block.sync
        def _(sp):
            sp.dma_start(tok[:, :, :], x.rearrange("(m p) d -> p m d", p=P)).then_inc(landed, 16)

        @block.tensor
        def _(pe):
            pe.wait_ge(landed, 16)
            for c in range(NC_D):
                for m in range(NT):
                    last = pe.transpose(k.ps[:, c, m * P:(m + 1) * P], tok[:, m, c * P:(c + 1) * P], k.ident[:, :])
                last.then_inc(turned, 1)

        @block.vector
        def _(dve):
            for c in range(NC_D):
                dve.wait_ge(turned, c + 1)
                dve.tensor_copy(k.resid[:, c, :], k.ps[:, c, :]).then_inc(copied, 1)


def normalise(k, name, src, gain, n, tmp, hi=None, lo=None, dst=None):
    nc = k.nc
    landed, squared, summed = k.sem(name + "_gain_landed"), k.sem(name + "_squared"), k.sem(name + "_summed")
    var, root, inverse = k.sem(name + "_var"), k.sem(name + "_root"), k.sem(name + "_inverse")
    scaled, hi_done, lo_done = k.sem(name + "_scaled"), k.sem(name + "_hi_done"), k.sem(name + "_lo_done")
    to = tmp if dst is None else dst
    with (nc.sbuf_tensor(name + "_gain", [P, n], F32) as g, nc.sbuf_tensor(name + "_rstd", [P, T], F32) as rstd,
          nc.Block() as block):
        @block.sync
        def _(sp):
            sp.dma_start(g[:, :], gain).then_inc(landed, 16)

        @block.scalar
        def _(act):
            for c in range(n):
                act.activation(tmp[:, c, :], src[:, c, :], ACT.Square).then_inc(squared, 1)
            act.wait_ge(var, 1)
            act.activation(rstd[:, :], rstd[:, :], ACT.Sqrt).then_inc(root, 1)
            if dst is None:
                for c in range(n):
                    act.wait_ge(scaled, c + 1)
                    act.copy(hi[:, c, :], tmp[:, c, :]).then_inc(hi_done, 1)

        @block.tensor
        def _(pe):
            for c in range(n):
                pe.wait_ge(squared, c + 1)
                last = pe.matmul(k.ps[:, 0, :], k.ones[:, :], tmp[:, c, :], start=(c == 0), stop=(c == n - 1))
            last.then_inc(summed, 1)

        @block.vector
        def _(dve):
            dve.wait_ge(summed, 1)
            dve.tensor_scalar(rstd[:, :], k.ps[:, 0, :], 1.0 / (n * P), EPS, ALU.mult, ALU.add).then_inc(var, 1)
            dve.wait_ge(root, 1)
            dve.reciprocal(rstd[:, :], rstd[:, :]).then_inc(inverse, 1)
            dve.wait_ge(inverse, 1)
            dve.wait_ge(landed, 16)
            for c in range(n + 1):
                if c < n:
                    dve.scalar_tensor_tensor(to[:, c, :], src[:, c, :], g[:, c:c + 1], rstd[:, :],
                                             ALU.mult, ALU.mult).then_inc(scaled, 1)
                if c >= 1 and dst is None:
                    dve.wait_ge(hi_done, c)
                    dve.tensor_tensor(lo[:, c - 1, :], tmp[:, c - 1, :], hi[:, c - 1, :].bitcast(F32),
                                      ALU.subtract).then_inc(lo_done, 1)


FEATURE, TOKEN = "feature-major", "token-major"
UC, OUTS = 4, 4


def segments(runs):
    out, n = [], 0
    total = sum(r.count for r in runs)
    for run in runs:
        j = 0
        while j < run.count:
            left = min(run.count - j, total - 1 - n)
            loop = run.rolled and n >= 2 and n % 2 == 0 and left >= 4
            take = left // 2 * 2 if loop else 1
            out.append((run, j, take, n, loop))
            j, n = j + take, n + take
    return out


def each_group(eng, runs, body):
    for run, j0, count, n0, loop in segments(runs):
        if loop:
            with eng.Fori(0, count // 2) as i:
                for s in range(2):
                    body(run, i * 2 + (j0 + s), i * 2 + (n0 + s), i + n0 // 2, s)
        else:
            body(run, j0, n0, n0 // 2, n0 % 2)


class Run:

    def __init__(self, count, unit, x, layout=FEATURE, out=None, rolled=True):
        self.count, self.unit, self.x, self.layout, self.out, self.rolled = count, unit, x, layout, out, rolled


def stream(k, name, runs, upg, finish):
    nc = k.nc
    w_landed = [k.sem(f"{name}_w_landed{s}") for s in range(2)]
    hi_done, lo_done, used = k.sem(name + "_w_hi"), k.sem(name + "_w_lo"), k.sem(name + "_w_used")
    products, freed = finish["products"], finish["freed"]
    total = sum(r.count for r in runs)
    with (nc.sbuf_tensor(name + "_w", [P, 2, UC, GW], F32) as raw, nc.sbuf_tensor(name + "_w_high", [P, 2, UC, GW], F32R) as hi,
          nc.sbuf_tensor(name + "_w_low", [P, 2, UC, GW], F32R) as lo, nc.Block() as block):
        def slot(n, parity, i):
            return i % 2 if upg % 2 == 0 else (parity + i) % 2

        def fill(n, half, parity, i):
            if upg % 2 == 0:
                return n * (upg // 2) + (i // 2 + 1)
            return half + 1

        @block.sync
        def _(sp):
            def load(run, j, n, half, parity):
                for i in range(upg):
                    if i >= 2:
                        sp.wait_ge(used, n * (upg - 1) + (i - 1))
                    elif not (isinstance(n, int) and n * upg + i < 2):
                        if upg == 1:
                            sp.wait_ge(products, (n - 1) * OUTS)
                        elif i == 0:
                            sp.wait_ge(used, n * (upg - 1))
                        else:
                            sp.wait_ge(products, n * OUTS)
                    s = slot(n, parity, i)
                    sp.dma_start(raw[:, s, :, :], run.unit(j, i)).then_inc(w_landed[s], 16)
            each_group(sp, runs, load)

        def split_hi(act, n, half, parity, i):
            s = slot(n, parity, i)
            act.wait_ge(w_landed[s], fill(n, half, parity, i) * 16)
            for c in range(UC):
                act.copy(hi[:, s, c, :], raw[:, s, c, :]).then_inc(hi_done, 1)

        def split_lo(dve, n, half, parity, i):
            s = slot(n, parity, i)
            for c in range(UC):
                dve.wait_ge(hi_done, (n * upg + i) * UC + (c + 1))
                dve.tensor_tensor(lo[:, s, c, :], raw[:, s, c, :], hi[:, s, c, :].bitcast(F32), ALU.subtract).then_inc(lo_done, 1)

        def splitter(eng, split, fin):
            def group(run, j, n, half, parity):
                if isinstance(n, int) and n == 0:
                    split(eng, 0, 0, 0, 0)
                for i in range(1, upg):
                    split(eng, n, half, parity, i)
                if not (isinstance(n, int) and n == total - 1):
                    split(eng, n + 1, half + parity, 1 - parity, 0)
                fin(eng, run, j, n, half, parity)
            each_group(eng, runs, group)

        @block.scalar
        def _(act):
            splitter(act, split_hi, finish["act"])
            finish["act_end"](act)

        @block.vector
        def _(dve):
            splitter(dve, split_lo, finish["dve"])

        @block.tensor
        def _(pe):
            def multiply(run, j, n, half, parity):
                for i in range(upg):
                    s = slot(n, parity, i)
                    for q in range(OUTS):
                        if i == 0 and not (isinstance(n, int) and n < 2):
                            freed(pe, n - 2, q)
                        for c in range(UC):
                            if q == 0:
                                pe.wait_ge(lo_done, (n * upg + i) * UC + (c + 1))
                            xh, xl = run.x(j, i)
                            for p, (w, x) in enumerate(((hi, xh), (lo, xh), (hi, xl))):
                                if run.layout == FEATURE:
                                    a, b = w[:, s, c, q * P:(q + 1) * P], x[:, c, :]
                                else:
                                    a, b = x[:, c, q * P:(q + 1) * P], w[:, s, c, :]
                                last = pe.matmul(k.ps[:, 4 * parity + q, :], a, b, start=(i == 0 and c == 0 and p == 0),
                                                 stop=(i == upg - 1 and c == UC - 1 and p == 2))
                        if i == upg - 1:
                            last.then_inc(products, 1)
                    if i < upg - 1:
                        last.then_inc(used, 1)
            each_group(pe, runs, multiply)


def nothing(*_):
    pass


def project(k, name, runs):
    nc = k.nc
    stored = [k.sem(f"{name}_stored{s}") for s in range(2)]
    products, drained_v, drained_a = k.sem(name + "_products"), k.sem(name + "_drained_v"), k.sem(name + "_drained_a")
    total = sum(r.count for r in runs)
    with nc.sbuf_tensor(name + "_out", [P, 2, OUTS, T], F32) as out:
        def take(eng, copy, first, drained, n, half, s):
            if not (isinstance(n, int) and n < 2):
                eng.wait_ge(stored[s], half * 16)
            for q in range(first, first + 2):
                eng.wait_ge(products, n * OUTS + (q + 1))
                copy(out[:, s, q, :], k.ps[:, 4 * s + q, :]).then_inc(drained, 1)

        def dve_take(dve, run, j, n, half, s):
            take(dve, dve.tensor_copy, 0, drained_v, n, half, s)

        def act_take(act, run, j, n, half, s):
            take(act, act.copy, 2, drained_a, n, half, s)
            act.wait_ge(drained_v, (n + 1) * 2)
            act.wait_ge(drained_a, (n + 1) * 2)
            act.dma_start(run.out(j), out[:, s, :, :]).then_inc(stored[s], 16)

        def act_end(act):
            for s in range(2):
                act.wait_ge(stored[s], 16 * ((total + 1 - s) // 2))

        def freed(pe, n, q):
            pe.wait_ge(drained_v if q < 2 else drained_a, n * 2 + (q % 2 + 1))

        stream(k, name, runs, 2, {"products": products, "freed": freed, "dve": dve_take, "act": act_take, "act_end": act_end})


def narrow(k, name, x, w_dram, cols, rows, dst):
    nc = k.nc
    landed, zeroed, hi_done, lo_done = k.sem(name + "_landed"), k.sem(name + "_zeroed"), k.sem(name + "_hi"), k.sem(name + "_lo")
    product, copied = k.sem(name + "_product"), k.sem(name + "_copied")
    M = cols if rows is None else P
    c0 = 0 if rows is None else rows.start
    xh, xl = x
    with (nc.sbuf_tensor(name + "_w", [P, NC_D, M], F32) as w, nc.sbuf_tensor(name + "_w_high", [P, NC_D, M], F32R) as hi,
          nc.sbuf_tensor(name + "_w_low", [P, NC_D, M], F32R) as lo, nc.Block() as block):
        @block.gpsimd
        def _(pool):
            pool.memset(w[:, :, :], 0.0).then_inc(zeroed, 1)

        @block.sync
        def _(sp):
            sp.wait_ge(zeroed, 1)
            sp.dma_start(w[:, :, c0:c0 + cols], w_dram).then_inc(landed, 16)

        @block.scalar
        def _(act):
            act.wait_ge(landed, 16)
            act.copy(hi[:, :, :], w[:, :, :]).then_inc(hi_done, 1)

        @block.tensor
        def _(pe):
            pe.wait_ge(lo_done, 1)
            for m in range(NT if rows is None else 1):
                for c in range(NC_D):
                    for p, (wp, xp) in enumerate(((hi, xh), (lo, xh), (hi, xl))):
                        first, final = c == 0 and p == 0, c == NC_D - 1 and p == 2
                        if rows is None:
                            last = pe.matmul(k.ps[:, 0, m * cols:(m + 1) * cols], xp[:, c, m * P:(m + 1) * P], wp[:, c, :],
                                             start=first, stop=final)
                        else:
                            last = pe.matmul(k.ps[:, 0, :], wp[:, c, :], xp[:, c, :], start=first, stop=final)
            last.then_inc(product, 1)

        @block.vector
        def _(dve):
            dve.wait_ge(hi_done, 1)
            dve.tensor_tensor(lo[:, :, :], w[:, :, :], hi[:, :, :].bitcast(F32), ALU.subtract).then_inc(lo_done, 1)
            dve.wait_ge(product, 1)
            if rows is None:
                dve.tensor_copy(dst[:, :, :].rearrange("p m c -> p (m c)"), k.ps[:, 0, 0:NT * cols]).then_inc(copied, 1)
            else:
                dve.tensor_copy(dst[0:rows.stop, :], k.ps[0:rows.stop, 0, :]).then_inc(copied, 1)


def add_product(k, name, x, view, kchunks):
    products, added = k.sem(name + "_products"), k.sem(name + "_added")
    xh, xl = x
    run = Run(2, lambda j, i: view(i, j), lambda j, i: (xh[:, i * UC:(i + 1) * UC, :], xl[:, i * UC:(i + 1) * UC, :]), rolled=False)

    def dve_take(dve, run, j, n, half, s):
        for q in range(OUTS):
            dve.wait_ge(products, n * OUTS + (q + 1))
            r = k.resid[:, OUTS * j + q, :]
            dve.tensor_tensor(r, r, k.ps[:, 4 * s + q, :], ALU.add).then_inc(added, 1)

    stream(k, name, [run], kchunks // UC, {"products": products, "freed": nothing, "dve": dve_take, "act": nothing, "act_end": nothing})


def merge_branches(k, name, branches, view, gates, merged, hi, lo):
    nc, nb = k.nc, len(branches)
    products, g_in, sig, summed = k.sem(name + "_products"), k.sem(name + "_g_in"), k.sem(name + "_sig"), k.sem(name + "_summed")
    taken, hi_done, lo_done = k.sem(name + "_taken"), k.sem(name + "_hi"), k.sem(name + "_lo")
    order = [(g, b) for g in range(2) for b in range(nb)]
    N = len(order)
    gate_in = [k.sem(f"{name}_gate_in{s}") for s in range(2)]
    with nc.sbuf_tensor(name + "_g", [P, 2, OUTS, T], F32) as g, nc.sbuf_tensor(name + "_t", [P, 2, T], F32) as t:
        runs = [Run(1, lambda j, i, gb=gb: view(gb[1], gb[0]), lambda j, i, gb=gb: branches[gb[1]], out=gb, rolled=False)
                for gb in order]

        def act_take(act, run, j, n, half, s):
            if n == 0:
                act.dma_start(g[:, 0, :, :], gates(*order[0][::-1])).then_inc(gate_in[0], 16)
            if n + 1 < N:
                if n >= 1:
                    act.wait_ge(taken, OUTS * n)
                act.dma_start(g[:, (n + 1) % 2, :, :], gates(*order[n + 1][::-1])).then_inc(gate_in[(n + 1) % 2], 16)
            act.wait_ge(gate_in[n % 2], 16 * (n // 2 + 1))
            act.activation(g[:, n % 2, :, :], g[:, n % 2, :, :], ACT.Sigmoid).then_inc(sig, 1)
            gg, b = run.out
            if b == nb - 1:
                for q in range(OUTS):
                    c = OUTS * gg + q
                    act.wait_ge(summed, N_sum(gg, b, q))
                    act.copy(hi[:, c, :], merged[:, c, :]).then_inc(hi_done, 1)

        def N_sum(gg, b, q):
            return (gg * nb + b) * OUTS + q + 1

        def dve_take(dve, run, j, n, half, s):
            gg, b = run.out
            dve.wait_ge(sig, n + 1)
            for q in range(OUTS):
                c = OUTS * gg + q
                dve.wait_ge(products, n * OUTS + q + 1)
                if b == 0:
                    dve.tensor_tensor(merged[:, c, :], g[:, n % 2, q, :], k.ps[:, 4 * s + q, :], ALU.mult).then_inc(taken, 1)
                    dve.sem_inc(summed, 1)
                    continue
                if n * OUTS + q >= 2:
                    dve.wait_ge(summed, n * OUTS + q - 1)
                dve.tensor_tensor(t[:, q % 2, :], g[:, n % 2, q, :], k.ps[:, 4 * s + q, :], ALU.mult).then_inc(taken, 1)
                dve.wait_ge(taken, n * OUTS + q + 1)
                dve.wait_ge(summed, n * OUTS + q)
                dve.tensor_tensor(merged[:, c, :], merged[:, c, :], t[:, q % 2, :], ALU.add).then_inc(summed, 1)
            if b == nb - 1:
                for q in range(OUTS):
                    c = OUTS * gg + q
                    dve.wait_ge(hi_done, c + 1)
                    dve.tensor_tensor(lo[:, c, :], merged[:, c, :], hi[:, c, :].bitcast(F32), ALU.subtract).then_inc(lo_done, 1)

        def freed(pe, n, q):
            pe.wait_ge(taken, n * OUTS + q + 1)

        stream(k, name, runs, 1, {"products": products, "freed": freed, "dve": dve_take, "act": act_take, "act_end": nothing})


def turn_and_split(k, name, tile, hi, lo):
    turned, hi_done, lo_done = k.sem(name + "_y_turned"), k.sem(name + "_y_hi"), k.sem(name + "_y_lo")
    with k.nc.Block() as block:
        @block.tensor
        def _(pe):
            for j in range(4):
                for m in range(NT):
                    last = pe.transpose(k.ps[:, j, m * P:(m + 1) * P], tile(j, m), k.ident[:, :])
                last.then_inc(turned, 1)

        @block.scalar
        def _(act):
            for j in range(4):
                act.wait_ge(turned, j + 1)
                act.copy(hi[:, j, :], k.ps[:, j, :]).then_inc(hi_done, 1)

        @block.vector
        def _(dve):
            for j in range(4):
                dve.wait_ge(hi_done, j + 1)
                dve.tensor_tensor(lo[:, j, :], k.ps[:, j, :], hi[:, j, :].bitcast(F32), ALU.subtract).then_inc(lo_done, 1)


def store_final(k, name, xT, out):
    nc = k.nc
    turned, copied, stored = k.sem(name + "_turned"), k.sem(name + "_copied"), k.sem(name + "_stored")
    with nc.sbuf_tensor(name + "_tok", [P, NT, D], F32) as tok, nc.Block() as block:
        @block.tensor
        def _(pe):
            for m in range(NT):
                for c in range(NC_D):
                    last = pe.transpose(k.ps[:, 2 * m + c // 4, (c % 4) * P:(c % 4 + 1) * P], xT[:, c, m * P:(m + 1) * P],
                                        k.ident[:, :])
                last.then_inc(turned, 1)

        @block.vector
        def _(dve):
            for m in range(NT):
                dve.wait_ge(turned, m + 1)
                dve.tensor_copy(tok[:, m, :].rearrange("p (b c) -> p b c", b=2), k.ps[:, 2 * m:2 * m + 2, :]).then_inc(copied, 1)

        @block.sync
        def _(sp):
            for m in range(NT):
                sp.wait_ge(copied, m + 1)
                sp.dma_start(out[m * P:(m + 1) * P, :], tok[:, m, :]).then_inc(stored, 16)
            sp.wait_ge(stored, 16 * NT)


def delta_features(k, name, pf, conv_w, qT, kT, v_tok, k_tok):
    nc = k.nc
    A = 3 * DH
    landed, padded = k.sem(name + "_landed"), k.sem(name + "_padded")
    convolved, activated = k.sem(name + "_convolved"), k.sem(name + "_activated")
    squared, summed, offset, rooted = (k.sem(name + "_squared"), k.sem(name + "_summed"), k.sem(name + "_offset"),
                                       k.sem(name + "_rooted"))
    inverted, scaled = k.sem(name + "_inverted"), k.sem(name + "_scaled")
    turned, copied = k.sem(name + "_turned"), k.sem(name + "_copied")
    with (nc.sbuf_tensor(name + "_raw", [P, A, T + 3], F32) as raw, nc.sbuf_tensor(name + "_cw", [P, A, 4], F32) as cw,
          nc.sbuf_tensor(name + "_acc", [P, A, T], F32) as acc, nc.Block() as block):
        heads = acc
        sq = raw[:, 0:2 * DH, 0:T]
        raw_v = raw[:, 2 * DH:A, 0:T]

        @block.sync
        def _(sp):
            sp.dma_start(raw[:, :, 2:T + 2], pf).then_inc(landed, 16)
            sp.dma_start(cw[:, :, :], conv_w).then_inc(landed, 16)

        @block.gpsimd
        def _(pool):
            pool.memset(raw[:, :, 0:2], 0.0).then_inc(padded, 1)
            pool.memset(raw[:, :, T + 2:T + 3], 0.0).then_inc(padded, 1)

        @block.vector
        def _(dve):
            dve.wait_ge(landed, 32)
            dve.wait_ge(padded, 2)
            for j in range(4):
                for a in range(A):
                    if j == 0:
                        ins = dve.tensor_scalar(acc[:, a, :], raw[:, a, 0:T], cw[:, a, 0:1], None, ALU.mult)
                    else:
                        dve.wait_ge(convolved, A * (j - 1) + a + 1)
                        ins = dve.scalar_tensor_tensor(acc[:, a, :], raw[:, a, j:j + T], cw[:, a, j:j + 1],
                                                       acc[:, a, :], ALU.mult, ALU.add)
                    ins.then_inc(convolved, 1)
            for a in range(2 * DH):
                dve.wait_ge(summed, a + 1)
                dve.tensor_scalar(sq[:, a, :], k.ps[:, a, :], EPS, None, ALU.add).then_inc(offset, 1)
            for a in range(2 * DH):
                dve.wait_ge(rooted, a + 1)
                dve.reciprocal(sq[:, a, :], sq[:, a, :]).then_inc(inverted, 1)
            for a in range(2 * DH):
                dve.wait_ge(inverted, a + 1)
                dst = qT[:, a, :] if a < DH else kT[:, a - DH, :]
                dve.scalar_tensor_tensor(dst, heads[:, a, :], DHD ** -0.5 if a < DH else 1.0, sq[:, a, :],
                                         ALU.mult, ALU.mult).then_inc(scaled, 1)
            for m in range(NT):
                dve.wait_ge(turned, 2 * m + 1)
                dve.tensor_copy(v_tok[:, m, :, :].rearrange("p h d -> p (h d)"), k.ps[:, 2 * m, :]).then_inc(copied, 1)
                dve.wait_ge(turned, 2 * m + 2)
                dve.tensor_copy(k_tok[:, m, :, :].rearrange("p h d -> p (h d)"), k.ps[:, 2 * m + 1, :]).then_inc(copied, 1)

        @block.scalar
        def _(act):
            for a in range(A):
                act.wait_ge(convolved, 3 * A + a + 1)
                act.activation(heads[:, a, :], acc[:, a, :], ACT.Silu).then_inc(activated, 1)
            for a in range(2 * DH):
                act.wait_ge(activated, a + 1)
                act.activation(sq[:, a, :], heads[:, a, :], ACT.Square).then_inc(squared, 1)
            for a in range(2 * DH):
                act.wait_ge(offset, a + 1)
                act.activation(sq[:, a, :], sq[:, a, :], ACT.Sqrt).then_inc(rooted, 1)

        @block.tensor
        def _(pe):
            for a in range(2 * DH):
                pe.wait_ge(squared, a + 1)
                pe.matmul(k.ps[:, a, :], k.ones[:, :], sq[:, a, :], start=True, stop=True).then_inc(summed, 1)
            pe.wait_ge(activated, A)
            pe.wait_ge(offset, 2 * DH)
            pe.wait_ge(scaled, 2 * DH)
            for m in range(NT):
                for src, b in ((None, 2 * m), (kT, 2 * m + 1)):
                    for h in range(DH):
                        a = heads[:, 2 * DH + h, m * P:(m + 1) * P] if src is None else kT[:, h, m * P:(m + 1) * P]
                        last = pe.transpose(k.ps[:, b, h * P:(h + 1) * P], a, k.ident[:, :])
                    last.then_inc(turned, 1)


def delta_rule(k, name, ab, a_log, dt_bias, qT, kT, k_tok, v_tok, tables, z_dram, out_norm, outT):
    nc, ps = k.nc, k.ps
    R = 2 * DH
    tri, strict, block1, level = tables
    es = ExitStack()
    with es:
        def sb(n, shape, dt=F32):
            return es.enter_context(nc.sbuf_tensor(name + "_" + n, shape, dt))

        alog, dtb = sb("alog", [P, R]), sb("dtb", [P, R])
        g, beta, tmp, gc, gt = (sb(n, [P, NT, R]) for n in ("g", "beta", "tmp", "gc", "gt"))
        be, kd = sb("beta_eg", [P, NT, R]), sb("kd", [P, NT, R])
        dec, qd, lo, X, Y, F, DT = (sb(n, [P, R, NT, P]) for n in ("dec", "qd", "lo", "X", "Y", "F", "DT"))
        state, gl = sb("state", [P, R, P]), sb("gl", [P, R, NCHUNK])

        def flat(b, r):
            return b[:, r, :, :].rearrange("p m c -> p (m c)")

        in_l, step_a, step_v, sums = (k.sem(name + "_gate_in"), k.sem(name + "_gate_act"), k.sem(name + "_gate_dve"),
                                      k.sem(name + "_gate_sums"))
        with nc.Block() as block:
            @block.sync
            def _(sp):
                sp.dma_start(alog[:, :], a_log.partition_broadcast(P)).then_inc(in_l, 16)
                sp.dma_start(dtb[:, :], dt_bias.partition_broadcast(P)).then_inc(in_l, 16)

            @block.vector
            def _(dve):
                v = Chain(dve, step_v)
                dve.wait_ge(in_l, 32)
                v(dve.tensor_tensor(g[:, :, :], ab[:, :, 0:R], dtb[:, :].unsqueeze(1).to_broadcast([P, NT, R]), ALU.add))
                dve.wait_ge(step_a, 5)
                v(dve.scalar_tensor_tensor(g[:, :, :], g[:, :, :], 0.0, tmp[:, :, :], ALU.max, ALU.add))
                v(dve.scalar_tensor_tensor(g[:, :, :], g[:, :, :], -1.0,
                                           alog[:, :].unsqueeze(1).to_broadcast([P, NT, R]), ALU.mult, ALU.mult))
                dve.wait_ge(sums, 1)
                v(dve.tensor_copy(gc[:, :, :], ps[:, 0, 0:NT * R].rearrange("p (m r) -> p m r", r=R)))
                v(dve.tensor_copy(gt[:, :, :], ps[:, 1, 0:NT * R].rearrange("p (m r) -> p m r", r=R)))
                v(dve.tensor_tensor(kd[:, :, :], gt[:, :, :], gc[:, :, :], ALU.subtract))
                dve.wait_ge(step_a, 7)
                v(dve.tensor_tensor(be[:, :, :], be[:, :, :], beta[:, :, :], ALU.mult))

            @block.scalar
            def _(act):
                a = Chain(act, step_a)
                act.wait_ge(in_l, 32)
                a(act.activation(beta[:, :, :], ab[:, :, R:2 * R], ACT.Sigmoid))
                a(act.activation(alog[:, :], alog[:, :], ACT.Exp))
                act.wait_ge(step_v, 1)
                a(act.activation(tmp[:, :, :], g[:, :, :], ACT.Abs))
                a(act.activation(tmp[:, :, :], tmp[:, :, :], ACT.Exp, scale=-1.0))
                a(act.activation(tmp[:, :, :], tmp[:, :, :], ACT.Ln, bias=1.0))
                act.wait_ge(step_v, 6)
                a(act.activation(be[:, :, :], gc[:, :, :], ACT.Exp))
                a(act.activation(kd[:, :, :], kd[:, :, :], ACT.Exp))

            @block.tensor
            def _(pe):
                pe.wait_ge(step_v, 3)
                for m in range(NT):
                    for d in range(2):
                        pe.matmul(ps[:, 0, m * R + d * DH:m * R + (d + 1) * DH], tri[:, d, :], g[:, m, d * DH:(d + 1) * DH],
                                  start=True, stop=True)
                pe.matmul(ps[:, 1, 0:NT * R], block1[:, :], g[:, :, :].rearrange("p m r -> p (m r)"),
                          start=True, stop=True).then_inc(sums, 1)

        STEPS = 5
        pe_done, dve_read, eg_done = k.sem(name + "_pe_done"), k.sem(name + "_bank_read"), k.sem(name + "_eg_done")
        arg_done, dec_done, masked = k.sem(name + "_arg_done"), k.sem(name + "_dec_done"), k.sem(name + "_masked")
        c_ready, f_ready = k.sem(name + "_c_ready"), k.sem(name + "_f_ready")
        chain_v, gbc_done = k.sem(name + "_chain_v"), k.sem(name + "_gbc_done")
        LEVELS = 6
        order = [("rows", 0), ("kk", 0), ("kq", 0), ("turn", 0), ("c0", 0)]
        for l in range(1, LEVELS):
            order += [("f", l)] + ([("e", l)] if l < LEVELS - 1 else []) + [("et", l)]

        def bufs(l):
            return (X, Y) if l % 2 == 1 else (Y, X)

        with nc.Block() as block:
            @block.gpsimd
            def _(pool):
                for r in range(R):
                    pool.tensor_copy(F[:, r, :, :], g[:, :, r:r + 1].to_broadcast([P, NT, P])).then_inc(gbc_done, 1)

            @block.tensor
            def _(pe):
                for s, (what, l) in enumerate(order):
                    for r in range(R):
                        h, d = r % DH, r // DH
                        if s == 0:
                            pe.wait_ge(gbc_done, r + 1)
                        else:
                            pe.wait_ge(dve_read, (s - 1) * R + r + 1)
                        if what == "c0":
                            pe.wait_ge(c_ready, r + 1)
                        if what == "f":
                            pe.wait_ge(c_ready, l * R + r + 1)
                        for m in range(NT):
                            o = ps[:, r, m * P:(m + 1) * P]
                            tok = slice(m * P, (m + 1) * P)
                            if what == "rows":
                                last = pe.matmul(o, F[:, r, m, :], tri[:, d, :], start=True, stop=True)
                            elif what == "kk":
                                last = pe.matmul(o, kT[:, h, tok], kT[:, h, tok], start=True, stop=True)
                            elif what == "kq":
                                last = pe.matmul(o, kT[:, h, tok], qT[:, h, tok], start=True, stop=True)
                            elif what == "turn":
                                last = pe.transpose(o, F[:, r, m, :], k.ident[:, :])
                            elif what == "c0":
                                last = pe.matmul(o, Y[:, r, m, :], k.ident[:, :], start=True, stop=True)
                            elif what == "f":
                                last = pe.matmul(o, bufs(l)[1][:, r, m, :], DT[:, r, m, :], start=True, stop=True)
                            elif what == "e":
                                last = pe.matmul(o, F[:, r, m, :], bufs(l)[0][:, r, m, :], start=True, stop=True)
                            else:
                                last = pe.matmul(o, bufs(l)[0][:, r, m, :], F[:, r, m, :], start=True, stop=True)
                        last.then_inc(pe_done, 1)

            @block.scalar
            def _(act):
                for r in range(R):
                    act.wait_ge(arg_done, r + 1)
                    act.activation(flat(X, r), ps[:, r, :], ACT.Exp).then_inc(eg_done, 1)
                    act.activation(flat(dec, r), flat(dec, r), ACT.Exp).then_inc(dec_done, 1)

            @block.vector
            def _(dve):
                v = Chain(dve, chain_v)

                def bc(t, d, l=None):
                    t = t[:, d, :] if l is None else t[:, d, l, :]
                    return t.unsqueeze(1).to_broadcast([P, NT, P])

                for s, (what, l) in enumerate(order):
                    if s == 1:
                        for r in range(R):
                            dve.wait_ge(eg_done, r + 1)
                            end = CH - 1 if r < DH else 0
                            dve.tensor_copy(gl[:, r, :], flat(X, r).rearrange("p (n c) -> p n c", c=CH)[:, :, end])
                            dve.tensor_tensor(flat(qd, r), qT[:, r % DH, :], flat(X, r), ALU.mult).then_inc(dve_read, 1)
                    for r in range(R):
                        h, d = r % DH, r // DH
                        bank = ps[:, r, :]
                        tiles = bank.rearrange("p (m c) -> p m c", m=NT)
                        dve.wait_ge(pe_done, s * R + r + 1)
                        if what == "rows":
                            for m in range(NT):
                                ins = dve.tensor_scalar(dec[:, r, m, :], tiles[:, m, :], gc[:, m, r:r + 1], 0.0,
                                                        ALU.subtract, ALU.min)
                            ins.then_inc(arg_done, 1)
                        elif what == "kk":
                            dve.wait_ge(dec_done, r + 1)
                            v(dve.tensor_tensor(dec[:, r, :, :], dec[:, r, :, :], bc(tri, d), ALU.mult))
                            v(dve.tensor_tensor(flat(F, r), bank, flat(dec, r), ALU.mult))
                            dve.tensor_tensor(F[:, r, :, :], F[:, r, :, :], bc(strict, d), ALU.mult).then_inc(dve_read, 1)
                        elif what == "kq":
                            dve.tensor_tensor(flat(dec, r), bank, flat(dec, r), ALU.mult).then_inc(dve_read, 1)
                        elif what == "turn":
                            v(dve.tensor_tensor(lo[:, r, :, :], tiles, beta[:, :, r:r + 1].to_broadcast([P, NT, P]), ALU.mult))
                            dve.sem_inc(dve_read, 1)
                            dve.tensor_tensor(Y[:, r, :, :], lo[:, r, :, :], bc(level, d, 0), ALU.mult).then_inc(c_ready, 1)
                        elif what == "c0":
                            ident = k.ident[:, :].unsqueeze(1).to_broadcast([P, NT, P])
                            v(dve.tensor_tensor(DT[:, r, :, :], ident, tiles, ALU.subtract))
                            v(dve.tensor_tensor(X[:, r, :, :], ident, Y[:, r, :, :], ALU.subtract))
                            dve.sem_inc(dve_read, 1)
                            dve.tensor_tensor(Y[:, r, :, :], lo[:, r, :, :], bc(level, d, 1), ALU.mult).then_inc(c_ready, 1)
                        elif what == "f":
                            dve.tensor_copy(flat(F, r), bank).then_inc(dve_read, 1)
                        elif what == "e":
                            D_, C_ = bufs(l)
                            dve.tensor_tensor(flat(C_, r), flat(D_, r), bank, ALU.subtract).then_inc(dve_read, 1)
                        else:
                            D_, C_ = bufs(l)
                            v(dve.tensor_tensor(flat(DT, r), flat(DT, r), bank, ALU.subtract))
                            dve.sem_inc(dve_read, 1)
                            if l < LEVELS - 1:
                                dve.tensor_tensor(D_[:, r, :, :], lo[:, r, :, :], bc(level, d, l + 1), ALU.mult).then_inc(c_ready, 1)

        rhs_v, rhs_k, kd_done = k.sem(name + "_rhs_v"), k.sem(name + "_rhs_k"), k.sem(name + "_kd_done")
        u_done, w_done, u_kept, w_kept = (k.sem(name + "_u_done"), k.sem(name + "_w_done"), k.sem(name + "_u_kept"),
                                          k.sem(name + "_w_kept"))
        U, WT, VN, KD, O = lo, F, Y, X, DT
        with nc.Block() as block:
            def by(t, r):
                return t[:, :, r:r + 1].to_broadcast([P, NT, P])

            @block.vector
            def _(dve):
                for r in range(R):
                    dve.tensor_tensor(X[:, r, :, :], v_tok[:, :, r % DH, :], by(beta, r), ALU.mult).then_inc(rhs_v, 1)
                    dve.tensor_tensor(Y[:, r, :, :], k_tok[:, :, r % DH, :], by(be, r), ALU.mult).then_inc(rhs_k, 1)
                for r in range(R):
                    dve.wait_ge(u_done, r + 1)
                    dve.tensor_copy(flat(U, r), ps[:, r, :]).then_inc(u_kept, 1)
                for r in range(R):
                    dve.tensor_tensor(KD[:, r, :, :], k_tok[:, :, r % DH, :], by(kd, r), ALU.mult).then_inc(kd_done, 1)

            @block.scalar
            def _(act):
                for r in range(R):
                    act.wait_ge(w_done, r + 1)
                    act.copy(flat(WT, r), ps[:, r, :]).then_inc(w_kept, 1)

            @block.tensor
            def _(pe):
                for r in range(R):
                    pe.wait_ge(rhs_v, r + 1)
                    for m in range(NT):
                        last = pe.matmul(ps[:, r, m * P:(m + 1) * P], DT[:, r, m, :], X[:, r, m, :], start=True, stop=True)
                    last.then_inc(u_done, 1)
                for r in range(R):
                    pe.wait_ge(rhs_k, r + 1)
                    pe.wait_ge(u_kept, r + 1)
                    for m in range(NT):
                        last = pe.matmul(ps[:, r, m * P:(m + 1) * P], Y[:, r, m, :], DT[:, r, m, :], start=True, stop=True)
                    last.then_inc(w_done, 1)

        ws_done, v_new, upd_done, s_new, o_copied = (k.sem(name + "_ws_done"), k.sem(name + "_v_new"),
                                                     k.sem(name + "_upd_done"), k.sem(name + "_s_new"),
                                                     k.sem(name + "_o_copied"))
        intra_done, o_done = k.sem(name + "_intra_done"), k.sem(name + "_o_done")

        def rows(b, d):
            return ps[:, b + d, :].rearrange("p (h c) -> p h c", h=DH)

        with nc.Block() as block:
            @block.tensor
            def _(pe):
                for c in range(NCHUNK):
                    for d in range(2):
                        n = c if d == 0 else NCHUNK - 1 - c
                        m, half = n // 2, (n % 2) * CH
                        if c > 0:
                            pe.wait_ge(s_new, DH * (2 * (c - 1) + d + 1))
                            if c > 1:
                                pe.wait_ge(o_copied, 2 * (c - 1) + d + 1)
                            for h in range(DH):
                                r = d * DH + h
                                pe.matmul(rows(0, d)[:, h, :], WT[:, r, m, :], state[:, r, :], start=True, stop=True)
                                last = pe.matmul(rows(2, d)[:, h, :], qd[:, r, m, :], state[:, r, :], start=True, stop=True)
                            last.then_inc(ws_done, 1)
                    for d in range(2):
                        n = c if d == 0 else NCHUNK - 1 - c
                        m, half = n // 2, (n % 2) * CH
                        pe.wait_ge(v_new, 2 * c + d + 1)
                        if c < NCHUNK - 1:
                            for h in range(DH):
                                r = d * DH + h
                                last = pe.matmul(rows(4, d)[:, h, :], KD[half:half + CH, r, m, :], VN[half:half + CH, r, m, :],
                                                 start=True, stop=True)
                            last.then_inc(upd_done, 1)
                pe.wait_ge(o_copied, 2 * NCHUNK)
                pe.wait_ge(s_new, 2 * DH * (NCHUNK - 1))
                for r in range(R):
                    for m in range(NT):
                        last = pe.matmul(ps[:, r, m * P:(m + 1) * P], dec[:, r, m, :], VN[:, r, m, :], start=True, stop=True)
                    last.then_inc(intra_done, 1)

            @block.vector
            def _(dve):
                for c in range(NCHUNK):
                    for d in range(2):
                        n = c if d == 0 else NCHUNK - 1 - c
                        m, half = n // 2, slice((n % 2) * CH, (n % 2) * CH + CH)
                        rs = slice(d * DH, (d + 1) * DH)
                        if c == 0:
                            ins = dve.tensor_copy(VN[half, rs, m, :], U[half, rs, m, :])
                        else:
                            dve.wait_ge(ws_done, 2 * (c - 1) + d + 1)
                            ins = dve.tensor_tensor(VN[half, rs, m, :], U[half, rs, m, :], rows(0, d)[half, :, :], ALU.subtract)
                        ins.then_inc(v_new, 1)
                    for d in range(2):
                        n = c if d == 0 else NCHUNK - 1 - c
                        if c == NCHUNK - 1:
                            continue
                        dve.wait_ge(upd_done, 2 * c + d + 1)
                        for h in range(DH):
                            r = d * DH + h
                            if c == 0:
                                ins = dve.tensor_copy(state[:, r, :], rows(4, d)[:, h, :])
                            else:
                                dve.wait_ge(s_new, DH * (2 * (c - 1) + d) + h + 1)
                                ins = dve.scalar_tensor_tensor(state[:, r, :], state[:, r, :], gl[:, r, n:n + 1],
                                                               rows(4, d)[:, h, :], ALU.mult, ALU.add)
                            ins.then_inc(s_new, 1)
                for r in range(R):
                    dve.wait_ge(intra_done, r + 1)
                    dve.wait_ge(o_copied, 2 * NCHUNK)
                    dve.tensor_tensor(flat(O, r), flat(O, r), ps[:, r, :], ALU.add).then_inc(o_done, 1)

            @block.scalar
            def _(act):
                for c in range(NCHUNK):
                    for d in range(2):
                        n = c if d == 0 else NCHUNK - 1 - c
                        m, half = n // 2, slice((n % 2) * CH, (n % 2) * CH + CH)
                        rs = slice(d * DH, (d + 1) * DH)
                        if c == 0:
                            act.mul(O[half, rs, m, :], U[half, rs, m, :], 0.0).then_inc(o_copied, 1)
                        else:
                            act.wait_ge(ws_done, 2 * (c - 1) + d + 1)
                            act.copy(O[half, rs, m, :], rows(2, d)[half, :, :]).then_inc(o_copied, 1)

        z_in, fv, fa = k.sem(name + "_z_in"), k.sem(name + "_fin_dve"), k.sem(name + "_fin_act")
        z, onorm, ss = Y, sb("onorm", [P, DHD]), sb("ss", [P, DH * NT])
        with nc.Block() as block:
            z_tok = z[:, 0:DH, :, :].rearrange("p h m c -> p (h m c)").rearrange("p (m n) -> p m n", m=NT)
            z_hm = z_tok.rearrange("p m (h c) -> p h m c", h=DH)
            o_all = O[:, 0:DH, :, :]
            o_rows = O[:, 0:DH, :, :].rearrange("p h m c -> p (h m) c")
            sq = O[:, DH:R, :, :].rearrange("p h m c -> p (h m) c")

            @block.sync
            def _(sp):
                sp.dma_start(z_tok, z_dram).then_inc(z_in, 16)
                sp.dma_start(onorm[:, :], out_norm.partition_broadcast(P)).then_inc(z_in, 16)

            @block.vector
            def _(dve):
                v = Chain(dve, fv)
                for h in range(DH):
                    v(dve.tensor_tensor(flat(O, h), flat(O, h), flat(O, DH + h), ALU.add))
                v(dve.tensor_tensor(sq, o_rows, o_rows, ALU.mult))
                v(dve.tensor_reduce(ss[:, :], sq, AX.X, ALU.add))
                v(dve.tensor_scalar(ss[:, :], ss[:, :], 1.0 / DHD, EPS, ALU.mult, ALU.add))
                dve.wait_ge(fa, 1)
                v(dve.reciprocal(ss[:, :], ss[:, :]))
                v(dve.tensor_tensor(o_rows, o_rows, ss[:, :].unsqueeze(2).to_broadcast([P, DH * NT, DHD]), ALU.mult))
                dve.wait_ge(z_in, 32)
                v(dve.tensor_tensor(o_rows, o_rows, onorm[:, :].unsqueeze(1).to_broadcast([P, DH * NT, DHD]), ALU.mult))
                dve.wait_ge(fa, 2)
                v(dve.tensor_tensor(o_all, o_all, z_hm, ALU.mult))

            @block.scalar
            def _(act):
                a = Chain(act, fa)
                act.wait_ge(fv, 7)
                a(act.activation(ss[:, :], ss[:, :], ACT.Sqrt))
                act.wait_ge(z_in, 32)
                a(act.activation(z_tok, z_tok, ACT.Silu))
        turn_and_split(k, name, lambda h, m: O[:, h, m, :], *outT)


def delta_tables():
    i = np.arange(P)
    same = (i[:, None] // CH) == (i[None, :] // CH)
    tri = np.stack([same & (i[:, None] <= i[None, :]), same & (i[:, None] >= i[None, :])], 1)
    strict = np.stack([same & (i[:, None] < i[None, :]), same & (i[:, None] > i[None, :])], 1)
    level = np.zeros((P, 2, 6, P), bool)
    for l in range(6):
        pair = (i[:, None] >> (l + 1)) == (i[None, :] >> (l + 1))
        up, low = (i[:, None] >> l) & 1, (i[None, :] >> l) & 1
        level[:, 0, l] = pair & (up == 1) & (low == 0)
        level[:, 1, l] = pair & (up == 0) & (low == 1)
    f = lambda a: np.ascontiguousarray(a.astype(np.float32))
    return f(tri), f(strict), f(same), f(level)


SIDE = 64
ELEN = 384


def t5_bucket(rel):
    half, exact = BUCKETS // 2, BUCKETS // 4
    n = np.abs(rel)
    large = exact + (np.log(np.maximum(n, 1) / exact) / math.log(1024 / exact) * (half - exact)).astype(np.int64)
    large = np.minimum(large, half - 1)
    return np.where(rel > 0, half, 0) + np.where(n < exact, n, large)


def bias_tables():
    hot = np.zeros((BUCKETS + 1, NG, ELEN), np.float32)
    for g, (window, dil) in enumerate(GROUPS):
        rel = np.arange(ELEN) - (191 if g == 0 else 127)
        ok = np.abs(rel) <= window // (2 * dil)
        b = t5_bucket(rel * dil)
        for x in range(ELEN):
            if ok[x]:
                hot[b[x], g, x] = 1.0
            else:
                hot[BUCKETS, g, x] = NEG
    i = np.arange(P) // 32
    block = np.where(i[:, None] == i[None, :], 0.0, NEG).astype(np.float32)
    return hot, block


def dilated_attention(k, name, qk_dram, v_dram, table, hot_dram, block_dram, e_scratch, o_scratch, lse_scratch, outT):
    nc, ps = k.nc, k.ps
    es = ExitStack()
    with es:
        def sb(n, shape, dt=F32):
            return es.enter_context(nc.sbuf_tensor(name + "_" + n, shape, dt))

        bias0, bias12 = sb("bias0", [P, 3, AH, 2 * P]), sb("bias12", [P, 2, AH, P])
        with nc.sbuf_tensor(name + "_hot", [BUCKETS + 1, NG, ELEN], F32) as hot, \
                nc.sbuf_tensor(name + "_tab", [BUCKETS + 1, NG * AH], F32) as tab, \
                nc.sbuf_tensor(name + "_tabw", [BUCKETS + 1, NG * AH, P], F32) as tabw, \
                nc.sbuf_tensor(name + "_e", [P, NG * AH, ELEN], F32) as e, \
                nc.sbuf_tensor(name + "_blk", [P, P], F32) as blk, nc.Block() as block:
            landed, ones_row, wide, made, kept = (k.sem(name + "_b_landed"), k.sem(name + "_b_ones"),
                                                  k.sem(name + "_b_wide"), k.sem(name + "_b_made"), k.sem(name + "_b_kept"))
            out, back, fixed = k.sem(name + "_b_out"), k.sem(name + "_b_back"), k.sem(name + "_b_fixed")

            @block.sync
            def _(sp):
                sp.dma_start(hot[:, :, :], hot_dram).then_inc(landed, 16)
                sp.dma_start(tab[0:BUCKETS, :], table).then_inc(landed, 16)
                sp.dma_start(blk[:, :], block_dram).then_inc(landed, 16)
                sp.wait_ge(kept, NG * AH)
                sp.dma_start(e_scratch.rearrange("(n p) x -> p n x", p=P), e[:, :, :]).then_inc(out, 16)
                sp.wait_ge(out, 16)
                size = P * ELEN
                skew = lambda n0, w: bass.AP(e_scratch.tensor, e_scratch.offset + n0 * size + P - 1,
                                             [[ELEN - 1, P], [size, AH], [1, w]])
                for v in range(3):
                    sp.dma_start(bias0[:, v, :, :], skew(0, 2 * P)).then_inc(back, 16)
                for g in (1, 2):
                    sp.dma_start(bias12[:, g - 1, :, :], skew(g * AH, P)).then_inc(back, 16)

            @block.vector
            def _(dve):
                dve.memset(tab[BUCKETS:BUCKETS + 1, :], 1.0).then_inc(ones_row, 1)
                dve.wait_ge(ones_row, 1)
                dve.wait_ge(landed, 48)
                dve.tensor_copy(tabw[:, :, :], tab[:, :].unsqueeze(2).to_broadcast([BUCKETS + 1, NG * AH, P])).then_inc(wide, 1)
                for n in range(NG * AH):
                    dve.wait_ge(made, n + 1)
                    dve.tensor_copy(e[:, n, :], ps[:, n % 8, 0:ELEN]).then_inc(kept, 1)
                dve.wait_ge(back, 80)
                dve.memset(bias0[:, 0, :, 0:SIDE], NEG).then_inc(fixed, 1)
                dve.memset(bias0[:, 2, :, 2 * P - SIDE:2 * P], NEG).then_inc(fixed, 1)
                dve.tensor_tensor(bias12[:, 1, :, :], bias12[:, 1, :, :],
                                  blk[:, :].unsqueeze(1).to_broadcast([P, AH, P]), ALU.add).then_inc(fixed, 1)

            @block.tensor
            def _(pe):
                pe.wait_ge(wide, 1)
                for n in range(NG * AH):
                    if n >= 8:
                        pe.wait_ge(kept, n - 7)
                    pe.matmul(ps[:, n % 8, 0:ELEN], tabw[:, n, :], hot[:, n // AH, :], start=True, stop=True).then_inc(made, 1)

        o = sb("o", [P, NG, NT, AH * P])
        nmx, l_sum, rl = sb("nmx", [P, NG, NT, AH]), sb("l", [P, NG, NT, AH]), sb("rl", [P, NG, NT, AH])
        es2 = ExitStack()
        with es2:
            def sb2(n, shape, dt=F32):
                return es2.enter_context(nc.sbuf_tensor(name + "_" + n, shape, dt))
            q0, k0 = sb2("q0", [P, AH, T]), sb2("k0", [P, AH, T + 2 * SIDE])
            q12, k12 = sb2("q12", [P, 2, AH, T]), sb2("k12", [P, 2, AH, T])
            raw = sb2("raw", [P, 2, AH, T])
            v0, v12 = sb2("v0", [P, NT + 1, AH * P]), sb2("v12", [P, 2, NT, AH * P])
            logit, pT = sb2("logit", [P, 2, 2 * P]), sb2("pT", [P, 2, 2, P])
            q_in, r_in, v_in, zeroed, moved = (k.sem(name + "_q_in"), [k.sem(f"{name}_r_in{i}") for i in range(2)],
                                               k.sem(name + "_v_in"), k.sem(name + "_zeroed"), k.sem(name + "_moved"))
            s_done, s_read, p_done, t_done, t_read, pv_done, o_done = (
                k.sem(name + "_s_done"), k.sem(name + "_max_done"), k.sem(name + "_p_done"), k.sem(name + "_t_done"),
                k.sem(name + "_t_read"), k.sem(name + "_pv_done"), k.sem(name + "_o_done"))
            chain, stored, lse_a, lse_v = (k.sem(name + "_chain"), k.sem(name + "_stored"), k.sem(name + "_lse_a"),
                                           k.sem(name + "_lse_v"))
            units = [(g, m, h) for g in range(NG) for m in range(NT) for h in range(AH)]
            N = len(units)
            qk = lambda which, g: qk_dram[:, which * NG * AH + g * AH:which * NG * AH + (g + 1) * AH, :]
            vg = lambda g: v_dram[:, g * AH * P:(g + 1) * AH * P]

            with nc.Block() as block:
                @block.sync
                def _(sp):
                    sp.dma_start(q0[:, :, :], qk(0, 0)).then_inc(q_in, 16)
                    sp.dma_start(k0[:, :, SIDE:T + SIDE], qk(1, 0)).then_inc(q_in, 16)
                    sp.dma_start(v0[:, 1:NT, :], vg(0)[SIDE:T - SIDE, :].rearrange("(m p) c -> p m c", p=P)).then_inc(v_in, 16)
                    sp.dma_start(v0[SIDE:P, 0, :], vg(0)[0:SIDE, :]).then_inc(v_in, 16)
                    sp.dma_start(v0[0:SIDE, NT, :], vg(0)[T - SIDE:T, :]).then_inc(v_in, 16)
                    sp.dma_start(v12[:, 0, :, :], vg(1).rearrange("(l m) c -> l m c", m=4)).then_inc(v_in, 16)
                    for r in range(4):
                        sp.dma_start(v12[r * 32:(r + 1) * 32, 1, :, :],
                                     vg(2).rearrange("(l m r) c -> r l m c", m=4, r=4)[r]).then_inc(v_in, 16)
                    for i, (which, g) in enumerate([(0, 1), (1, 1), (0, 2), (1, 2)]):
                        if i >= 2:
                            sp.wait_ge(moved, AH * (i - 1))
                        sp.dma_start(raw[:, i % 2, :, :], qk(which, g)).then_inc(r_in[i % 2], 16)
                    for g in range(NG):
                        sp.wait_ge(o_done, NT * AH * (g + 1))
                        if g == 0:
                            sp.dma_start(o_scratch[0].rearrange("(m p) c -> p m c", p=P), o[:, 0, :, :]).then_inc(stored, 16)
                        elif g == 1:
                            sp.dma_start(o_scratch[1].rearrange("(l m) c -> l m c", m=4), o[:, 1, :, :]).then_inc(stored, 16)
                        else:
                            for r in range(4):
                                sp.dma_start(o_scratch[2].rearrange("(l m r) c -> r l m c", m=4, r=4)[r],
                                             o[r * 32:(r + 1) * 32, 2, :, :]).then_inc(stored, 16)
                    sp.wait_ge(lse_v, 1)
                    sp.dma_start(lse_scratch[0].rearrange("(m p) c -> p m c", p=P), l_sum[:, 0, :, :]).then_inc(stored, 16)
                    sp.dma_start(lse_scratch[1].rearrange("(l m) c -> l m c", m=4), l_sum[:, 1, :, :]).then_inc(stored, 16)
                    for r in range(4):
                        sp.dma_start(lse_scratch[2].rearrange("(l m r) c -> r l m c", m=4, r=4)[r],
                                     l_sum[r * 32:(r + 1) * 32, 2, :, :]).then_inc(stored, 16)
                    sp.wait_ge(stored, 16 * 12)

                @block.gpsimd
                def _(pool):
                    pool.memset(k0[:, :, 0:SIDE], 0.0).then_inc(zeroed, 1)
                    pool.memset(k0[:, :, T + SIDE:T + 2 * SIDE], 0.0).then_inc(zeroed, 1)
                    pool.wait_ge(zeroed, 2)
                    pool.memset(v0[0:SIDE, 0, :], 0.0).then_inc(zeroed, 1)
                    pool.wait_ge(zeroed, 3)
                    pool.memset(v0[SIDE:P, NT, :], 0.0).then_inc(zeroed, 1)
                    pool.wait_ge(zeroed, 4)
                    for i in range(4):
                        pool.wait_ge(r_in[i % 2], 16 * (i // 2 + 1))
                        dst = (q12, k12)[i % 2]
                        n = (4, 16)[i // 2]
                        for h in range(AH):
                            pool.tensor_copy(dst[:, i // 2, h, :].rearrange("p (n l) -> p n l", n=n),
                                             raw[:, i % 2, h, :].rearrange("p (l n) -> p n l", n=n)).then_inc(moved, 1)

                def keys(g):
                    return 2 * P if g == 0 else P

                @block.tensor
                def _(pe):
                    for i in range(N + 2):
                        if i < N:
                            g, m, h = units[i]
                            if i == 0:
                                pe.wait_ge(q_in, 32)
                                pe.wait_ge(zeroed, 4)
                            elif (m, h) == (0, 0):
                                pe.wait_ge(moved, 2 * AH * g)
                            if i >= 2:
                                pe.wait_ge(s_read, i - 1)
                            if g == 0:
                                pe.matmul(ps[:, i % 2, 0:2 * P], q0[:, h, m * P:(m + 1) * P], k0[:, h, m * P:(m + 2) * P],
                                          start=True, stop=True).then_inc(s_done, 1)
                            else:
                                tok = slice(m * P, (m + 1) * P)
                                pe.matmul(ps[:, i % 2, 0:P], q12[:, g - 1, h, tok], k12[:, g - 1, h, tok],
                                          start=True, stop=True).then_inc(s_done, 1)
                        if 1 <= i <= N:
                            j = i - 1
                            g = units[j][0]
                            pe.wait_ge(p_done, j + 1)
                            if j >= 2:
                                pe.wait_ge(t_read, j - 1)
                            for c in range(keys(g) // P):
                                last = pe.transpose(ps[:, 2 + j % 2, c * P:(c + 1) * P], logit[:, j % 2, c * P:(c + 1) * P],
                                                    k.ident[:, :])
                            last.then_inc(t_done, 1)
                        if i >= 2:
                            j = i - 2
                            g, m, h = units[j]
                            pe.wait_ge(t_read, j + 1)
                            if j == 0:
                                pe.wait_ge(v_in, 16 * 8)
                            if j >= 2:
                                pe.wait_ge(o_done, j - 1)
                            nk = keys(g) // P
                            for c in range(nk):
                                v = v0[:, m + c, h * P:(h + 1) * P] if g == 0 else v12[:, g - 1, m, h * P:(h + 1) * P]
                                last = pe.matmul(ps[:, 4 + j % 2, 0:P], pT[:, j % 2, c, :], v, start=(c == 0), stop=(c == nk - 1))
                            last.then_inc(pv_done, 1)

                @block.vector
                def _(dve):
                    n_chain = 0
                    for i in range(N + 2):
                        if i < N:
                            g, m, h = units[i]
                            w = keys(g)
                            dve.wait_ge(s_done, i + 1)
                            if i >= 2:
                                dve.wait_ge(t_done, i - 1)
                            b = bias0[:, (0 if m == 0 else 2 if m == NT - 1 else 1), h, :] if g == 0 else bias12[:, g - 1, h, :]
                            dve.scalar_tensor_tensor(logit[:, i % 2, 0:w], ps[:, i % 2, 0:w], P ** -0.5, b,
                                                     ALU.mult, ALU.add).then_inc(chain, 1)
                            n_chain += 1
                            dve.wait_ge(chain, n_chain)
                            dve.tensor_reduce(nmx[:, g, m, h:h + 1], logit[:, i % 2, 0:w], AX.X, ALU.max,
                                              negate=True).then_inc(s_read, 1)
                        if i >= 2:
                            j = i - 2
                            g, m, h = units[j]
                            dve.wait_ge(pv_done, j + 1)
                            dve.reciprocal(rl[:, g, m, h:h + 1], l_sum[:, g, m, h:h + 1]).then_inc(chain, 1)
                            n_chain += 1
                            dve.wait_ge(chain, n_chain)
                            dve.tensor_scalar(o[:, g, m, h * P:(h + 1) * P], ps[:, 4 + j % 2, 0:P], rl[:, g, m, h:h + 1],
                                              None, ALU.mult).then_inc(o_done, 1)
                    dve.wait_ge(lse_a, 1)
                    dve.tensor_tensor(l_sum[:, :, :, :], l_sum[:, :, :, :], nmx[:, :, :, :], ALU.subtract).then_inc(lse_v, 1)

                @block.scalar
                def _(act):
                    for i in range(N + 1):
                        if i < N:
                            g, m, h = units[i]
                            w = keys(g)
                            act.wait_ge(s_read, i + 1)
                            act.activation(logit[:, i % 2, 0:w], logit[:, i % 2, 0:w], ACT.Exp, bias=nmx[:, g, m, h:h + 1],
                                           accum_out=l_sum[:, g, m, h:h + 1]).then_inc(p_done, 1)
                        if i >= 1:
                            j = i - 1
                            w = keys(units[j][0])
                            act.wait_ge(t_done, j + 1)
                            if j >= 2:
                                act.wait_ge(pv_done, j - 1)
                            act.copy(pT[:, j % 2, :, :].rearrange("p c q -> p (c q)")[:, 0:w],
                                     ps[:, 2 + j % 2, 0:w]).then_inc(t_read, 1)
                    act.wait_ge(o_done, N)
                    act.activation(l_sum[:, :, :, :], l_sum[:, :, :, :], ACT.Ln).then_inc(lse_a, 1)

        lse, mx, tot = sb("lse", [P, NG, NT, AH]), sb("mx", [P, NT, AH]), sb("tot", [P, NT, AH])
        acc = sb("acc", [P, NT, AH * P])
        back, mv, ma = k.sem(name + "_m_in"), k.sem(name + "_m_dve"), k.sem(name + "_m_act")
        with nc.Block() as block:
            @block.sync
            def _(sp):
                for g in range(NG):
                    sp.dma_start(lse[:, g, :, :], lse_scratch[g].rearrange("(m p) c -> p m c", p=P)).then_inc(back, 16)
                    sp.dma_start(o[:, g, :, :], o_scratch[g].rearrange("(m p) c -> p m c", p=P)).then_inc(back, 16)

            @block.vector
            def _(dve):
                v = Chain(dve, mv)
                dve.wait_ge(back, 16 * 2 * NG)
                v(dve.tensor_tensor(mx[:, :, :], lse[:, 0, :, :], lse[:, 1, :, :], ALU.max))
                v(dve.tensor_tensor(mx[:, :, :], mx[:, :, :], lse[:, 2, :, :], ALU.max))
                v(dve.tensor_tensor(lse[:, :, :, :], lse[:, :, :, :], mx[:, :, :].unsqueeze(1).to_broadcast([P, NG, NT, AH]),
                                    ALU.subtract))
                dve.wait_ge(ma, 1)
                v(dve.tensor_tensor(tot[:, :, :], lse[:, 0, :, :], lse[:, 1, :, :], ALU.add))
                v(dve.tensor_tensor(tot[:, :, :], tot[:, :, :], lse[:, 2, :, :], ALU.add))
                v(dve.reciprocal(tot[:, :, :], tot[:, :, :]))
                v(dve.tensor_tensor(lse[:, :, :, :], lse[:, :, :, :], tot[:, :, :].unsqueeze(1).to_broadcast([P, NG, NT, AH]),
                                    ALU.mult))
                for g in range(NG):
                    og = o[:, g, :, :].rearrange("p m (h c) -> p (m h) c", h=AH)
                    w = lse[:, g, :, :].rearrange("p m h -> p (m h)").unsqueeze(2).to_broadcast([P, NT * AH, P])
                    v(dve.tensor_tensor(og, og, w, ALU.mult))
                v(dve.tensor_tensor(acc[:, :, :], o[:, 0, :, :], o[:, 1, :, :], ALU.add))
                v(dve.tensor_tensor(acc[:, :, :], acc[:, :, :], o[:, 2, :, :], ALU.add))

            @block.scalar
            def _(act):
                act.wait_ge(mv, 3)
                act.activation(lse[:, :, :, :], lse[:, :, :, :], ACT.Exp).then_inc(ma, 1)
        turn_and_split(k, name, lambda h, m: acc[:, m, h * P:(h + 1) * P], *outT)


SETS = 2 * PH
MHN = NT * PH


def peer_route(k, name, qh_dram, sub_keysT, iota_dram, idxT, gateT):
    nc, ps = k.nc, k.ps
    with ExitStack() as es:
        def sb(n, shape, dt=F32):
            return es.enter_context(nc.sbuf_tensor(name + "_" + n, shape, dt))
        sv, si = sb("sv", [P, NT, SETS, TOPK]), sb("si", [P, NT, SETS, TOPK], U32)
        sif = sb("sif", [P, NT, SETS, TOPK])
        landed, scored, val_a, idx_a, cut, val_b, top = (k.sem(name + "_landed"), k.sem(name + "_scored"),
                                                         k.sem(name + "_val_a"), k.sem(name + "_idx_a"), k.sem(name + "_cut"),
                                                         k.sem(name + "_val_b"), k.sem(name + "_top"))
        with (nc.sbuf_tensor(name + "_qT", [P, SETS, T], F32) as qT, nc.sbuf_tensor(name + "_kT", [P, SETS, NKEY], F32) as kT,
              nc.sbuf_tensor(name + "_rest", [P, SETS, NKEY], F32) as rest, nc.Block() as block):
            @block.sync
            def _(sp):
                sp.dma_start(qT[:, :, :], qh_dram).then_inc(landed, 16)
                sp.dma_start(kT[:, :, :], sub_keysT).then_inc(landed, 16)

            @block.tensor
            def _(pe):
                pe.wait_ge(landed, 32)
                for m in range(NT):
                    if m >= 2:
                        pe.wait_ge(top, SETS * (m - 1))
                    for s in range(SETS):
                        last = pe.matmul(ps[:, 4 * (m % 2) + s // 4, (s % 4) * NKEY:(s % 4 + 1) * NKEY],
                                         qT[:, s, m * P:(m + 1) * P], kT[:, s, :], start=True, stop=True)
                    last.then_inc(scored, 1)

            @block.vector
            def _(dve):
                for m in range(NT):
                    dve.wait_ge(scored, m + 1)
                    S = lambda s: ps[:, 4 * (m % 2) + s // 4, (s % 4) * NKEY:(s % 4 + 1) * NKEY]
                    n = m * SETS
                    for s in range(SETS):
                        dve.max(sv[:, m, s, 0:8], S(s)).then_inc(val_a, 1)
                    for s in range(SETS):
                        dve.wait_ge(val_a, n + s + 1)
                        dve.max_index(si[:, m, s, 0:8], sv[:, m, s, 0:8], S(s)).then_inc(idx_a, 1)
                        if m:
                            dve.wait_ge(top, n)
                        dve.match_replace(rest[:, s, :], sv[:, m, s, 0:8], S(s), -3e38).then_inc(cut, 1)
                    for s in range(SETS):
                        dve.wait_ge(cut, n + s + 1)
                        dve.max(sv[:, m, s, 8:16], rest[:, s, :]).then_inc(val_b, 1)
                    for s in range(SETS):
                        dve.wait_ge(val_b, n + s + 1)
                        dve.max_index(si[:, m, s, 8:16], sv[:, m, s, 8:16], rest[:, s, :]).then_inc(top, 1)

        cand, rest2 = sb("cand", [P, MHN, TOPK, TOPK]), sb("rest2", [P, MHN, TOPK * TOPK])
        cv, ci = sb("cv", [P, MHN, TOPK]), sb("ci", [P, MHN, TOPK], U32)
        digit, digf, i12 = sb("digit", [P, MHN, TOPK], U32), sb("digf", [P, MHN, TOPK]), sb("i12", [P, 2, MHN, TOPK])
        ej, iota = sb("exp", [P, MHN, TOPK]), sb("iota", [P, TOPK])
        tot = sb("tot", [P, MHN])
        cd, i_in, a_done, turned = k.sem(name + "_c_dve"), k.sem(name + "_iota_in"), k.sem(name + "_exp_act"), k.sem(name + "_turned")
        val_a, cut, val_b, top, fin = (k.sem(name + "_c_val_a"), k.sem(name + "_c_cut"), k.sem(name + "_c_val_b"),
                                       k.sem(name + "_c_top"), k.sem(name + "_c_fin"))
        ready = k.sem(name + "_ready")
        with nc.Block() as block:
            four = [P, MHN, TOPK, TOPK]
            pair = lambda t, c: t[:, :, :, :].rearrange("p m (h c) i -> p (m h) c i", c=2)[:, :, c, :]

            @block.sync
            def _(sp):
                sp.dma_start(iota[:, :], iota_dram.partition_broadcast(P)).then_inc(i_in, 16)

            @block.vector
            def _(dve):
                v = Chain(dve, cd)
                v(dve.tensor_copy(sif[:, :, :, :], si[:, :, :, :]))
                v(dve.tensor_tensor(cand[:, :, :, :], pair(sv, 0).unsqueeze(3).to_broadcast(four),
                                    pair(sv, 1).unsqueeze(2).to_broadcast(four), ALU.add))
                C = lambda n: cand[:, n, :, :].rearrange("p a b -> p (a b)")
                for n in range(MHN):
                    dve.max(cv[:, n, 0:8], C(n)).then_inc(val_a, 1)
                for n in range(MHN):
                    dve.wait_ge(val_a, n + 1)
                    dve.max_index(ci[:, n, 0:8], cv[:, n, 0:8], C(n)).then_inc(top, 1)
                    dve.match_replace(rest2[:, n, :], cv[:, n, 0:8], C(n), -3e38).then_inc(cut, 1)
                for n in range(MHN):
                    dve.wait_ge(cut, n + 1)
                    dve.max(cv[:, n, 8:16], rest2[:, n, :]).then_inc(val_b, 1)
                for n in range(MHN):
                    dve.wait_ge(val_b, n + 1)
                    dve.max_index(ci[:, n, 8:16], cv[:, n, 8:16], rest2[:, n, :]).then_inc(top, 1)
                v(dve.tensor_tensor(ej[:, :, :], cv[:, :, :], cv[:, :, 0:1].to_broadcast([P, MHN, TOPK]), ALU.subtract))
                dve.wait_ge(top, 2 * MHN)
                dve.wait_ge(i_in, 16)
                for c in range(2):
                    if c == 0:
                        v(dve.tensor_scalar(digit[:, :, :], ci[:, :, :], 4, None, ALU.logical_shift_right))
                    else:
                        v(dve.tensor_scalar(digit[:, :, :], ci[:, :, :], 15, None, ALU.bitwise_and))
                    v(dve.tensor_copy(digf[:, :, :], digit[:, :, :]))
                    v(dve.tensor_tensor(cand[:, :, :, :], digf[:, :, :].unsqueeze(3).to_broadcast(four),
                                        iota[:, :].unsqueeze(1).unsqueeze(1).to_broadcast(four), ALU.is_equal))
                    v(dve.tensor_tensor(cand[:, :, :, :], cand[:, :, :, :], pair(sif, c).unsqueeze(2).to_broadcast(four), ALU.mult))
                    v(dve.tensor_reduce(i12[:, c, :, :], cand[:, :, :, :], AX.X, ALU.add))
                v(dve.scalar_tensor_tensor(i12[:, 0, :, :], i12[:, 0, :, :], float(NKEY), i12[:, 1, :, :], ALU.mult, ALU.add))
                dve.wait_ge(a_done, 1)
                v(dve.tensor_reduce(tot[:, :], ej[:, :, :], AX.X, ALU.add))
                v(dve.reciprocal(tot[:, :], tot[:, :]))
                v(dve.tensor_tensor(ej[:, :, :], ej[:, :, :], tot[:, :].unsqueeze(2).to_broadcast([P, MHN, TOPK]), ALU.mult))
                dve.sem_inc(ready, 1)
                dve.wait_ge(turned, 1)
                dve.tensor_copy(idxT[:, :], ps[:, 0, :]).then_inc(fin, 1)
                dve.tensor_copy(gateT[:, :], ps[:, 1, :]).then_inc(fin, 1)

            @block.scalar
            def _(act):
                act.wait_ge(cd, 3)
                act.activation(ej[:, :, :], ej[:, :, :], ACT.Exp).then_inc(a_done, 1)

            @block.tensor
            def _(pe):
                pe.wait_ge(ready, 1)
                for b, src in ((0, i12[:, 0, :, :]), (1, ej[:, :, :])):
                    for m in range(NT):
                        last = pe.transpose(ps[:, b, m * P:(m + 1) * P],
                                            src[:, m * PH:(m + 1) * PH, :].rearrange("p h j -> p (h j)"), k.ident[:, :])
                last.then_inc(turned, 1)


GRP = 32
UR, VR, BATCH = 8, 16, 8
LAG = BATCH + 2


def peer_split(k, name, xnT, xs):
    nc, ps = k.nc, k.ps
    turned, copied, chain, parts, moved = (k.sem(name + "_turned"), k.sem(name + "_copied"), k.sem(name + "_chain"),
                                           k.sem(name + "_parts"), k.sem(name + "_moved"))
    with (nc.sbuf_tensor(name + "_tok", [P, NT, D], F32) as tok, nc.sbuf_tensor(name + "_part", [P, 3, NT, D], BF16) as part,
          nc.Block() as block):
        @block.tensor
        def _(pe):
            for m in range(NT):
                for c in range(NC_D):
                    last = pe.transpose(ps[:, 2 * m + c // 4, (c % 4) * P:(c % 4 + 1) * P], xnT[:, c, m * P:(m + 1) * P],
                                        k.ident[:, :])
                last.then_inc(turned, 1)

        @block.vector
        def _(dve):
            v = Chain(dve, chain)
            for m in range(NT):
                dve.wait_ge(turned, m + 1)
                v(dve.tensor_copy(tok[:, m, :].rearrange("p (b c) -> p b c", b=2), ps[:, 2 * m:2 * m + 2, :]))
            for q in range(3):
                v(dve.tensor_copy(part[:, q, :, :], tok[:, :, :]))
                dve.sem_inc(parts, 1)
                if q < 2:
                    v(dve.tensor_tensor(tok[:, :, :], tok[:, :, :], part[:, q, :, :], ALU.subtract))

        @block.sync
        def _(sp):
            for q in range(3):
                sp.wait_ge(parts, q + 1)
                for a in range(4):
                    sp.dma_start(xs[GRP * q:GRP * (q + 1), :, :].rearrange("p (m a) d -> p m a d", a=4)[:, :, a, :],
                                 part[GRP * a:GRP * (a + 1), q, :, :]).then_inc(moved, 16)
            sp.wait_ge(moved, 16 * 12)


def peer_experts(k, name, xs, sel_dram, idxT, gateT, u_rows, v_rows):
    nc, ps = k.nc, k.ps
    sem = lambda n: k.sem(name + "_" + n)
    u_in = [k.gather_sem(f"{name}_u_in{s}") for s in range(UR)]
    v_in = [k.gather_sem(f"{name}_v_in{s}") for s in range(VR)]
    dots, v_used, x_wide, acts, gelus = sem("dots"), sem("v_used"), sem("x_wide"), sem("acts"), sem("gelus")
    weights, y_done, y_kept, y_turned, added = sem("weights"), sem("y_done"), sem("y_kept"), sem("y_turned"), sem("added")
    slot_free, turning = sem("slot_free"), sem("turning")
    idx_a, idx_b, start, s_in = sem("idx_a"), sem("idx_b"), sem("start"), sem("sel_in")
    TURNS = T // GRP
    NB = GRP // BATCH
    with ExitStack() as es:
        def sb(n, shape, dt=F32):
            return es.enter_context(nc.sbuf_tensor(name + "_" + n, shape, dt))
        U, V = sb("U", [P, UR, D]), sb("V", [P, VR, D])
        junk, act_in, act_out = sb("junk", [P, D]), sb("act_in", [P, 2, BATCH]), sb("act_out", [P, 2, BATCH])
        WZ, idx = sb("WZ", [P, GRP * GRP + GRP]), sb("idx", [P, 2, GRP // 2], I32)
        self_, sel, y = sb("self", [3 * GRP, GRP]), sb("sel", [3 * GRP, GRP, P], BF16), sb("y", [GRP, D])
        diag = WZ[:, :].rearrange("p (s c) -> p s c", c=GRP + 1)[:, 0:GRP, 0]

        with nc.Block() as block:
            @block.sync
            def _(sp):
                sp.dma_start(self_[:, :], sel_dram).then_inc(s_in, 16)

            @block.gpsimd
            def _(pool):
                with pool.Fori(0, TURNS) as it:
                    for half in range(2):
                        pool.wait_ge(dots, it * GRP + half * 16 + UR + 1 - UR)
                        pool.wait_ge(v_used, it * GRP + half * 16 + 1)
                        done = (idx_a, idx_b)[half]
                        pool.tensor_copy(idx[:, half, :], idxT[:, bass.ds(it * GRP + half * 16, 16)]).then_inc(done, 1)
                        pool.wait_ge(done, it + 1)
                        for j in range(16):
                            s = half * 16 + j
                            pool.wait_ge(dots, it * GRP + (s + 1))
                            pool.sem_inc(slot_free, 1)
                            pool.indirect_dma_start(U[:, s % UR, :], None, u_rows,
                                                    bass.IndirectOffsetOnAxis(ap=idx[:, half, j:j + 1], axis=0)
                                                    ).then_inc(u_in[s % UR], 16)
                            pool.wait_ge(v_used, it * GRP + (s + 1))
                            pool.sem_inc(slot_free, 1)
                            pool.indirect_dma_start(V[:, s % VR, :], None, v_rows,
                                                    bass.IndirectOffsetOnAxis(ap=idx[:, half, j:j + 1], axis=0)
                                                    ).then_inc(v_in[s % VR], 16)

            @block.tensor
            def _(pe):
                pe.sem_inc(v_used, VR)
                pe.wait_ge(start, 2)
                with pe.Fori(0, TURNS) as it:
                    def widen(s):
                        pe.wait_ge(dots, it * GRP + (s + UR - 1))
                        for c in range(2):
                            last = pe.matmul(ps[:, 2 + 2 * (s % 2) + c, :], sel[:, s, :], xs[:, it, c * 512:(c + 1) * 512],
                                             start=True, stop=True)
                        last.then_inc(x_wide, 1)

                    def combine(s):
                        b = s // BATCH
                        if s % BATCH == 0:
                            pe.wait_ge(weights, it * NB + (b + 1))
                        if s == 0:
                            pe.wait_ge(y_kept, it + 1)
                        pe.wait_ge(v_in[s % VR], (it * (GRP // VR) + (s // VR + 1)) * 16)
                        for c in range(2):
                            last = pe.matmul(ps[0:GRP, c, :], WZ[:, s * GRP:(s + 1) * GRP], V[:, s % VR, c * 512:(c + 1) * 512],
                                             start=(s == 0), stop=(s == GRP - 1))
                        last.then_inc(v_used, 1)

                    for s in range(GRP + LAG):
                        if s < GRP:
                            widen(s)
                        if s >= LAG:
                            combine(s - LAG)
                    pe.wait_ge(y_kept, it + 2)
                    pe.wait_ge(added, it + 1)
                    pe.sem_inc(turning, 1)
                    for c in range(NC_D):
                        last = pe.transpose(ps[:, 6, c * GRP:(c + 1) * GRP], y[:, c * P:(c + 1) * P], k.ident[0:GRP, 0:GRP])
                    last.then_inc(y_turned, 1)

            @block.vector
            def _(dve):
                dve.wait_ge(s_in, 16)
                dve.memset(WZ[:, :], 0.0).then_inc(start, 1)
                dve.tensor_copy(sel[:, :, :], self_[:, :].unsqueeze(2).to_broadcast([3 * GRP, GRP, P])).then_inc(start, 1)
                dve.wait_ge(start, 2)
                dve.sem_inc(dots, UR)
                dve.sem_inc(y_kept, 1)
                dve.sem_inc(added, 1)
                with dve.Fori(0, TURNS) as it:
                    def weigh(b):
                        dve.wait_ge(gelus, it * NB + (b + 1))
                        dve.wait_ge(v_used, it * GRP + (b * BATCH + BATCH - GRP + VR)) if b * BATCH + BATCH - GRP + VR > 0 else None
                        dve.tensor_tensor(diag[:, b * BATCH:(b + 1) * BATCH], act_out[:, b % 2, :],
                                          gateT[:, bass.ds(it * GRP + b * BATCH, BATCH)], ALU.mult).then_inc(weights, 1)

                    for b in range(NB):
                        for s in range(b * BATCH, (b + 1) * BATCH):
                            dve.wait_ge(u_in[s % UR], (it * NB + (b + 1)) * 16)
                            dve.wait_ge(x_wide, it * GRP + (s + 1))
                            dve.wait_ge(dots, it * GRP + (s + UR))
                            n = 2 + 2 * (s % 2)
                            dve.tensor_tensor_reduce(junk[:, :].rearrange("p (a c) -> p a c", a=2),
                                                     U[:, s % UR, :].rearrange("p (a c) -> p a c", a=2), ps[:, n:n + 2, :],
                                                     1.0, 0.0, ALU.mult, ALU.add,
                                                     act_in[:, b % 2, s % BATCH:s % BATCH + 1]).then_inc(dots, 1)
                            if b > 0 and s % BATCH == LAG - BATCH - 1:
                                weigh(b - 1)
                    weigh(NB - 1)
                    dve.wait_ge(y_done, it + 1)
                    dve.tensor_copy(y[:, :].rearrange("p (a c) -> p a c", a=2), ps[0:GRP, 0:2, :]).then_inc(y_kept, 1)
                    dve.wait_ge(y_turned, it + 1)
                    r = k.resid[:, :, bass.ds(it * GRP, GRP)]
                    dve.tensor_tensor(r, r, ps[:, 6, 0:NC_D * GRP].rearrange("p (c i) -> p c i", c=NC_D), ALU.add).then_inc(added, 1)

            @block.scalar
            def _(act):
                with act.Fori(0, TURNS) as it:
                    for b in range(NB):
                        act.wait_ge(dots, it * GRP + ((b + 1) * BATCH + UR))
                        act.wait_ge(weights, it * NB + (b - 1)) if b >= 2 else None
                        act.activation(act_out[:, b % 2, :], act_in[:, b % 2, :], ACT.Gelu_apprx_tanh).then_inc(gelus, 1)
                    act.wait_ge(v_used, it * GRP + (GRP + VR))
                    act.sem_inc(y_done, 1)


QD = M_NOPE + M_ROPE


def block2_tables():
    f = lambda a: np.ascontiguousarray(np.asarray(a).astype(np.float32))
    i = np.arange(P)
    t = {}
    def rot(n, half, base):
        r = np.zeros((n, n), np.float32)
        for m in base:
            for j in range(half):
                r[m + half + j, m + j] = -1.0
                r[m + j, m + half + j] = 1.0
        return r
    t["rot_r"] = rot(P, RD // 2, (0, RD))
    t["rot_m"] = rot(QD, M_ROPE // 2, (M_NOPE,))
    inv = lambda dim: np.float32(10000.0) ** (-np.arange(0, dim, 2, dtype=np.float32) / np.float32(dim))
    t["inv_r"] = f(inv(RD)[i % (RD // 2)])[:, None]
    t["inv_m"] = f(inv(M_ROPE)[i % (M_ROPE // 2)])[:, None]
    cm = np.zeros((P, T), np.float32)
    cm[:, T - P:] = np.where(i[None, :] <= i[:, None], 0.0, NEG)
    t["causal"] = cm
    t["later"] = f(i[:, None] > i[None, :])
    t["before"] = f(i[:, None] < i[None, :])
    lg = np.log1p(-np.exp2(-5.0 - np.arange(RH, dtype=np.float64)))
    d = i[None, :] - i[:, None]
    t["decay"] = f(np.where(d[:, None, :] >= 0, np.exp(np.maximum(d, 0)[:, None, :] * lg[None, :, None]), 0.0) * RD ** -0.5)
    t["zeta"] = f(np.exp((P - 1 - i)[:, None] * lg[None, :]) * RD ** -0.5)
    t["xi"] = f(np.exp((i + 1.0)[:, None] * lg[None, :]))
    pairs = 2 * np.arange(RH // 2)[None, :] + (i // RD)[:, None]
    t["chunk_decay"] = f(np.exp(P * lg)[pairs])
    t["pair"] = f((i[:, None] // RD) == (i[None, :] // RD))
    return t


def rope_tables(k, name, pos, inv_r, inv_m, cos_r, sin_r, cos_m, sin_m):
    nc = k.nc
    c1 = 6.28125
    c2 = float(np.float32(np.floor((2 * math.pi - c1) * 2 ** 21) / 2 ** 21))
    c3 = float(2 * math.pi - c1 - c2)
    TOP = 3.1415925
    landed, step, done = k.sem(name + "_landed"), k.sem(name + "_step"), k.sem(name + "_done")
    with (nc.sbuf_tensor(name + "_pi", [P, T], I32) as pi, nc.sbuf_tensor(name + "_pf", [P, T], F32) as pf,
          nc.sbuf_tensor(name + "_n", [P, 2, T], F32) as n, nc.sbuf_tensor(name + "_r", [P, 2, T], F32) as r,
          nc.sbuf_tensor(name + "_c", [P, 2, T], F32) as c, nc.sbuf_tensor(name + "_iv", [P, 2], F32) as iv,
          nc.Block() as block):
        @block.sync
        def _(sp):
            sp.dma_start(pi[:, :], pos.partition_broadcast(P)).then_inc(landed, 16)
            sp.dma_start(iv[:, 0:1], inv_r).then_inc(landed, 16)
            sp.dma_start(iv[:, 1:2], inv_m).then_inc(landed, 16)

        @block.vector
        def _(dve):
            v = Chain(dve, step)
            dve.wait_ge(landed, 48)
            v(dve.tensor_copy(pf[:, :], pi[:, :]))
            for j in range(2):
                v(dve.tensor_scalar(r[:, j, :], pf[:, :], iv[:, j:j + 1], None, ALU.mult))
            v(dve.tensor_scalar(n[:, :, :], r[:, :, :], 1.0 / (2 * math.pi), 12582912.0, ALU.mult, ALU.add))
            v(dve.tensor_scalar(n[:, :, :], n[:, :, :], -12582912.0, None, ALU.add))
            for part in (c1, c2, c3):
                v(dve.scalar_tensor_tensor(r[:, :, :], n[:, :, :], -part, r[:, :, :], ALU.mult, ALU.add))
            v(dve.tensor_scalar(n[:, :, :], r[:, :, :], math.pi / 2, -2 * math.pi, ALU.is_gt, ALU.mult))
            v(dve.scalar_tensor_tensor(c[:, :, :], r[:, :, :], math.pi / 2, n[:, :, :], ALU.add, ALU.add))
            v(dve.tensor_scalar(c[:, :, :], c[:, :, :], TOP, -TOP, ALU.min, ALU.max))
            v(dve.tensor_scalar(r[:, :, :], r[:, :, :], TOP, -TOP, ALU.min, ALU.max))

        @block.scalar
        def _(act):
            act.wait_ge(step, 12)
            for dst, src in ((cos_r, c[:, 0, :]), (sin_r, r[:, 0, :]), (cos_m, c[:, 1, :]), (sin_m, r[:, 1, :])):
                act.activation(dst[:, :], src, ACT.Sin).then_inc(done, 1)


def project_latent(k, name, x, w_dram, cT):
    nc, ps = k.nc, k.ps
    n = (M_QR + M_KVR) // P
    landed = [k.sem(f"{name}_landed{s}") for s in range(2)]
    hi_done, lo_done, product, copied = (k.sem(name + "_hi"), k.sem(name + "_lo"), k.sem(name + "_product"),
                                         k.sem(name + "_copied"))
    xh, xl = x
    with (nc.sbuf_tensor(name + "_w", [P, 2, NC_D, P], F32) as w, nc.sbuf_tensor(name + "_w_high", [P, 2, NC_D, P], F32R) as hi,
          nc.sbuf_tensor(name + "_w_low", [P, 2, NC_D, P], F32R) as lo, nc.Block() as block):
        @block.sync
        def _(sp):
            for a in range(n):
                if a >= 2:
                    sp.wait_ge(product, a - 1)
                sp.dma_start(w[:, a % 2, :, :], w_dram[:, :, a * P:(a + 1) * P]).then_inc(landed[a % 2], 16)

        @block.scalar
        def _(act):
            for a in range(n):
                act.wait_ge(landed[a % 2], 16 * (a // 2 + 1))
                act.copy(hi[:, a % 2, :, :], w[:, a % 2, :, :]).then_inc(hi_done, 1)

        @block.tensor
        def _(pe):
            for a in range(n):
                pe.wait_ge(lo_done, a + 1)
                for c in range(NC_D):
                    for p, (wp, xp) in enumerate(((hi, xh), (lo, xh), (hi, xl))):
                        last = pe.matmul(ps[:, a, :], wp[:, a % 2, c, :], xp[:, c, :], start=(c == 0 and p == 0),
                                         stop=(c == NC_D - 1 and p == 2))
                last.then_inc(product, 1)

        @block.vector
        def _(dve):
            for a in range(n + 1):
                if a < n:
                    dve.wait_ge(hi_done, a + 1)
                    dve.tensor_tensor(lo[:, a % 2, :, :], w[:, a % 2, :, :], hi[:, a % 2, :, :].bitcast(F32),
                                      ALU.subtract).then_inc(lo_done, 1)
                if a >= 1:
                    dve.wait_ge(product, a)
                    dve.tensor_copy(cT[:, a - 1, :], ps[:, a - 1, :]).then_inc(copied, 1)


def latent_attention(k, name, cT, peT, uq_dram, ukv_dram, rot_m, cos_m, sin_m, causal, outT):
    nc, ps = k.nc, k.ps
    rope = slice(M_NOPE, QD)
    with ExitStack() as es:
        def sb(n, shape, dt=F32):
            return es.enter_context(nc.sbuf_tensor(name + "_" + n, shape, dt))
        sem = lambda n: k.sem(name + "_" + n)
        qT, kT, v = sb("qT", [QD, MH, T]), sb("kT", [QD, MH, T]), sb("v", [P, NT, MH * M_V])
        y = sb("y", [P, NT, MH * M_V])
        with (nc.sbuf_tensor(name + "_wq", [P, 3, MH * QD], F32) as wq, nc.sbuf_tensor(name + "_wkv", [P, 2, MH, P], F32) as wkv,
              nc.sbuf_tensor(name + "_t", [QD, 2, T], F32) as t, nc.Block() as block):
            landed, prod, rot, kept, free, chain = sem("w_in"), sem("prod"), sem("rot"), sem("kept"), sem("bank_free"), sem("chain_r")

            @block.sync
            def _(sp):
                sp.dma_start(wq[:, :, :], uq_dram).then_inc(landed, 16)
                sp.dma_start(wkv[:, :, :, :], ukv_dram).then_inc(landed, 16)

            @block.tensor
            def _(pe):
                pe.wait_ge(landed, 32)
                for s in range(21):
                    if s >= 2:
                        pe.wait_ge(free, s - 1)
                    o = ps[:, s % 2, :]
                    if s < 8:
                        for c in range(3):
                            last = pe.matmul(o[0:QD, :], wq[:, c, s * QD:(s + 1) * QD], cT[:, c, :], start=(c == 0), stop=(c == 2))
                        last.then_inc(prod, 1)
                    elif 8 < s < 17:
                        for c in range(2):
                            last = pe.matmul(o[0:M_NOPE, :], wkv[:, c, s - 9, 0:M_NOPE], cT[:, 3 + c, :], start=(c == 0), stop=(c == 1))
                        last.then_inc(prod, 1)
                    elif s >= 17:
                        m = s - 17
                        for c in range(2):
                            last = pe.matmul(o, cT[:, 3 + c, m * P:(m + 1) * P], wkv[:, c, :, M_NOPE:P], start=(c == 0), stop=(c == 1))
                        last.then_inc(prod, 1)
                    if s <= 8:
                        if s < 8:
                            pe.wait_ge(kept, s + 1)
                        src = qT[:, s, :] if s < 8 else peT[:, :]
                        pe.matmul(ps[0:QD, 2 + s % 2, :], rot_m[:, :], src, start=True, stop=True).then_inc(rot, 1)

            @block.vector
            def _(dve):
                v_ = Chain(dve, chain)
                for s in range(21):
                    if s < 8:
                        dve.wait_ge(prod, s + 1)
                        dve.tensor_copy(qT[:, s, :], ps[0:QD, s % 2, :]).then_inc(kept, 1)
                        dve.wait_ge(kept, s + 1)
                    if s <= 8:
                        src = qT[rope, s, :] if s < 8 else peT[rope, :]
                        dve.wait_ge(rot, s + 1)
                        v_(dve.tensor_tensor(t[rope, 0, :], src, cos_m[rope, :], ALU.mult))
                        v_(dve.tensor_tensor(t[rope, 1, :], ps[rope, 2 + s % 2, :], sin_m[rope, :], ALU.mult))
                        v_(dve.tensor_tensor(src, t[rope, 0, :], t[rope, 1, :], ALU.add))
                        dve.sem_inc(free, 1)
                    elif s < 17:
                        h = s - 9
                        dve.wait_ge(prod, s)
                        dve.tensor_copy(kT[0:M_NOPE, h, :], ps[0:M_NOPE, s % 2, :]).then_inc(chain, 1)
                        dve.tensor_copy(kT[rope, h, :], peT[rope, :]).then_inc(free, 1)
                        v_.n += 1
                        dve.wait_ge(chain, v_.n)
                    else:
                        dve.wait_ge(prod, s)
                        dve.tensor_copy(v[:, s - 17, :], ps[:, s % 2, :]).then_inc(free, 1)

        units = [(m, h) for m in range(NT) for h in range(MH)]
        N = len(units)
        with (nc.sbuf_tensor(name + "_logit", [P, 2, T], F32) as logit, nc.sbuf_tensor(name + "_pT", [P, 2, T], F32) as pT,
              nc.sbuf_tensor(name + "_st", [P, 3, N], F32) as st, nc.Block() as block):
            nmx, ls, rl = st[:, 0, :], st[:, 1, :], st[:, 2, :]
            s_done, s_read, p_done, t_done, t_read, pv_done, o_done, chain = (
                sem("s_done"), sem("max_done"), sem("p_done"), sem("t_done"), sem("t_read"), sem("pv_done"), sem("o_done"),
                sem("chain"))

            @block.tensor
            def _(pe):
                for i in range(N + 2):
                    if i < N:
                        m, h = units[i]
                        if i >= 2:
                            pe.wait_ge(s_read, i - 1)
                        pe.matmul(ps[:, i % 2, 0:(m + 1) * P], qT[:, h, m * P:(m + 1) * P], kT[:, h, 0:(m + 1) * P],
                                  start=True, stop=True).then_inc(s_done, 1)
                    if 1 <= i <= N:
                        j = i - 1
                        m, h = units[j]
                        pe.wait_ge(p_done, j + 1)
                        if j >= 2:
                            pe.wait_ge(t_read, j - 1)
                        for c in range(m + 1):
                            last = pe.transpose(ps[:, 2 + j % 2, c * P:(c + 1) * P], logit[:, j % 2, c * P:(c + 1) * P], k.ident[:, :])
                        last.then_inc(t_done, 1)
                    if i >= 2:
                        j = i - 2
                        m, h = units[j]
                        pe.wait_ge(t_read, j + 1)
                        if j >= 2:
                            pe.wait_ge(o_done, j - 1)
                        for c in range(m + 1):
                            last = pe.matmul(ps[:, 4 + j % 2, 0:M_V], pT[:, j % 2, c * P:(c + 1) * P],
                                             v[:, c, h * M_V:(h + 1) * M_V], start=(c == 0), stop=(c == m))
                        last.then_inc(pv_done, 1)

            @block.vector
            def _(dve):
                v_ = Chain(dve, chain)
                for i in range(N + 2):
                    if i < N:
                        m, h = units[i]
                        w = (m + 1) * P
                        dve.wait_ge(s_done, i + 1)
                        if i >= 2:
                            dve.wait_ge(t_done, i - 1)
                        v_(dve.scalar_tensor_tensor(logit[:, i % 2, 0:w], ps[:, i % 2, 0:w], QD ** -0.5, causal[:, T - w:T],
                                                    ALU.mult, ALU.add))
                        dve.tensor_reduce(nmx[:, i:i + 1], logit[:, i % 2, 0:w], AX.X, ALU.max, negate=True).then_inc(s_read, 1)
                    if i >= 2:
                        j = i - 2
                        m, h = units[j]
                        dve.wait_ge(pv_done, j + 1)
                        v_(dve.reciprocal(rl[:, j:j + 1], ls[:, j:j + 1]))
                        dve.tensor_scalar(y[:, m, h * M_V:(h + 1) * M_V], ps[:, 4 + j % 2, 0:M_V], rl[:, j:j + 1], None,
                                          ALU.mult).then_inc(o_done, 1)

            @block.scalar
            def _(act):
                for i in range(N + 1):
                    if i < N:
                        w = (units[i][0] + 1) * P
                        act.wait_ge(s_read, i + 1)
                        act.activation(logit[:, i % 2, 0:w], logit[:, i % 2, 0:w], ACT.Exp, bias=nmx[:, i:i + 1],
                                       accum_out=ls[:, i:i + 1]).then_inc(p_done, 1)
                    if i >= 1:
                        j = i - 1
                        w = (units[j][0] + 1) * P
                        act.wait_ge(t_done, j + 1)
                        if j >= 2:
                            act.wait_ge(pv_done, j - 1)
                        act.copy(pT[:, j % 2, 0:w], ps[:, 2 + j % 2, 0:w]).then_inc(t_read, 1)
        turn_and_split(k, name, lambda j, m: y[:, m, j * P:(j + 1) * P], *outT)


def stick_breaking(k, name, q_dram, k_dram, v_dram, later, before, outT):
    nc, ps = k.nc, k.ps
    W = sum(T - P * j for j in range(NT))
    off = [sum(T - P * j for j in range(kt)) for kt in range(NT)]
    bank = [(0, 0), (1, 0), (2, 0), (2, 2 * P)]
    wid = [T - P * kt for kt in range(NT)]
    with ExitStack() as es:
        def sb(n, shape, dt=F32):
            return es.enter_context(nc.sbuf_tensor(name + "_" + n, shape, dt))
        sem = lambda n: k.sem(name + "_" + n)
        qT, kT, v = sb("qT", [P, 4, T]), sb("kT", [P, 4, T]), sb("v", [P, NT, SBH * SBD])
        z, t, sp_, lb = (sb(n, [P, 2, W]) for n in ("z", "t", "sp", "lb"))
        landed, z_done, z_kept, ln_done, sp_done, lb_done, sums, args, expd, masked, o_done, o_kept, chain = (
            sem("in"), sem("z_done"), sem("z_kept"), sem("ln_done"), sem("sp_done"), sem("lb_done"), sem("sums"), sem("args"),
            sem("exp"), sem("masked"), sem("o_done"), sem("o_kept"), sem("chain"))
        act_chain, y_hi, y_lo = sem("act_chain"), sem("y_hi"), sem("y_lo")
        yT = sb("yT", [P, 4, T])
        y_high, y_low = outT

        def two(b0):
            return ((ps[:, b0:b0 + 2, :].rearrange("p b c -> p (b c)")[:, 0:off[2]], slice(0, off[2])),
                    (ps[:, b0 + 2, 0:wid[2] + wid[3]], slice(off[2], W)))

        with nc.Block() as block:
            @block.sync
            def _(sp):
                sp.dma_start(qT[:, :, :], q_dram).then_inc(landed, 16)
                sp.dma_start(kT[:, :, :], k_dram).then_inc(landed, 16)
                sp.dma_start(v[:, :, :], v_dram).then_inc(landed, 16)

            @block.tensor
            def _(pe):
                def scores(h):
                    if h >= 1:
                        pe.wait_ge(z_kept, h)
                    r = slice(SBD * (h % 2), SBD * (h % 2) + SBD)
                    for kt in range(NT):
                        b, c = bank[kt]
                        last = pe.matmul(ps[:, b, c:c + wid[kt]], kT[r, h // 2, kt * P:(kt + 1) * P], qT[r, h // 2, kt * P:T],
                                         start=True, stop=True)
                    last.then_inc(z_done, 1)

                pe.wait_ge(landed, 48)
                scores(0)
                for h in range(SBH):
                    if h + 1 < SBH:
                        scores(h + 1)
                    pe.wait_ge(sp_done, h + 1)
                    if h >= 1:
                        pe.wait_ge(args, h)
                    for kt in range(NT):
                        b, c = bank[kt]
                        for j in range(kt, NT):
                            o = ps[:, 3 + b, c + (j - kt) * P:c + wid[kt]]
                            last = pe.matmul(o, later[:, :] if j == kt else k.ones[:, :], sp_[:, h % 2, off[j]:off[j] + wid[j]],
                                             start=(j == kt), stop=(j == NT - 1))
                    last.then_inc(sums, 1)
                    pe.wait_ge(masked, h + 1)
                    if h >= 1:
                        pe.wait_ge(o_kept, h)
                    for kt in range(NT):
                        last = pe.matmul(ps[0:SBD, 6, kt * P:T], v[:, kt, h * SBD:(h + 1) * SBD], lb[:, h % 2, off[kt]:off[kt] + wid[kt]],
                                         start=(kt == 0), stop=(kt == NT - 1))
                    last.then_inc(o_done, 1)

            @block.vector
            def _(dve):
                v_ = Chain(dve, chain)

                def mask(buf, h):
                    for kt in range(NT):
                        d = buf[:, h % 2, off[kt]:off[kt] + P]
                        ins = dve.tensor_tensor(d, d, before[:, :], ALU.mult)
                        ins.then_inc(chain, 1)
                        v_.n += 1
                    dve.wait_ge(chain, v_.n)

                def keep(h):
                    dve.wait_ge(z_done, h + 1)
                    for src, cols in two(0):
                        v_(dve.tensor_scalar(z[:, h % 2, cols], src, SBD ** -0.5, None, ALU.mult))
                    dve.sem_inc(z_kept, 1)

                keep(0)
                for h in range(SBH):
                    zz, tt, ss, ll = (b[:, h % 2, :] for b in (z, t, sp_, lb))
                    if h + 1 < SBH:
                        keep(h + 1)
                    dve.wait_ge(ln_done, h + 1)
                    if h >= 2:
                        dve.wait_ge(o_done, h - 1)
                    v_(dve.scalar_tensor_tensor(ss, zz, 0.0, tt, ALU.max, ALU.add))
                    v_(dve.tensor_tensor(ll, zz, ss, ALU.subtract))
                    mask(sp_, h)
                    dve.sem_inc(sp_done, 1)
                    dve.wait_ge(sums, h + 1)
                    for src, cols in two(3):
                        v_(dve.tensor_tensor(lb[:, h % 2, cols], lb[:, h % 2, cols], src, ALU.subtract))
                    dve.sem_inc(args, 1)
                    dve.wait_ge(expd, h + 1)
                    mask(lb, h)
                    dve.sem_inc(masked, 1)
                for j in range(4):
                    dve.wait_ge(y_hi, j + 1)
                    dve.tensor_tensor(y_low[:, j, :], yT[:, j, :], y_high[:, j, :].bitcast(F32), ALU.subtract).then_inc(y_lo, 1)

            @block.scalar
            def _(act):
                a = Chain(act, act_chain)

                def log1p(h):
                    zz, tt = z[:, h % 2, :], t[:, h % 2, :]
                    act.wait_ge(z_kept, h + 1)
                    a(act.activation(tt, zz, ACT.Abs))
                    a(act.activation(tt, tt, ACT.Exp, scale=-1.0))
                    act.activation(tt, tt, ACT.Ln, bias=1.0).then_inc(ln_done, 1)

                log1p(0)
                for h in range(SBH):
                    if h + 1 < SBH:
                        log1p(h + 1)
                    act.wait_ge(args, h + 1)
                    act.activation(lb[:, h % 2, :], lb[:, h % 2, :], ACT.Exp).then_inc(expd, 1)
                    act.wait_ge(o_done, h + 1)
                    act.copy(yT[SBD * (h % 2):SBD * (h % 2) + SBD, h // 2, :], ps[0:SBD, 6, :]).then_inc(o_kept, 1)
                    if h % 2 == 1:
                        act.wait_ge(o_kept, h + 1)
                        act.copy(y_high[:, h // 2, :], yT[:, h // 2, :]).then_inc(y_hi, 1)


def retention(k, name, q_dram, k_dram, v_dram, gate_dram, norm_dram, tab, cos_r, sin_r, outT):
    nc, ps = k.nc, k.ps
    NP_ = RH // 2
    with ExitStack() as es:
        def sb(n, shape, dt=F32):
            return es.enter_context(nc.sbuf_tensor(name + "_" + n, shape, dt))
        sem = lambda n: k.sem(name + "_" + n)
        xT, rT = sb("xT", [P, 2, NP_, T]), sb("rT", [P, 2, T])
        v, kz, y, z = (sb(n, [P, NT, RH * RD]) for n in ("v", "kz", "y", "z"))
        s = sb("s", [P, NT, RH, P])
        state = sb("state", [P, NT - 1, NP_, P])
        kv = sb("kv", [P, NP_, P])
        g = sb("g", [P, RH * RD])
        st = sb("st", [P, 2, NT * RH])
        landed, tab_in = sem("in"), sem("tab_in")
        rot, roped, chain = sem("rot"), sem("roped"), sem("chain")
        with nc.Block() as block:
            @block.sync
            def _(sp):
                sp.dma_start(xT[:, 0, :, :], q_dram).then_inc(landed, 16)
                sp.dma_start(xT[:, 1, :, :], k_dram).then_inc(landed, 16)
                sp.dma_start(v[:, :, :], v_dram).then_inc(tab_in, 16)
                sp.dma_start(z[:, :, :], gate_dram).then_inc(tab_in, 16)
                sp.dma_start(g[:, :], norm_dram.partition_broadcast(P)).then_inc(tab_in, 16)

            @block.tensor
            def _(pe):
                pe.wait_ge(landed, 32)
                for n in range(2 * NP_):
                    pe.matmul(ps[:, n, :], tab["rot_r"][:, :], xT[:, n // NP_, n % NP_, :], start=True, stop=True).then_inc(rot, 1)

            @block.vector
            def _(dve):
                v_ = Chain(dve, chain)
                for n in range(2 * NP_):
                    x = xT[:, n // NP_, n % NP_, :]
                    dve.wait_ge(rot, n + 1)
                    v_(dve.tensor_tensor(rT[:, 0, :], x, cos_r[:, :], ALU.mult))
                    v_(dve.tensor_tensor(rT[:, 1, :], ps[:, n, :], sin_r[:, :], ALU.mult))
                    v_(dve.tensor_tensor(x, rT[:, 0, :], rT[:, 1, :], ALU.add))

            @block.scalar
            def _(act):
                act.wait_ge(tab_in, 48)
                act.activation(z[:, :, :], z[:, :, :], ACT.Silu).then_inc(roped, 1)

        sc_done, s_kept, k_turned, k_kept, kv_done, st_done = (sem("sc_done"), sem("s_kept"), sem("k_turned"), sem("k_kept"),
                                                               sem("kv_done"), sem("st_done"))
        y_in, y_x, y_kept, chain2 = sem("y_in"), sem("y_x"), sem("y_kept"), sem("chain2")
        with nc.Block() as block:
            @block.tensor
            def _(pe):
                for m in range(NT):
                    tok = slice(m * P, (m + 1) * P)
                    if m >= 1:
                        pe.wait_ge(s_kept, 2 * m)
                        pe.wait_ge(k_kept, m)
                    for h in range(RH):
                        r = slice(RD * (h % 2), RD * (h % 2) + RD)
                        last = pe.matmul(ps[:, h % 2, (h // 2) * P:(h // 2 + 1) * P], xT[r, 1, h // 2, tok], xT[r, 0, h // 2, tok],
                                         start=True, stop=True)
                        if h >= RH - 2:
                            last.then_inc(sc_done, 1)
                    for j in range(NP_):
                        last = pe.transpose(ps[:, 2, j * P:(j + 1) * P], xT[:, 1, j, tok], k.ident[:, :])
                    last.then_inc(k_turned, 1)
                    if m < NT - 1:
                        pe.wait_ge(k_kept, m + 1)
                        if m >= 1:
                            pe.wait_ge(st_done, m)
                        for j in range(NP_):
                            last = pe.matmul(ps[:, 3, j * P:(j + 1) * P], kz[:, m, j * P:(j + 1) * P], v[:, m, j * P:(j + 1) * P],
                                             start=True, stop=True)
                        last.then_inc(kv_done, 1)
                for m in range(NT):
                    tok = slice(m * P, (m + 1) * P)
                    pe.wait_ge(s_kept, 2 * (m + 1))
                    if m >= 2:
                        pe.wait_ge(y_kept, m - 1)
                    for h in range(RH):
                        last = pe.matmul(ps[:, 4 + m % 2, h * RD:(h + 1) * RD], s[:, m, h, :], v[:, m, h * RD:(h + 1) * RD],
                                         start=True, stop=True)
                    if m >= 1:
                        pe.wait_ge(st_done, m)
                        for j in range(NP_):
                            last = pe.matmul(ps[:, 6 + m % 2, j * P:(j + 1) * P], xT[:, 0, j, tok], state[:, m - 1, j, :],
                                             start=True, stop=True)
                    last.then_inc(y_in, 1)

            @block.vector
            def _(dve):
                v_ = Chain(dve, chain2)
                pair = tab["pair"][:, :].unsqueeze(1).to_broadcast([P, NP_, P])
                for m in range(NT):
                    for half in range(2):
                        dve.wait_ge(sc_done, 2 * m + half + 1)
                        dve.tensor_tensor(s[:, m, half:RH:2, :], ps[:, half, :].rearrange("p (h q) -> p h q", h=4),
                                          tab["decay"][:, half:RH:2, :], ALU.mult).then_inc(s_kept, 1)
                    dve.wait_ge(k_turned, m + 1)
                    dve.tensor_tensor(kz[:, m, :].rearrange("p (h d) -> p h d", h=RH), ps[:, 2, :].rearrange("p (h d) -> p h d", h=RH),
                                      tab["zeta"][:, :].unsqueeze(2).to_broadcast([P, RH, RD]), ALU.mult).then_inc(k_kept, 1)
                    if m < NT - 1:
                        dve.wait_ge(kv_done, m + 1)
                        ks = ps[:, 3, :].rearrange("p (j c) -> p j c", j=NP_)
                        if m == 0:
                            v_(dve.tensor_tensor(state[:, 0, :, :], ks, pair, ALU.mult))
                        else:
                            v_(dve.tensor_tensor(kv[:, :, :], ks, pair, ALU.mult))
                            v_(dve.tensor_tensor(state[:, m, :, :], state[:, m - 1, :, :],
                                                 tab["chunk_decay"][:, :].unsqueeze(2).to_broadcast([P, NP_, P]), ALU.mult))
                            v_(dve.tensor_tensor(state[:, m, :, :], state[:, m, :, :], kv[:, :, :], ALU.add))
                        dve.sem_inc(st_done, 1)
                heads = lambda a: a.rearrange("p (h d) -> p h d", h=RH)
                for m in range(NT):
                    dve.wait_ge(y_in, m + 1)
                    if m == 0:
                        v_(dve.tensor_copy(y[:, m, :], ps[:, 4, :]))
                    else:
                        v_(dve.tensor_tensor(heads(y[:, m, :]), heads(ps[:, 6 + m % 2, :]),
                                             tab["xi"][:, :].unsqueeze(2).to_broadcast([P, RH, RD]), ALU.mult))
                        v_(dve.tensor_tensor(y[:, m, :], y[:, m, :], ps[:, 4 + m % 2, :], ALU.add))
                    dve.sem_inc(y_kept, 1)
                rows = y[:, :, :].rearrange("p m (h d) -> p (m h) d", h=RH)
                sq = kz[:, :, :].rearrange("p m (h d) -> p (m h) d", h=RH)
                bc = lambda a: a.unsqueeze(2).to_broadcast([P, NT * RH, RD])
                v_(dve.tensor_reduce(st[:, 0, :], rows, AX.X, ALU.add))
                v_(dve.tensor_scalar(st[:, 0, :], st[:, 0, :], 1.0 / RD, None, ALU.mult))
                v_(dve.tensor_tensor(rows, rows, bc(st[:, 0, :]), ALU.subtract))
                v_(dve.tensor_tensor(sq, rows, rows, ALU.mult))
                v_(dve.tensor_reduce(st[:, 1, :], sq, AX.X, ALU.add))
                v_(dve.tensor_scalar(st[:, 1, :], st[:, 1, :], 1.0 / RD, EPS, ALU.mult, ALU.add))
                dve.sem_inc(y_kept, 1)
                dve.wait_ge(y_x, 1)
                v_(dve.reciprocal(st[:, 1, :], st[:, 1, :]))
                v_(dve.tensor_tensor(rows, rows, bc(st[:, 1, :]), ALU.mult))
                v_(dve.tensor_tensor(y[:, :, :], y[:, :, :], g[:, :].unsqueeze(1).to_broadcast([P, NT, RH * RD]), ALU.mult))
                v_(dve.tensor_tensor(y[:, :, :], y[:, :, :], z[:, :, :], ALU.mult))

            @block.scalar
            def _(act):
                act.wait_ge(y_kept, NT + 1)
                act.activation(st[:, 1, :], st[:, 1, :], ACT.Sqrt).then_inc(y_x, 1)
        turn_and_split(k, name, lambda j, m: y[:, m, j * P:(j + 1) * P], *outT)


def mlp_up(k, name, x, view, groups, hi, lo):
    products, relus, squares = k.sem(name + "_products"), k.sem(name + "_relus"), k.sem(name + "_squares")
    hi_done, lo_done = k.sem(name + "_h_hi"), k.sem(name + "_h_lo")
    xh, xl = x
    run = Run(groups, view, lambda j, i: (xh[:, i * UC:(i + 1) * UC, :], xl[:, i * UC:(i + 1) * UC, :]), rolled=False)
    with k.nc.sbuf_tensor(name + "_r", [P, 2, T], F32) as r:
        def act_take(act, run, j, n, half, s):
            for q in range(OUTS + 1):
                c = OUTS * j + q
                if q < OUTS:
                    act.wait_ge(products, c + 1)
                    if c >= 2:
                        act.wait_ge(lo_done, c - 1)
                    act.activation(r[:, q % 2, :], k.ps[:, 4 * s + q, :], ACT.Relu).then_inc(relus, 1)
                if q >= 1:
                    act.wait_ge(squares, c)
                    act.copy(hi[:, c - 1, :], r[:, (q - 1) % 2, :]).then_inc(hi_done, 1)

        def dve_take(dve, run, j, n, half, s):
            for q in range(OUTS + 1):
                c = OUTS * j + q
                if q < OUTS:
                    dve.wait_ge(relus, c + 1)
                    dve.tensor_tensor(r[:, q % 2, :], r[:, q % 2, :], r[:, q % 2, :], ALU.mult).then_inc(squares, 1)
                if q >= 1:
                    dve.wait_ge(hi_done, c)
                    dve.tensor_tensor(lo[:, c - 1, :], r[:, (q - 1) % 2, :], hi[:, c - 1, :].bitcast(F32), ALU.subtract).then_inc(lo_done, 1)

        def freed(pe, n, q):
            pe.wait_ge(relus, n * OUTS + q + 1)

        stream(k, name, [run], 2, {"products": products, "freed": freed, "dve": dve_take, "act": act_take, "act_end": nothing})


def build(nc, a, scratch, out):
    ctx = ExitStack()
    with ctx:
        k = Kernel(nc, ctx)

        def keep(stack, name, shape, dt=F32):
            return stack.enter_context(nc.sbuf_tensor(name, shape, dt))

        k.ps = ctx.enter_context(nc.psum_tensor("ps", [P, 8, T], F32))
        k.resid = keep(ctx, "resid", [P, NC_D, T])
        k.ident, k.ones = keep(ctx, "ident_sb", [P, P]), keep(ctx, "ones_sb", [P, P])
        load_constants(k, [(k.ident[:, :], a["c_ident"]), (k.ones[:, :], a["c_ones"])])
        load_residual(k, "in", a["x"])
        groups = lambda d: d.rearrange("(g q p) t -> g p q t", q=4, p=P)
        tokens = lambda d: d.rearrange("(m p) n -> p m n", p=P)
        tiles = lambda d: d.rearrange("(a p) t -> p a t", p=P)

        def pair(stack, name, n):
            return keep(stack, name + "_high", [P, n, T], F32R), keep(stack, name + "_low", [P, n, T], F32R)

        def chunks(x):
            return lambda j, i: tuple(h[:, i * UC:(i + 1) * UC, :] for h in x)

        def units(w, c0=0):
            return lambda j, i: w[:, i * UC:(i + 1) * UC, bass.ds(c0 + j * GW, GW)]

        C_Z, C_AB = 3 * T, 4 * T
        C_QK = C_AB + 4 * DH
        C_AV = C_QK + 2 * NG * AH * P
        C_G = C_AV + NG * AH * P
        pf1, pt1 = scratch("pf1", [3 * T + (C_AV - C_QK) + 2 * D, T]), scratch("pt1", [T, T + NG * AH * P])
        w_in = a["w_in"].rearrange("(c p) n -> p c n", p=P)
        with ExitStack() as s1:
            odn, oda = pair(s1, "odn", DH), pair(s1, "oda", AH)
            with ExitStack() as s2:
                ab = keep(s2, "ab", [P, NT, 4 * DH])
                with ExitStack() as s3:
                    xn = pair(s3, "xn1", NC_D)
                    with nc.sbuf_tensor("tmp1", [P, NC_D, T], F32) as tmp:
                        normalise(k, "mix", k.resid, a["norm_mix"][0], NC_D, tmp, *xn)
                    fm = lambda g0: lambda j: groups(pf1)[j + g0]
                    tm = lambda c0: lambda j: tokens(pt1)[:, :, bass.ds(c0 + j * GW, GW)]
                    project(k, "in1", [Run(3, units(w_in, 0), chunks(xn), FEATURE, fm(0)), Run(1, units(w_in, C_Z), chunks(xn), TOKEN, tm(0)),
                                       Run(6, units(w_in, C_QK), chunks(xn), FEATURE, fm(3)),
                                       Run(4, units(w_in, C_G), chunks(xn), FEATURE, fm(9)),
                                       Run(3, units(w_in, C_AV), chunks(xn), TOKEN, tm(GW))])
                    narrow(k, "ab", xn, w_in[:, :, C_AB:C_QK], 4 * DH, None, ab)
                    k.recycle()
                tri, strict = keep(s2, "tri_sb", [P, 2, P]), keep(s2, "strict_sb", [P, 2, P])
                same, level = keep(s2, "same_sb", [P, P]), keep(s2, "level_sb", [P, 2, 6, P])
                load_constants(k, [(tri[:, :, :], a["c_tri"]), (strict[:, :, :], a["c_strict"]), (same[:, :], a["c_same"]),
                                   (level[:, :, :, :], a["c_level"])], "delta_tables")
                qT, kT = keep(s2, "dn_qT", [P, DH, T]), keep(s2, "dn_kT", [P, DH, T])
                v_tok, k_tok = keep(s2, "dn_v", [P, NT, DH, P]), keep(s2, "dn_k", [P, NT, DH, P])
                delta_features(k, "dnf", tiles(pf1)[:, 0:3 * DH, :], a["dn_conv"], qT, kT, v_tok, k_tok)
                delta_rule(k, "dn", ab, a["dn_a_log"], a["dn_dt_bias"], qT, kT, k_tok, v_tok, (tri, strict, same, level),
                           tokens(pt1)[:, :, 0:T], a["dn_out_norm"], odn)
                k.recycle()
            n_qk = 3 * DH
            dilated_attention(k, "da", tiles(pf1)[:, n_qk:n_qk + 2 * NG * AH, :], pt1[:, T:T + NG * AH * P], a["rel_bias"],
                              a["c_hot"], a["c_block"], scratch("bias_rows", [NG * AH * P, ELEN]),
                              scratch("da_o", [NG, T, AH * P]), scratch("da_lse", [NG, T, AH]), oda)
            k.recycle()
            n_g = n_qk + 2 * NG * AH
            w_b1 = [a[n].rearrange("(j p) n -> p j n", p=P) for n in ("w_branch_dn", "w_branch_da")]
            with ExitStack() as s2:
                merged = pair(s2, "merged1", NC_D)
                with nc.sbuf_tensor("merged1_sum", [P, NC_D, T], F32) as total:
                    merge_branches(k, "mg1", [odn, oda], lambda b, g: w_b1[b][:, :, g * GW:(g + 1) * GW],
                                   lambda b, g: tiles(pf1)[:, n_g + b * NC_D + OUTS * g:n_g + b * NC_D + OUTS * (g + 1), :],
                                   total, *merged)
                w_out = units(a["w_out"].rearrange("(c p) n -> p c n", p=P))
                add_product(k, "wo1", merged, lambda b, g: w_out(g, b), NC_D)
                k.recycle()

        with ExitStack() as s1:
            idxT, gateT = keep(s1, "idx_T", [P, T], I32), keep(s1, "gate_T", [P, T])
            xs = keep(s1, "x_parts", [3 * GRP, T // GRP, D], BF16)
            qh = scratch("peer_q", [SETS * P, T])
            with nc.sbuf_tensor("xn_p", [P, NC_D, T], F32) as xn_whole:
                with ExitStack() as s2:
                    xn = pair(s2, "xn_p", NC_D)
                    normalise(k, "ffn", k.resid, a["norm_ffn"][0], NC_D, xn_whole, *xn)
                    wq = a["peer_wq"].rearrange("(c p) n -> p c n", p=P)
                    project(k, "pq", [Run(4, units(wq), chunks(xn), FEATURE, lambda j: groups(qh)[j])])
                peer_split(k, "px", xn_whole, xs)
                k.recycle()
            peer_route(k, "pr", tiles(qh), a["peer_sub_keys"], a["c_iota"], idxT, gateT)
            k.recycle()
            peer_experts(k, "pe", xs, a["c_sel"], idxT, gateT, a["peer_u"], a["peer_v"])
            k.recycle()
        norm_out(k, nc, "nf", a["norm_final"][0])

        with ExitStack() as s1:
            tab = {n: keep(s1, n + "_sb", list(a["c_" + n].shape)) for n in
                   ("rot_r", "rot_m", "causal", "later", "before", "decay", "zeta", "xi", "chunk_decay", "pair")}
            full = lambda t: t[tuple([slice(None)] * len(t.shape))]
            load_constants(k, [(full(t), a["c_" + n]) for n, t in tab.items()], "tables2")
            cos_r, sin_r, cos_m, sin_m = (keep(s1, n, [P, T]) for n in ("cos_r", "sin_r", "cos_m", "sin_m"))
            rope_tables(k, "rope", a["positions_2"], a["c_inv_r"], a["c_inv_m"], cos_r, sin_r, cos_m, sin_m)
            pf2, pt2 = scratch("pf2", [(4 + 6) * GW, T]), scratch("pt2", [T, 3 * GW])
            w_in2 = a["w_in_2"].rearrange("l (c p) n -> l p c n", p=P)
            uq = a["mla_w_uq_2"].rearrange("l (c p) n -> l p c n", p=P)
            ukv = a["mla_w_ukv_2"].rearrange("l (c p) (h x) -> l p c h x", p=P, x=P)
            w_br = a["w_branch_2"].rearrange("l b (j p) n -> l b p j n", p=P)
            w_o2 = a["w_out_2"].rearrange("l (c p) n -> l p c n", p=P)
            w_up = a["w_up_2"].rearrange("l (c p) n -> l p c n", p=P)
            w_dn = a["w_down_2"].rearrange("l (c p) n -> l p c n", p=P)
            C_PE = M_QR + M_KVR
            C_SB = C_PE + M_ROPE
            C_RET = C_SB + 3 * GW
            C_G2 = C_RET + 4 * GW
            k.recycle()
            with nc.Fori(0, 2) as l, ExitStack() as s2:
                ya, yb, yc = (pair(s2, n, 4) for n in ("ya", "yb", "yc"))
                with ExitStack() as s3:
                    cT, peT = keep(s3, "c_T", [P, 5, T]), keep(s3, "pe_T", [QD, T])
                    with ExitStack() as s4:
                        xn = pair(s4, "xn2", NC_D)
                        with nc.sbuf_tensor("tmp2", [P, NC_D, T], F32) as tmp:
                            normalise(k, "mix2", k.resid, a["norm_mix_g_2"][l], NC_D, tmp, *xn)
                        w_l = w_in2[l]
                        fm = lambda g0: lambda j: groups(pf2)[j + g0]
                        tm = lambda c0: lambda j: tokens(pt2)[:, :, bass.ds(c0 + j * GW, GW)]
                        project(k, "in2", [Run(2, units(w_l, C_SB), chunks(xn), FEATURE, fm(0)),
                                           Run(6, units(w_l, C_G2), chunks(xn), FEATURE, fm(4)),
                                           Run(2, units(w_l, C_RET), chunks(xn), FEATURE, fm(2)),
                                           Run(2, units(w_l, C_RET + 2 * GW), chunks(xn), TOKEN, tm(GW)),
                                           Run(1, units(w_l, C_SB + 2 * GW), chunks(xn), TOKEN, tm(0))])
                        project_latent(k, "lat", xn, w_l[:, :, 0:C_PE], cT)
                        narrow(k, "kpe", xn, w_l[:, :, C_PE:C_SB], M_ROPE, slice(M_NOPE, QD), peT)
                        k.recycle()
                    with nc.sbuf_tensor("sq3", [P, 3, T], F32) as sq:
                        normalise(k, "nq", cT[:, 0:3, :], a["mla_q_norm_g_2"][l], 3, sq, dst=cT[:, 0:3, :])
                        normalise(k, "nkv", cT[:, 3:5, :], a["mla_kv_norm_g_2"][l], 2, sq, dst=cT[:, 3:5, :])
                    latent_attention(k, "mla", cT, peT, uq[l], ukv[l], tab["rot_m"], cos_m, sin_m, tab["causal"], ya)
                    k.recycle()
                p2 = tiles(pf2)
                stick_breaking(k, "sb", p2[:, 0:4, :], p2[:, 4:8, :], tokens(pt2)[:, :, 0:GW], tab["later"], tab["before"], yb)
                k.recycle()
                retention(k, "ret", p2[:, 8:12, :], p2[:, 12:16, :], tokens(pt2)[:, :, GW:2 * GW], tokens(pt2)[:, :, 2 * GW:3 * GW],
                          a["ret_norm_g_2"][l], tab, cos_r, sin_r, yc)
                k.recycle()
                with ExitStack() as s3:
                    merged = pair(s3, "merged2", NC_D)
                    with nc.sbuf_tensor("merged2_sum", [P, NC_D, T], F32) as total:
                        merge_branches(k, "mg2", [ya, yb, yc], lambda b, g: w_br[l, b][:, :, g * GW:(g + 1) * GW],
                                       lambda b, g: p2[:, 16 + b * NC_D + OUTS * g:16 + b * NC_D + OUTS * (g + 1), :],
                                       total, *merged)
                    w_o = units(w_o2[l])
                    add_product(k, "wo2", merged, lambda b, g: w_o(g, b), NC_D)
                k.recycle()
                s2.close()
                with ExitStack() as s3:
                    xn = pair(s3, "xn3", NC_D)
                    with nc.sbuf_tensor("tmp3", [P, NC_D, T], F32) as tmp:
                        normalise(k, "mlp", k.resid, a["norm_mlp_g_2"][l], NC_D, tmp, *xn)
                    hidden = pair(s3, "hidden", FF // P // 2)
                    for b in range(2):
                        up, down = units(w_up[l], b * FF // 2), units(w_dn[l][:, b * FF // P // 2:(b + 1) * FF // P // 2, :])
                        mlp_up(k, f"up{b}", xn, up, FF // GW // 2, *hidden)
                        add_product(k, f"dn{b}", hidden, lambda i, g: down(g, i), FF // P // 2)
                k.recycle()
        norm_out(k, nc, "ng", a["final_norm_g_2"][0])
        store_final(k, "fin", k.resid, out)


def norm_out(k, nc, name, gain):
    with nc.sbuf_tensor(name + "_sq", [P, NC_D, T], F32) as sq:
        normalise(k, name, k.resid, gain, NC_D, sq, dst=k.resid)


def constants():
    hot, blk = bias_tables()
    tri, strict, same, level = delta_tables()
    c = {"ident": np.eye(P, dtype=np.float32), "ones": np.ones((P, P), np.float32), "hot": hot, "block": blk, "tri": tri,
         "strict": strict, "same": same, "level": level, "iota": np.arange(TOPK, dtype=np.float32),
         "sel": np.tile(np.eye(GRP, dtype=np.float32), (3, 1))}
    c.update(block2_tables())
    return {"c_" + n: v for n, v in c.items()}


def layout(x, norm_mix, w_in, dn_conv, dn_a_log, dn_dt_bias, dn_out_norm, rel_bias, w_branch_dn, w_branch_da, w_out,
           norm_ffn, peer_wq, peer_sub_keys, peer_u, peer_v, norm_final, positions_2, norm_mix_g_2, w_in_2,
           mla_q_norm_g_2, mla_w_uq_2, mla_kv_norm_g_2, mla_w_ukv_2, ret_norm_g_2, w_branch_2, w_out_2, norm_mlp_g_2,
           w_up_2, w_down_2, final_norm_g_2):
    def gains(g):
        g = np.asarray(g)
        return np.ascontiguousarray(g.reshape(-1, g.shape[-1] // P, P).transpose(0, 2, 1))
    f = lambda v: np.ascontiguousarray(np.asarray(v))
    a = {
        "x": f(x)[0], "norm_mix": gains(norm_mix), "w_in": f(w_in)[0],
        "dn_conv": f(f(dn_conv)[0].T.reshape(3 * DH, P, 4).transpose(1, 0, 2)),
        "dn_a_log": f(dn_a_log).reshape(2 * DH), "dn_dt_bias": f(dn_dt_bias).reshape(2 * DH),
        "dn_out_norm": f(dn_out_norm)[0], "rel_bias": f(rel_bias), "w_branch_dn": f(w_branch_dn)[0],
        "w_branch_da": f(w_branch_da)[0], "w_out": f(w_out)[0], "norm_ffn": gains(norm_ffn), "peer_wq": f(peer_wq)[0],
        "peer_sub_keys": f(f(peer_sub_keys).reshape(SETS, NKEY, P).transpose(2, 0, 1)),
        "peer_u": f(peer_u)[0], "peer_v": f(peer_v)[0], "norm_final": gains(norm_final),
        "positions_2": f(positions_2)[0], "norm_mix_g_2": gains(norm_mix_g_2), "w_in_2": f(w_in_2),
        "mla_q_norm_g_2": gains(mla_q_norm_g_2), "mla_w_uq_2": f(mla_w_uq_2), "mla_kv_norm_g_2": gains(mla_kv_norm_g_2),
        "mla_w_ukv_2": f(mla_w_ukv_2), "ret_norm_g_2": f(ret_norm_g_2), "w_branch_2": f(w_branch_2), "w_out_2": f(w_out_2),
        "norm_mlp_g_2": gains(norm_mlp_g_2), "w_up_2": f(w_up_2), "w_down_2": f(w_down_2), "final_norm_g_2": gains(final_norm_g_2),
    }
    return a


def kernel(**inputs):
    import concourse.bacc as _bacc
    from concourse.bass_utils import run_bass_kernel_spmd as _run

    nc = _bacc.Bacc("TRN2", target_bir_lowering=False, num_devices=1)
    arrays, aps = {}, {}
    for name, v in {**layout(**inputs), **constants()}.items():
        arrays[f"in_{name}"] = v
        aps[name] = nc.dram_tensor(f"in_{name}", v.shape, mybir.dt.from_np(v.dtype), kind="ExternalInput").ap()
    out = nc.dram_tensor("out_0_dram", (T, D), F32, kind="ExternalOutput").ap()
    build(nc, aps, lambda name, shape: nc.dram_tensor("dram_" + name, shape, F32).ap(), out)
    r = _run(nc, [arrays], core_ids=[0])
    return r.results[0]["out_0_dram"].reshape(1, T, D)
```

```python
import math
from contextlib import ExitStack, nullcontext

import numpy as np

import concourse.bass as bass
from concourse import mybir

ALU = mybir.AluOpType
ACT = mybir.ActivationFunctionType
AX = mybir.AxisListType
F32 = mybir.dt.float32
F32R = mybir.dt.float32r
BF16 = mybir.dt.bfloat16
I32 = mybir.dt.int32
U32 = mybir.dt.uint32

P = 128
T = 512
D = 1024
NT = T // P
NC_D = D // P
GW = 512
EPS = 1e-6
NEG = -1e30

DH = 4
DHD = 128
CH = 64
NCHUNK = T // CH
GROUPS = ((128, 1), (512, 4), (2048, 16))
NG = len(GROUPS)
AH = 4
BUCKETS = 32
PH = 8
NKEY = 128
TOPK = 16
MH, M_NOPE, M_ROPE, M_V, M_QR, M_KVR = 8, 64, 32, 64, 384, 256
SBH, SBD = 8, 64
RH, RD = 8, 64
FF = 4096


class Chain:

    def __init__(self, eng, sem):
        self.eng, self.sem, self.n = eng, sem, 0

    def __call__(self, ins):
        ins.then_inc(self.sem, 1)
        self.n += 1
        self.eng.wait_ge(self.sem, self.n)


class Kernel:

    def __init__(self, nc, ctx):
        self.nc, self.ctx, self.live = nc, ctx, []

    def sem(self, name):
        s = self.nc.alloc_semaphore(name)
        self.live.append(s)
        return s

    def gather_sem(self, name):
        return self.nc.alloc_semaphore(name)

    def recycle(self):
        numbers = sorted(s.num for s in self.live)
        with self.nc.Block() as block:
            @block.gpsimd
            def _(pool):
                first = last = numbers[0]
                for n in numbers[1:] + [None]:
                    if n is not None and n == last + 1:
                        last = n
                        continue
                    pool.sem_clear(range(first, last + 1))
                    first = last = n
        for s in self.live:
            self.nc.release_semaphore(s)
        self.live = []


def load_constants(k, pairs, name="constants"):
    landed = k.sem(name + "_landed")
    with k.nc.Block() as block:
        @block.sync
        def _(sp):
            for dst, src in pairs:
                sp.dma_start(dst, src).then_inc(landed, 16)
            sp.wait_ge(landed, 16 * len(pairs))


def load_residual(k, name, x):
    nc = k.nc
    landed, turned, copied = k.sem(name + "_x_landed"), k.sem(name + "_turned"), k.sem(name + "_copied")
    with nc.sbuf_tensor(name + "_tok", [P, NT, D], F32) as tok, nc.Block() as block:
        @block.sync
        def _(sp):
            sp.dma_start(tok[:, :, :], x.rearrange("(m p) d -> p m d", p=P)).then_inc(landed, 16)

        @block.tensor
        def _(pe):
            pe.wait_ge(landed, 16)
            for c in range(NC_D):
                for m in range(NT):
                    last = pe.transpose(k.ps[:, c, m * P:(m + 1) * P], tok[:, m, c * P:(c + 1) * P], k.ident[:, :])
                last.then_inc(turned, 1)

        @block.vector
        def _(dve):
            for c in range(NC_D):
                dve.wait_ge(turned, c + 1)
                dve.tensor_copy(k.resid[:, c, :], k.ps[:, c, :]).then_inc(copied, 1)


def normalise(k, name, src, gain, n, tmp, hi=None, lo=None, dst=None, early=()):
    nc = k.nc
    landed, squared, summed = k.sem(name + "_gain_landed"), k.sem(name + "_squared"), k.sem(name + "_summed")
    var, root, inverse = k.sem(name + "_var"), k.sem(name + "_root"), k.sem(name + "_inverse")
    scaled, hi_done, lo_done = k.sem(name + "_scaled"), k.sem(name + "_hi_done"), k.sem(name + "_lo_done")
    early_in = k.sem(name + "_early_in")
    to = tmp if dst is None else dst
    with (nc.sbuf_tensor(name + "_gain", [P, n], F32) as g, nc.sbuf_tensor(name + "_rstd", [P, T], F32) as rstd,
          nc.Block() as block):
        @block.sync
        def _(sp):
            sp.dma_start(g[:, :], gain).then_inc(landed, 16)
            for to_, from_ in early:
                sp.dma_start(to_, from_).then_inc(early_in, 16)
            if early:
                sp.wait_ge(early_in, 16 * len(early))

        @block.scalar
        def _(act):
            for c in range(n):
                act.activation(tmp[:, c, :], src[:, c, :], ACT.Square).then_inc(squared, 1)
            act.wait_ge(var, 1)
            act.activation(rstd[:, :], rstd[:, :], ACT.Sqrt).then_inc(root, 1)
            if dst is None:
                for c in range(n):
                    act.wait_ge(scaled, c + 1)
                    act.copy(hi[:, c, :], tmp[:, c, :]).then_inc(hi_done, 1)

        @block.tensor
        def _(pe):
            for c in range(n):
                pe.wait_ge(squared, c + 1)
                last = pe.matmul(k.ps[:, 0, :], k.ones[:, :], tmp[:, c, :], start=(c == 0), stop=(c == n - 1))
            last.then_inc(summed, 1)

        @block.vector
        def _(dve):
            dve.wait_ge(summed, 1)
            dve.tensor_scalar(rstd[:, :], k.ps[:, 0, :], 1.0 / (n * P), EPS, ALU.mult, ALU.add).then_inc(var, 1)
            dve.wait_ge(root, 1)
            dve.reciprocal(rstd[:, :], rstd[:, :]).then_inc(inverse, 1)
            dve.wait_ge(inverse, 1)
            dve.wait_ge(landed, 16)
            for c in range(n + 1):
                if c < n:
                    dve.scalar_tensor_tensor(to[:, c, :], src[:, c, :], g[:, c:c + 1], rstd[:, :],
                                             ALU.mult, ALU.mult).then_inc(scaled, 1)
                if c >= 1 and dst is None:
                    dve.wait_ge(hi_done, c)
                    dve.tensor_tensor(lo[:, c - 1, :], tmp[:, c - 1, :], hi[:, c - 1, :].bitcast(F32),
                                      ALU.subtract).then_inc(lo_done, 1)


FEATURE, TOKEN = "feature-major", "token-major"
UC, OUTS = 4, 4


def segments(runs):
    out, n = [], 0
    total = sum(r.count for r in runs)
    for run in runs:
        j = 0
        while j < run.count:
            left = min(run.count - j, total - 1 - n)
            loop = run.rolled and n >= 2 and n % 2 == 0 and left >= 4
            take = left // 2 * 2 if loop else 1
            out.append((run, j, take, n, loop))
            j, n = j + take, n + take
    return out


def each_group(eng, runs, body):
    for run, j0, count, n0, loop in segments(runs):
        if loop:
            with eng.Fori(0, count // 2) as i:
                for s in range(2):
                    body(run, i * 2 + (j0 + s), i * 2 + (n0 + s), i + n0 // 2, s)
        else:
            body(run, j0, n0, n0 // 2, n0 % 2)


class Run:

    def __init__(self, count, unit, x, layout=FEATURE, out=None, rolled=True):
        self.count, self.unit, self.x, self.layout, self.out, self.rolled = count, unit, x, layout, out, rolled


def ahead(k, stack, name, unit):
    raw = stack.enter_context(k.nc.sbuf_tensor(name + "_w", [P, 2, UC, GW], F32))
    return raw, [(raw[:, i, :, :], unit(0, i)) for i in range(2)]


def stream(k, name, runs, upg, finish, walk=each_group, total=None, raw=None):
    nc = k.nc
    w_landed = [k.sem(f"{name}_w_landed{s}") for s in range(2)]
    hi_done, lo_done, used = k.sem(name + "_w_hi"), k.sem(name + "_w_lo"), k.sem(name + "_w_used")
    first_landed = [k.sem(f"{name}_first_landed{c}") for c in range(UC)]
    products, freed = finish["products"], finish["freed"]
    total = sum(r.count for r in runs) if total is None else total
    loaded = raw is not None
    with (nullcontext(raw) if loaded else nc.sbuf_tensor(name + "_w", [P, 2, UC, GW], F32) as raw,
          nc.sbuf_tensor(name + "_w_high", [P, 2, UC, GW], F32R) as hi,
          nc.sbuf_tensor(name + "_w_low", [P, 2, UC, GW], F32R) as lo, nc.Block() as block):
        def slot(n, parity, i):
            return i % 2 if upg % 2 == 0 else (parity + i) % 2

        def fill(n, half, parity, i):
            first = 1 if loaded or slot(n, parity, i) == 0 else 0
            if upg % 2 == 0:
                return n * (upg // 2) + (i // 2 + 1 - first)
            return half + (1 - first)

        @block.sync
        def _(sp):
            def load(run, j, n, half, parity):
                for i in range(2 if loaded and isinstance(n, int) and n == 0 else 0, upg):
                    if i >= 2:
                        sp.wait_ge(used, n * (upg - 1) + (i - 1))
                    elif not (isinstance(n, int) and n * upg + i < 2):
                        if upg == 1:
                            sp.wait_ge(products, (n - 1) * OUTS)
                        elif i == 0:
                            sp.wait_ge(used, n * (upg - 1))
                        else:
                            sp.wait_ge(products, n * OUTS)
                    s = slot(n, parity, i)
                    if isinstance(n, int) and n == 0 and i == 0:
                        for c in range(UC):
                            sp.dma_start(raw[:, s, c, :], run.unit(j, i)[:, c, :]).then_inc(first_landed[c], 16)
                    else:
                        sp.dma_start(raw[:, s, :, :], run.unit(j, i)).then_inc(w_landed[s], 16)
                finish.get("load", nothing)(sp, run, j)
            walk(sp, runs, load)

        def split_hi(act, n, half, parity, i):
            s = slot(n, parity, i)
            first = isinstance(n, int) and n == 0 and i == 0
            before = loaded and isinstance(n, int) and n == 0 and i < 2
            if not first and not before:
                act.wait_ge(w_landed[s], fill(n, half, parity, i) * 16)
            for c in range(UC):
                if first and not before:
                    act.wait_ge(first_landed[c], 16)
                act.copy(hi[:, s, c, :], raw[:, s, c, :]).then_inc(hi_done, 1)

        def split_lo(dve, n, half, parity, i):
            s = slot(n, parity, i)
            for c in range(UC):
                dve.wait_ge(hi_done, (n * upg + i) * UC + (c + 1))
                dve.tensor_tensor(lo[:, s, c, :], raw[:, s, c, :], hi[:, s, c, :].bitcast(F32), ALU.subtract).then_inc(lo_done, 1)

        def splitter(eng, split, fin):
            def group(run, j, n, half, parity):
                if isinstance(n, int) and n == 0:
                    split(eng, 0, 0, 0, 0)
                for i in range(1, upg):
                    split(eng, n, half, parity, i)
                if not (isinstance(n, int) and n == total - 1):
                    split(eng, n + 1, half + parity, 1 - parity, 0)
                fin(eng, run, j, n, half, parity)
            walk(eng, runs, group)

        @block.scalar
        def _(act):
            splitter(act, split_hi, finish["act"])
            finish["act_end"](act)

        @block.vector
        def _(dve):
            splitter(dve, split_lo, finish["dve"])

        @block.tensor
        def _(pe):
            def multiply(run, j, n, half, parity):
                for i in range(upg):
                    s = slot(n, parity, i)
                    for q in range(OUTS):
                        if i == 0 and not (isinstance(n, int) and n < 2):
                            if walk is each_group:
                                freed(pe, n - 2, q)
                            else:
                                freed(pe, run, j, q)
                        for c in range(UC):
                            if q == 0:
                                pe.wait_ge(lo_done, (n * upg + i) * UC + (c + 1))
                            xh, xl = run.x(j, i)
                            for p, (w, x) in enumerate(((hi, xh), (lo, xh), (hi, xl))):
                                if run.layout == FEATURE:
                                    a, b = w[:, s, c, q * P:(q + 1) * P], x[:, c, :]
                                else:
                                    a, b = x[:, c, q * P:(q + 1) * P], w[:, s, c, :]
                                last = pe.matmul(k.ps[:, 4 * parity + q, :], a, b, start=(i == 0 and c == 0 and p == 0),
                                                 stop=(i == upg - 1 and c == UC - 1 and p == 2))
                        if i == upg - 1:
                            last.then_inc(products, 1)
                    if i < upg - 1:
                        last.then_inc(used, 1)
            walk(pe, runs, multiply)


def nothing(*_):
    pass


def project(k, name, runs, raw=None):
    nc = k.nc
    stored = [k.sem(f"{name}_stored{s}") for s in range(2)]
    products, drained_v, drained_a = k.sem(name + "_products"), k.sem(name + "_drained_v"), k.sem(name + "_drained_a")
    total = sum(r.count for r in runs)
    with nc.sbuf_tensor(name + "_out", [P, 2, OUTS, T], F32) as out:
        def take(eng, copy, first, drained, n, half, s):
            if not (isinstance(n, int) and n < 2):
                eng.wait_ge(stored[s], half * 16)
            for q in range(first, first + 2):
                eng.wait_ge(products, n * OUTS + (q + 1))
                copy(out[:, s, q, :], k.ps[:, 4 * s + q, :]).then_inc(drained, 1)

        def dve_take(dve, run, j, n, half, s):
            take(dve, dve.tensor_copy, 0, drained_v, n, half, s)

        def act_take(act, run, j, n, half, s):
            take(act, act.copy, 2, drained_a, n, half, s)
            act.wait_ge(drained_v, (n + 1) * 2)
            act.wait_ge(drained_a, (n + 1) * 2)
            act.dma_start(run.out(j), out[:, s, :, :]).then_inc(stored[s], 16)

        def act_end(act):
            for s in range(2):
                act.wait_ge(stored[s], 16 * ((total + 1 - s) // 2))

        def freed(pe, n, q):
            pe.wait_ge(drained_v if q < 2 else drained_a, n * 2 + (q % 2 + 1))

        stream(k, name, runs, 2, {"products": products, "freed": freed, "dve": dve_take, "act": act_take, "act_end": act_end},
               raw=raw)


def narrow(k, name, x, w_dram, rows, dst, turned=False):
    nc = k.nc
    landed, zeroed, hi_done, lo_done = k.sem(name + "_landed"), k.sem(name + "_zeroed"), k.sem(name + "_hi"), k.sem(name + "_lo")
    product, copied, turns = k.sem(name + "_product"), k.sem(name + "_copied"), k.sem(name + "_turns")
    xh, xl = x
    with (nc.sbuf_tensor(name + "_w", [P, NC_D, P], F32) as w, nc.sbuf_tensor(name + "_w_high", [P, NC_D, P], F32R) as hi,
          nc.sbuf_tensor(name + "_w_low", [P, NC_D, P], F32R) as lo, nc.sbuf_tensor(name + "_out", [P, T], F32) as out,
          nc.Block() as block):
        @block.gpsimd
        def _(pool):
            pool.memset(w[:, :, :], 0.0).then_inc(zeroed, 1)

        @block.sync
        def _(sp):
            sp.wait_ge(zeroed, 1)
            sp.dma_start(w[:, :, rows], w_dram).then_inc(landed, 16)

        @block.scalar
        def _(act):
            act.wait_ge(landed, 16)
            act.copy(hi[:, :, :], w[:, :, :]).then_inc(hi_done, 1)

        @block.tensor
        def _(pe):
            pe.wait_ge(lo_done, 1)
            for c in range(NC_D):
                for p, (wp, xp) in enumerate(((hi, xh), (lo, xh), (hi, xl))):
                    last = pe.matmul(k.ps[:, 0, :], wp[:, c, :], xp[:, c, :], start=(c == 0 and p == 0),
                                     stop=(c == NC_D - 1 and p == 2))
            last.then_inc(product, 1)
            if turned:
                pe.wait_ge(copied, 1)
                for m in range(NT):
                    last = pe.transpose(k.ps[:, 1, m * P:(m + 1) * P], out[:, m * P:(m + 1) * P], k.ident[:, :])
                last.then_inc(turns, 1)

        @block.vector
        def _(dve):
            dve.wait_ge(hi_done, 1)
            dve.tensor_tensor(lo[:, :, :], w[:, :, :], hi[:, :, :].bitcast(F32), ALU.subtract).then_inc(lo_done, 1)
            dve.wait_ge(product, 1)
            if turned:
                dve.tensor_copy(out[:, :], k.ps[:, 0, :]).then_inc(copied, 1)
                dve.wait_ge(turns, 1)
                dve.tensor_copy(dst[:, :, :], k.ps[:, 1, :].rearrange("p (m c) -> p m c", m=NT)[:, :, rows]).then_inc(copied, 1)
            else:
                dve.tensor_copy(dst[0:rows.stop, :], k.ps[0:rows.stop, 0, :]).then_inc(copied, 1)


def add_product(k, name, x, view, kchunks):
    products, added = k.sem(name + "_products"), k.sem(name + "_added")
    xh, xl = x
    run = Run(2, lambda j, i: view(i, j), lambda j, i: (xh[:, i * UC:(i + 1) * UC, :], xl[:, i * UC:(i + 1) * UC, :]), rolled=False)

    def dve_take(dve, run, j, n, half, s):
        for q in range(OUTS):
            dve.wait_ge(products, n * OUTS + (q + 1))
            r = k.resid[:, OUTS * j + q, :]
            dve.tensor_tensor(r, r, k.ps[:, 4 * s + q, :], ALU.add).then_inc(added, 1)

    stream(k, name, [run], kchunks // UC, {"products": products, "freed": nothing, "dve": dve_take, "act": nothing, "act_end": nothing})


def merge_branches(k, name, branches, view, gates, merged, hi, lo):
    nc, nb = k.nc, len(branches)
    products, g_in, sig, summed = k.sem(name + "_products"), k.sem(name + "_g_in"), k.sem(name + "_sig"), k.sem(name + "_summed")
    taken, hi_done, lo_done = k.sem(name + "_taken"), k.sem(name + "_hi"), k.sem(name + "_lo")
    order = [(g, b) for g in range(2) for b in range(nb)]
    N = len(order)
    gate_in = [k.sem(f"{name}_gate_in{s}") for s in range(2)]
    with nc.sbuf_tensor(name + "_g", [P, 2, OUTS, T], F32) as g, nc.sbuf_tensor(name + "_t", [P, 2, T], F32) as t:
        runs = [Run(1, lambda j, i, gb=gb: view(gb[1], gb[0]), lambda j, i, gb=gb: branches[gb[1]], out=gb, rolled=False)
                for gb in order]

        def act_take(act, run, j, n, half, s):
            if n == 0:
                act.dma_start(g[:, 0, :, :], gates(*order[0][::-1])).then_inc(gate_in[0], 16)
            if n + 1 < N:
                if n >= 1:
                    act.wait_ge(taken, OUTS * n)
                act.dma_start(g[:, (n + 1) % 2, :, :], gates(*order[n + 1][::-1])).then_inc(gate_in[(n + 1) % 2], 16)
            act.wait_ge(gate_in[n % 2], 16 * (n // 2 + 1))
            act.activation(g[:, n % 2, :, :], g[:, n % 2, :, :], ACT.Sigmoid).then_inc(sig, 1)
            gg, b = run.out
            if b == nb - 1:
                for q in range(OUTS):
                    c = OUTS * gg + q
                    act.wait_ge(summed, N_sum(gg, b, q))
                    act.copy(hi[:, c, :], merged[:, c, :]).then_inc(hi_done, 1)

        def N_sum(gg, b, q):
            return (gg * nb + b) * OUTS + q + 1

        def dve_take(dve, run, j, n, half, s):
            gg, b = run.out
            dve.wait_ge(sig, n + 1)
            for q in range(OUTS):
                c = OUTS * gg + q
                dve.wait_ge(products, n * OUTS + q + 1)
                if b == 0:
                    dve.tensor_tensor(merged[:, c, :], g[:, n % 2, q, :], k.ps[:, 4 * s + q, :], ALU.mult).then_inc(taken, 1)
                    dve.sem_inc(summed, 1)
                    continue
                if n * OUTS + q >= 2:
                    dve.wait_ge(summed, n * OUTS + q - 1)
                dve.tensor_tensor(t[:, q % 2, :], g[:, n % 2, q, :], k.ps[:, 4 * s + q, :], ALU.mult).then_inc(taken, 1)
                dve.wait_ge(taken, n * OUTS + q + 1)
                dve.wait_ge(summed, n * OUTS + q)
                dve.tensor_tensor(merged[:, c, :], merged[:, c, :], t[:, q % 2, :], ALU.add).then_inc(summed, 1)
            if b == nb - 1:
                for q in range(OUTS):
                    c = OUTS * gg + q
                    dve.wait_ge(hi_done, c + 1)
                    dve.tensor_tensor(lo[:, c, :], merged[:, c, :], hi[:, c, :].bitcast(F32), ALU.subtract).then_inc(lo_done, 1)

        def freed(pe, n, q):
            pe.wait_ge(taken, n * OUTS + q + 1)

        stream(k, name, runs, 1, {"products": products, "freed": freed, "dve": dve_take, "act": act_take, "act_end": nothing})


class Half(Run):

    def __init__(self, up, half, slot, unit, x):
        super().__init__(None, unit, x)
        self.up, self.half, self.slot = up, half, slot


def feed_forward(k, name, x, up, down, blocks, act_fn, gates=None, rolled=False, raw=None):
    nc = k.nc
    B = blocks
    hb = 2 * OUTS
    products, raised, scaled = k.sem(name + "_products"), k.sem(name + "_raised"), k.sem(name + "_scaled")
    hi_done, lo_done, added = k.sem(name + "_h_hi"), k.sem(name + "_h_lo"), k.sem(name + "_added")
    gate_in = [k.sem(f"{name}_gate_in{s}") for s in range(2)]
    xh, xl = x
    with ExitStack() as es:
        def sb(n, shape, dt=F32):
            return es.enter_context(nc.sbuf_tensor(name + "_" + n, shape, dt))
        hh, hl = sb("hidden_high", [P, 2, hb, T], F32R), sb("hidden_low", [P, 2, hb, T], F32R)
        r = sb("r", [P, 2, T])
        gt = sb("gates", [P, 2, OUTS, T]) if gates else None
        c4 = lambda i: slice(i * UC, (i + 1) * UC)
        ups = [[Half(True, h, p, lambda b, i, h=h: up(b * 2 + h, i), lambda b, i: (xh[:, c4(i), :], xl[:, c4(i), :]))
                for p in range(2)] for h in range(2)]
        downs = [[Half(False, h, p, lambda b, i, h=h: down(b, h, i),
                       lambda b, i, p=p: (hh[:, p, c4(i), :], hl[:, p, c4(i), :])) for p in range(2)] for h in range(2)]

        def walk(eng, runs, body):
            def block_of(b, p, half):
                body(ups[0][p], b, half * 2, half, 0)
                body(downs[0][1 - p], b - 1, half * 2 + 1, half, 1)
                body(ups[1][p], b, half * 2 + 2, half + 1, 0)
                body(downs[1][1 - p], b - 1, half * 2 + 3, half + 1, 1)
            body(ups[0][0], 0, 0, 0, 0)
            body(ups[1][0], 0, 1, 0, 1)
            block_of(1, 1, 1)
            if rolled:
                with eng.Fori(0, (B - 2) // 2) as it:
                    for o in range(2):
                        block_of(it * 2 + (2 + o), o, it * 4 + (3 + 2 * o))
            else:
                for b in range(2, B):
                    block_of(b, b % 2, 2 * b - 1)
            body(downs[0][(B - 1) % 2], B - 1, 4 * B - 2, 2 * B - 1, 0)
            body(downs[1][(B - 1) % 2], B - 1, 4 * B - 1, 2 * B - 1, 1)

        def load(sp, run, b):
            if run.up and gates:
                if not (isinstance(b, int) and b == 0):
                    sp.wait_ge(scaled, b * hb + OUTS * (run.half - 1))
                sp.dma_start(gt[:, run.half, :, :], gates(b * 2 + run.half)).then_inc(gate_in[run.half], 16)

        def freed(pe, run, b, q):
            last_block = isinstance(b, int) and b == B - 1
            if run.up:
                pe.wait_ge(raised, (b * 2 + (run.half - 1)) * OUTS + (q + 1))
                return
            if q == 0:
                pe.wait_ge(lo_done, b * hb + hb)
            if run.half == 0:
                if not last_block and not (isinstance(b, int) and b == 0):
                    pe.wait_ge(added, (b * 2 - 1) * OUTS + (q + 1))
            elif last_block:
                pe.wait_ge(added, (2 * B - 3) * OUTS + q + 1)
            else:
                pe.wait_ge(added, b * 2 * OUTS + (q + 1))

        def act_take(act, run, b, n, half, s):
            if not run.up:
                return
            for q in range(OUTS + 1):
                c = b * hb + (OUTS * run.half + q)
                if q < OUTS:
                    act.wait_ge(products, n * OUTS + (q + 1))
                    if not (isinstance(c, int) and c < 2):
                        act.wait_ge(lo_done, c - 1)
                    act.activation(r[:, q % 2, :], k.ps[:, 4 * s + q, :], act_fn).then_inc(raised, 1)
                if q >= 1:
                    act.wait_ge(scaled, c)
                    act.copy(hh[:, run.slot, OUTS * run.half + q - 1, :], r[:, (q - 1) % 2, :]).then_inc(hi_done, 1)

        def dve_take(dve, run, b, n, half, s):
            if not run.up:
                for q in range(OUTS):
                    dve.wait_ge(products, n * OUTS + (q + 1))
                    o = k.resid[:, OUTS * run.half + q, :]
                    dve.tensor_tensor(o, o, k.ps[:, 4 * s + q, :], ALU.add).then_inc(added, 1)
                return
            if gates:
                dve.wait_ge(gate_in[run.half], b * 16 + 16)
            for q in range(OUTS + 1):
                c = b * hb + (OUTS * run.half + q)
                if q < OUTS:
                    dve.wait_ge(raised, c + 1)
                    by = gt[:, run.half, q, :] if gates else r[:, q % 2, :]
                    dve.tensor_tensor(r[:, q % 2, :], r[:, q % 2, :], by, ALU.mult).then_inc(scaled, 1)
                if q >= 1:
                    at = OUTS * run.half + q - 1
                    dve.wait_ge(hi_done, c)
                    dve.tensor_tensor(hl[:, run.slot, at, :], r[:, (q - 1) % 2, :], hh[:, run.slot, at, :].bitcast(F32),
                                      ALU.subtract).then_inc(lo_done, 1)

        stream(k, name, None, 2, {"products": products, "freed": freed, "dve": dve_take, "act": act_take,
                                  "act_end": nothing, "load": load}, walk, 4 * B, raw)


def turn_and_split(k, name, tile, hi, lo):
    turned, hi_done, lo_done = k.sem(name + "_y_turned"), k.sem(name + "_y_hi"), k.sem(name + "_y_lo")
    with k.nc.Block() as block:
        @block.tensor
        def _(pe):
            for j in range(4):
                for m in range(NT):
                    last = pe.transpose(k.ps[:, j, m * P:(m + 1) * P], tile(j, m), k.ident[:, :])
                last.then_inc(turned, 1)

        @block.scalar
        def _(act):
            for j in range(4):
                act.wait_ge(turned, j + 1)
                act.copy(hi[:, j, :], k.ps[:, j, :]).then_inc(hi_done, 1)

        @block.vector
        def _(dve):
            for j in range(4):
                dve.wait_ge(hi_done, j + 1)
                dve.tensor_tensor(lo[:, j, :], k.ps[:, j, :], hi[:, j, :].bitcast(F32), ALU.subtract).then_inc(lo_done, 1)


def store_final(k, name, xT, out):
    nc = k.nc
    turned, copied, stored = k.sem(name + "_turned"), k.sem(name + "_copied"), k.sem(name + "_stored")
    with nc.sbuf_tensor(name + "_tok", [P, NT, D], F32) as tok, nc.Block() as block:
        @block.tensor
        def _(pe):
            for m in range(NT):
                for c in range(NC_D):
                    last = pe.transpose(k.ps[:, 2 * m + c // 4, (c % 4) * P:(c % 4 + 1) * P], xT[:, c, m * P:(m + 1) * P],
                                        k.ident[:, :])
                last.then_inc(turned, 1)

        @block.vector
        def _(dve):
            for m in range(NT):
                dve.wait_ge(turned, m + 1)
                dve.tensor_copy(tok[:, m, :].rearrange("p (b c) -> p b c", b=2), k.ps[:, 2 * m:2 * m + 2, :]).then_inc(copied, 1)

        @block.sync
        def _(sp):
            for m in range(NT):
                sp.wait_ge(copied, m + 1)
                sp.dma_start(out[m * P:(m + 1) * P, :], tok[:, m, :]).then_inc(stored, 16)
            sp.wait_ge(stored, 16 * NT)


def delta_features(k, name, pf, conv_w, to_row_dram, from_row_dram, qT, kT, v_tok, k_tok):
    nc = k.nc
    A = 3 * DH
    rows_in = k.sem(name + "_rows_in")
    landed, cw_in, padded = [k.sem(f"{name}_landed{g}") for g in range(3)], k.sem(name + "_cw_in"), k.sem(name + "_padded")
    convolved, activated = k.sem(name + "_convolved"), k.sem(name + "_activated")
    squared, summed, offset, rooted = (k.sem(name + "_squared"), k.sem(name + "_summed"), k.sem(name + "_offset"),
                                       k.sem(name + "_rooted"))
    inverted, spread, scaled = k.sem(name + "_inverted"), k.sem(name + "_spread"), k.sem(name + "_scaled")
    turned, copied, k_copied = k.sem(name + "_turned"), k.sem(name + "_copied"), k.sem(name + "_k_copied")
    with (nc.sbuf_tensor(name + "_raw", [P, A, T + 3], F32) as raw, nc.sbuf_tensor(name + "_cw", [P, A, 4], F32) as cw,
          nc.sbuf_tensor(name + "_acc", [P, A, T], F32) as acc, nc.sbuf_tensor(name + "_norms", [2 * DH, T], F32) as norms,
          nc.sbuf_tensor(name + "_to_row", [P, 2 * DH, 2 * DH], F32) as to_row,
          nc.sbuf_tensor(name + "_from_row", [2 * DH, 2 * DH, P], F32) as from_row, nc.Block() as block):
        heads = acc
        sq = raw[:, 0:2 * DH, 0:T]
        raw_v = raw[:, 2 * DH:A, 0:T]

        @block.sync
        def _(sp):
            sp.dma_start(cw[:, :, :], conv_w).then_inc(cw_in, 16)
            for g in range(3):
                sp.dma_start(raw[:, DH * g:DH * (g + 1), 2:T + 2], pf[:, DH * g:DH * (g + 1), :]).then_inc(landed[g], 16)
            sp.dma_start(to_row[:, :, :], to_row_dram).then_inc(rows_in, 16)
            sp.dma_start(from_row[:, :, :], from_row_dram).then_inc(rows_in, 16)

        @block.gpsimd
        def _(pool):
            pool.memset(raw[:, :, 0:2], 0.0).then_inc(padded, 1)
            pool.memset(raw[:, :, T + 2:T + 3], 0.0).then_inc(padded, 1)

        @block.vector
        def _(dve):
            dve.wait_ge(cw_in, 16)
            dve.wait_ge(padded, 2)
            for g in range(3):
                dve.wait_ge(landed[g], 16)
                for j in range(4):
                    for h in range(DH):
                        a = DH * g + h
                        if j == 0:
                            ins = dve.tensor_scalar(acc[:, a, :], raw[:, a, 0:T], cw[:, a, 0:1], None, ALU.mult)
                        else:
                            dve.wait_ge(convolved, 4 * DH * g + DH * (j - 1) + h + 1)
                            ins = dve.scalar_tensor_tensor(acc[:, a, :], raw[:, a, j:j + T], cw[:, a, j:j + 1],
                                                           acc[:, a, :], ALU.mult, ALU.add)
                        ins.then_inc(convolved, 1)
            dve.wait_ge(summed, 1)
            dve.tensor_scalar(norms[:, :], k.ps[0:2 * DH, 0, :], EPS, None, ALU.add).then_inc(offset, 1)
            dve.wait_ge(rooted, 1)
            dve.reciprocal(norms[:, :], norms[:, :]).then_inc(inverted, 1)
            for a in range(2 * DH):
                dve.wait_ge(spread, a + 1)
                dst = qT[:, a, :] if a < DH else kT[:, a - DH, :]
                dve.scalar_tensor_tensor(dst, heads[:, a, :], DHD ** -0.5 if a < DH else 1.0, k.ps[:, a, :],
                                         ALU.mult, ALU.mult).then_inc(scaled, 1)
            for m in range(NT):
                dve.wait_ge(turned, 2 * m + 1)
                dve.tensor_copy(v_tok[:, m, :, :].rearrange("p h d -> p (h d)"), k.ps[:, 2 * m, :]).then_inc(copied, 1)

        @block.scalar
        def _(act):
            for a in range(A):
                act.wait_ge(convolved, 4 * DH * (a // DH) + 3 * DH + a % DH + 1)
                act.activation(heads[:, a, :], acc[:, a, :], ACT.Silu).then_inc(activated, 1)
            for a in range(2 * DH):
                act.wait_ge(activated, a + 1)
                act.activation(sq[:, a, :], heads[:, a, :], ACT.Square).then_inc(squared, 1)
            act.wait_ge(offset, 1)
            act.activation(norms[:, :], norms[:, :], ACT.Sqrt).then_inc(rooted, 1)
            for m in range(NT):
                act.wait_ge(turned, 2 * m + 2)
                act.copy(k_tok[:, m, :, :].rearrange("p h d -> p (h d)"), k.ps[:, 2 * m + 1, :]).then_inc(k_copied, 1)

        @block.tensor
        def _(pe):
            pe.wait_ge(rows_in, 32)
            for a in range(2 * DH):
                pe.wait_ge(squared, a + 1)
                last = pe.matmul(k.ps[0:2 * DH, 0, :], to_row[:, a, :], sq[:, a, :], start=(a == 0), stop=(a == 2 * DH - 1))
            last.then_inc(summed, 1)
            pe.wait_ge(inverted, 1)
            for a in range(2 * DH):
                pe.matmul(k.ps[:, a, :], from_row[:, a, :], norms[:, :], start=True, stop=True).then_inc(spread, 1)
            pe.wait_ge(activated, A)
            pe.wait_ge(scaled, 2 * DH)
            for m in range(NT):
                for src, b in ((None, 2 * m), (kT, 2 * m + 1)):
                    for h in range(DH):
                        a = heads[:, 2 * DH + h, m * P:(m + 1) * P] if src is None else kT[:, h, m * P:(m + 1) * P]
                        last = pe.transpose(k.ps[:, b, h * P:(h + 1) * P], a, k.ident[:, :])
                    last.then_inc(turned, 1)


def delta_rule(k, name, ab, a_log, dt_bias, qT, kT, k_tok, v_tok, tables, z_dram, out_norm, outT):
    nc, ps = k.nc, k.ps
    R = 2 * DH
    tri, strict, block1, level = tables
    es = ExitStack()
    with es:
        def sb(n, shape, dt=F32):
            return es.enter_context(nc.sbuf_tensor(name + "_" + n, shape, dt))

        alog, dtb = sb("alog", [P, R]), sb("dtb", [P, R])
        g, beta, tmp, gc, gt = (sb(n, [P, NT, R]) for n in ("g", "beta", "tmp", "gc", "gt"))
        be, kd = sb("beta_eg", [P, NT, R]), sb("kd", [P, NT, R])
        dec, qd, lo, X, Y, F, DT = (sb(n, [P, R, NT, P]) for n in ("dec", "qd", "lo", "X", "Y", "F", "DT"))
        state, gl = sb("state", [P, R, P]), sb("gl", [P, R, NCHUNK])

        def flat(b, r):
            return b[:, r, :, :].rearrange("p m c -> p (m c)")

        in_l, step_a, step_v, sums = (k.sem(name + "_gate_in"), k.sem(name + "_gate_act"), k.sem(name + "_gate_dve"),
                                      k.sem(name + "_gate_sums"))
        with nc.Block() as block:
            @block.sync
            def _(sp):
                sp.dma_start(alog[:, :], a_log.partition_broadcast(P)).then_inc(in_l, 16)
                sp.dma_start(dtb[:, :], dt_bias.partition_broadcast(P)).then_inc(in_l, 16)

            @block.vector
            def _(dve):
                v = Chain(dve, step_v)
                dve.wait_ge(in_l, 32)
                v(dve.tensor_tensor(g[:, :, :], ab[:, :, 0:R], dtb[:, :].unsqueeze(1).to_broadcast([P, NT, R]), ALU.add))
                dve.wait_ge(step_a, 5)
                v(dve.scalar_tensor_tensor(g[:, :, :], g[:, :, :], 0.0, tmp[:, :, :], ALU.max, ALU.add))
                v(dve.scalar_tensor_tensor(g[:, :, :], g[:, :, :], -1.0,
                                           alog[:, :].unsqueeze(1).to_broadcast([P, NT, R]), ALU.mult, ALU.mult))
                dve.wait_ge(sums, 1)
                v(dve.tensor_copy(gc[:, :, :], ps[:, 0, 0:NT * R].rearrange("p (m r) -> p m r", r=R)))
                v(dve.tensor_copy(gt[:, :, :], ps[:, 1, 0:NT * R].rearrange("p (m r) -> p m r", r=R)))
                v(dve.tensor_tensor(kd[:, :, :], gt[:, :, :], gc[:, :, :], ALU.subtract))
                dve.wait_ge(step_a, 7)
                v(dve.tensor_tensor(be[:, :, :], be[:, :, :], beta[:, :, :], ALU.mult))

            @block.scalar
            def _(act):
                a = Chain(act, step_a)
                act.wait_ge(in_l, 32)
                a(act.activation(beta[:, :, :], ab[:, :, R:2 * R], ACT.Sigmoid))
                a(act.activation(alog[:, :], alog[:, :], ACT.Exp))
                act.wait_ge(step_v, 1)
                a(act.activation(tmp[:, :, :], g[:, :, :], ACT.Abs))
                a(act.activation(tmp[:, :, :], tmp[:, :, :], ACT.Exp, scale=-1.0))
                a(act.activation(tmp[:, :, :], tmp[:, :, :], ACT.Ln, bias=1.0))
                act.wait_ge(step_v, 6)
                a(act.activation(be[:, :, :], gc[:, :, :], ACT.Exp))
                a(act.activation(kd[:, :, :], kd[:, :, :], ACT.Exp))

            @block.tensor
            def _(pe):
                pe.wait_ge(step_v, 3)
                for m in range(NT):
                    for d in range(2):
                        pe.matmul(ps[:, 0, m * R + d * DH:m * R + (d + 1) * DH], tri[:, d, :], g[:, m, d * DH:(d + 1) * DH],
                                  start=True, stop=True)
                pe.matmul(ps[:, 1, 0:NT * R], block1[:, :], g[:, :, :].rearrange("p m r -> p (m r)"),
                          start=True, stop=True).then_inc(sums, 1)

        STEPS = 5
        pe_done, dve_read, eg_done = k.sem(name + "_pe_done"), k.sem(name + "_bank_read"), k.sem(name + "_eg_done")
        arg_done, dec_done, masked = k.sem(name + "_arg_done"), k.sem(name + "_dec_done"), k.sem(name + "_masked")
        c_ready, f_ready = k.sem(name + "_c_ready"), k.sem(name + "_f_ready")
        chain_v, gbc_done = k.sem(name + "_chain_v"), k.sem(name + "_gbc_done")
        LEVELS = 6
        order = [("rows", 0), ("kk", 0), ("kq", 0), ("turn", 0), ("c0", 0)]
        for l in range(1, LEVELS):
            order += [("f", l)] + ([("e", l)] if l < LEVELS - 1 else []) + [("et", l)]

        def bufs(l):
            return (X, Y) if l % 2 == 1 else (Y, X)

        with nc.Block() as block:
            @block.gpsimd
            def _(pool):
                for r in range(R):
                    pool.tensor_copy(F[:, r, :, :], g[:, :, r:r + 1].to_broadcast([P, NT, P])).then_inc(gbc_done, 1)

            @block.tensor
            def _(pe):
                for s, (what, l) in enumerate(order):
                    for r in range(R):
                        h, d = r % DH, r // DH
                        if s == 0:
                            pe.wait_ge(gbc_done, r + 1)
                        else:
                            if order[s - 1][0] == "f":
                                pe.wait_ge(f_ready, (order[s - 1][1] - 1) * R + r + 1)
                            else:
                                pe.wait_ge(dve_read, (sum(w != "f" for w, _ in order[:s]) - 1) * R + r + 1)
                        if what == "c0":
                            pe.wait_ge(c_ready, r + 1)
                        if what == "f":
                            pe.wait_ge(c_ready, l * R + r + 1)
                        for m in range(NT):
                            o = ps[:, r, m * P:(m + 1) * P]
                            tok = slice(m * P, (m + 1) * P)
                            if what == "rows":
                                last = pe.matmul(o, F[:, r, m, :], tri[:, d, :], start=True, stop=True)
                            elif what == "kk":
                                last = pe.matmul(o, kT[:, h, tok], kT[:, h, tok], start=True, stop=True)
                            elif what == "kq":
                                last = pe.matmul(o, kT[:, h, tok], qT[:, h, tok], start=True, stop=True)
                            elif what == "turn":
                                last = pe.transpose(o, F[:, r, m, :], k.ident[:, :])
                            elif what == "c0":
                                last = pe.matmul(o, Y[:, r, m, :], k.ident[:, :], start=True, stop=True)
                            elif what == "f":
                                last = pe.matmul(o, bufs(l)[1][:, r, m, :], DT[:, r, m, :], start=True, stop=True)
                            elif what == "e":
                                last = pe.matmul(o, F[:, r, m, :], bufs(l)[0][:, r, m, :], start=True, stop=True)
                            else:
                                last = pe.matmul(o, bufs(l)[0][:, r, m, :], F[:, r, m, :], start=True, stop=True)
                        last.then_inc(pe_done, 1)

            @block.scalar
            def _(act):
                for r in range(R):
                    act.wait_ge(arg_done, r + 1)
                    act.activation(flat(X, r), ps[:, r, :], ACT.Exp).then_inc(eg_done, 1)
                    act.activation(flat(dec, r), flat(dec, r), ACT.Exp).then_inc(dec_done, 1)
                for s, (what, l) in enumerate(order):
                    if what == "f":
                        for r in range(R):
                            act.wait_ge(pe_done, s * R + r + 1)
                            act.copy(flat(F, r), ps[:, r, :]).then_inc(f_ready, 1)

            @block.vector
            def _(dve):
                v = Chain(dve, chain_v)

                def bc(t, d, l=None):
                    t = t[:, d, :] if l is None else t[:, d, l, :]
                    return t.unsqueeze(1).to_broadcast([P, NT, P])

                for s, (what, l) in enumerate(order):
                    if s == 1:
                        for r in range(R):
                            dve.wait_ge(eg_done, r + 1)
                            end = CH - 1 if r < DH else 0
                            dve.tensor_copy(gl[:, r, :], flat(X, r).rearrange("p (n c) -> p n c", c=CH)[:, :, end])
                            dve.tensor_tensor(flat(qd, r), qT[:, r % DH, :], flat(X, r), ALU.mult).then_inc(dve_read, 1)
                    for r in range(R if what != "f" else 0):
                        h, d = r % DH, r // DH
                        bank = ps[:, r, :]
                        tiles = bank.rearrange("p (m c) -> p m c", m=NT)
                        dve.wait_ge(pe_done, s * R + r + 1)
                        if what == "rows":
                            for m in range(NT):
                                ins = dve.tensor_scalar(dec[:, r, m, :], tiles[:, m, :], gc[:, m, r:r + 1], 0.0,
                                                        ALU.subtract, ALU.min)
                            ins.then_inc(arg_done, 1)
                        elif what == "kk":
                            dve.wait_ge(dec_done, r + 1)
                            v(dve.tensor_tensor(dec[:, r, :, :], dec[:, r, :, :], bc(tri, d), ALU.mult))
                            v(dve.tensor_tensor(flat(F, r), bank, flat(dec, r), ALU.mult))
                            dve.tensor_tensor(F[:, r, :, :], F[:, r, :, :], bc(strict, d), ALU.mult).then_inc(dve_read, 1)
                        elif what == "kq":
                            dve.tensor_tensor(flat(dec, r), bank, flat(dec, r), ALU.mult).then_inc(dve_read, 1)
                        elif what == "turn":
                            v(dve.tensor_tensor(lo[:, r, :, :], tiles, beta[:, :, r:r + 1].to_broadcast([P, NT, P]), ALU.mult))
                            dve.sem_inc(dve_read, 1)
                            dve.tensor_tensor(Y[:, r, :, :], lo[:, r, :, :], bc(level, d, 0), ALU.mult).then_inc(c_ready, 1)
                        elif what == "c0":
                            ident = k.ident[:, :].unsqueeze(1).to_broadcast([P, NT, P])
                            v(dve.tensor_tensor(DT[:, r, :, :], ident, tiles, ALU.subtract))
                            v(dve.tensor_tensor(X[:, r, :, :], ident, Y[:, r, :, :], ALU.subtract))
                            dve.sem_inc(dve_read, 1)
                            dve.tensor_tensor(Y[:, r, :, :], lo[:, r, :, :], bc(level, d, 1), ALU.mult).then_inc(c_ready, 1)
                        elif what == "e":
                            D_, C_ = bufs(l)
                            dve.tensor_tensor(flat(C_, r), flat(D_, r), bank, ALU.subtract).then_inc(dve_read, 1)
                        else:
                            D_, C_ = bufs(l)
                            v(dve.tensor_tensor(flat(DT, r), flat(DT, r), bank, ALU.subtract))
                            dve.sem_inc(dve_read, 1)
                            if l < LEVELS - 1:
                                dve.tensor_tensor(D_[:, r, :, :], lo[:, r, :, :], bc(level, d, l + 1), ALU.mult).then_inc(c_ready, 1)

        rhs_v, rhs_k, kd_done = k.sem(name + "_rhs_v"), k.sem(name + "_rhs_k"), k.sem(name + "_kd_done")
        u_done, w_done, u_kept, w_kept = (k.sem(name + "_u_done"), k.sem(name + "_w_done"), k.sem(name + "_u_kept"),
                                          k.sem(name + "_w_kept"))
        U, WT, VN, KD, O = lo, F, Y, X, DT
        with nc.Block() as block:
            def by(t, r):
                return t[:, :, r:r + 1].to_broadcast([P, NT, P])

            @block.vector
            def _(dve):
                for r in range(R):
                    dve.tensor_tensor(X[:, r, :, :], v_tok[:, :, r % DH, :], by(beta, r), ALU.mult).then_inc(rhs_v, 1)
                    dve.tensor_tensor(Y[:, r, :, :], k_tok[:, :, r % DH, :], by(be, r), ALU.mult).then_inc(rhs_k, 1)
                for r in range(R):
                    dve.wait_ge(u_done, r + 1)
                    dve.tensor_copy(flat(U, r), ps[:, r, :]).then_inc(u_kept, 1)
                for r in range(R):
                    dve.tensor_tensor(KD[:, r, :, :], k_tok[:, :, r % DH, :], by(kd, r), ALU.mult).then_inc(kd_done, 1)

            @block.scalar
            def _(act):
                for r in range(R):
                    act.wait_ge(w_done, r + 1)
                    act.copy(flat(WT, r), ps[:, r, :]).then_inc(w_kept, 1)

            @block.tensor
            def _(pe):
                for r in range(R):
                    pe.wait_ge(rhs_v, r + 1)
                    for m in range(NT):
                        last = pe.matmul(ps[:, r, m * P:(m + 1) * P], DT[:, r, m, :], X[:, r, m, :], start=True, stop=True)
                    last.then_inc(u_done, 1)
                for r in range(R):
                    pe.wait_ge(rhs_k, r + 1)
                    pe.wait_ge(u_kept, r + 1)
                    for m in range(NT):
                        last = pe.matmul(ps[:, r, m * P:(m + 1) * P], Y[:, r, m, :], DT[:, r, m, :], start=True, stop=True)
                    last.then_inc(w_done, 1)

        ws_done, v_new, upd_done, s_new, o_copied = (k.sem(name + "_ws_done"), k.sem(name + "_v_new"),
                                                     k.sem(name + "_upd_done"), k.sem(name + "_s_new"),
                                                     k.sem(name + "_o_copied"))
        intra_done, o_done = k.sem(name + "_intra_done"), k.sem(name + "_o_done")

        def rows(b, d):
            return ps[:, b + d, :].rearrange("p (h c) -> p h c", h=DH)

        with nc.Block() as block:
            @block.tensor
            def _(pe):
                for c in range(NCHUNK):
                    for d in range(2):
                        n = c if d == 0 else NCHUNK - 1 - c
                        m, half = n // 2, (n % 2) * CH
                        if c > 0:
                            pe.wait_ge(s_new, DH * (2 * (c - 1) + d + 1))
                            if c > 1:
                                pe.wait_ge(o_copied, 2 * (c - 1) + d + 1)
                            for h in range(DH):
                                r = d * DH + h
                                pe.matmul(rows(0, d)[:, h, :], WT[:, r, m, :], state[:, r, :], start=True, stop=True)
                                last = pe.matmul(rows(2, d)[:, h, :], qd[:, r, m, :], state[:, r, :], start=True, stop=True)
                            last.then_inc(ws_done, 1)
                    for d in range(2):
                        n = c if d == 0 else NCHUNK - 1 - c
                        m, half = n // 2, (n % 2) * CH
                        pe.wait_ge(v_new, 2 * c + d + 1)
                        if c < NCHUNK - 1:
                            for h in range(DH):
                                r = d * DH + h
                                last = pe.matmul(rows(4, d)[:, h, :], KD[half:half + CH, r, m, :], VN[half:half + CH, r, m, :],
                                                 start=True, stop=True)
                            last.then_inc(upd_done, 1)
                pe.wait_ge(o_copied, 2 * NCHUNK)
                pe.wait_ge(s_new, 2 * DH * (NCHUNK - 1))
                for r in range(R):
                    for m in range(NT):
                        last = pe.matmul(ps[:, r, m * P:(m + 1) * P], dec[:, r, m, :], VN[:, r, m, :], start=True, stop=True)
                    last.then_inc(intra_done, 1)

            @block.vector
            def _(dve):
                for c in range(NCHUNK):
                    for d in range(2):
                        n = c if d == 0 else NCHUNK - 1 - c
                        m, half = n // 2, slice((n % 2) * CH, (n % 2) * CH + CH)
                        rs = slice(d * DH, (d + 1) * DH)
                        if c == 0:
                            ins = dve.tensor_copy(VN[half, rs, m, :], U[half, rs, m, :])
                        else:
                            dve.wait_ge(ws_done, 2 * (c - 1) + d + 1)
                            ins = dve.tensor_tensor(VN[half, rs, m, :], U[half, rs, m, :], rows(0, d)[half, :, :], ALU.subtract)
                        ins.then_inc(v_new, 1)
                    for d in range(2):
                        n = c if d == 0 else NCHUNK - 1 - c
                        if c == NCHUNK - 1:
                            continue
                        dve.wait_ge(upd_done, 2 * c + d + 1)
                        for h in range(DH):
                            r = d * DH + h
                            if c == 0:
                                ins = dve.tensor_copy(state[:, r, :], rows(4, d)[:, h, :])
                            else:
                                dve.wait_ge(s_new, DH * (2 * (c - 1) + d) + h + 1)
                                ins = dve.scalar_tensor_tensor(state[:, r, :], state[:, r, :], gl[:, r, n:n + 1],
                                                               rows(4, d)[:, h, :], ALU.mult, ALU.add)
                            ins.then_inc(s_new, 1)
                for r in range(R):
                    dve.wait_ge(intra_done, r + 1)
                    dve.wait_ge(o_copied, 2 * NCHUNK)
                    dve.tensor_tensor(flat(O, r), flat(O, r), ps[:, r, :], ALU.add).then_inc(o_done, 1)

            @block.scalar
            def _(act):
                for c in range(NCHUNK):
                    for d in range(2):
                        n = c if d == 0 else NCHUNK - 1 - c
                        m, half = n // 2, slice((n % 2) * CH, (n % 2) * CH + CH)
                        rs = slice(d * DH, (d + 1) * DH)
                        if c == 0:
                            act.mul(O[half, rs, m, :], U[half, rs, m, :], 0.0).then_inc(o_copied, 1)
                        else:
                            act.wait_ge(ws_done, 2 * (c - 1) + d + 1)
                            act.copy(O[half, rs, m, :], rows(2, d)[half, :, :]).then_inc(o_copied, 1)

        z_in, fv, fa = k.sem(name + "_z_in"), k.sem(name + "_fin_dve"), k.sem(name + "_fin_act")
        z, onorm, ss = Y, sb("onorm", [P, DHD]), sb("ss", [P, DH * NT])
        with nc.Block() as block:
            z_tok = z[:, 0:DH, :, :].rearrange("p h m c -> p (h m c)").rearrange("p (m n) -> p m n", m=NT)
            z_hm = z_tok.rearrange("p m (h c) -> p h m c", h=DH)
            o_all = O[:, 0:DH, :, :]
            o_rows = O[:, 0:DH, :, :].rearrange("p h m c -> p (h m) c")
            sq = O[:, DH:R, :, :].rearrange("p h m c -> p (h m) c")

            @block.sync
            def _(sp):
                sp.dma_start(z_tok, z_dram).then_inc(z_in, 16)
                sp.dma_start(onorm[:, :], out_norm.partition_broadcast(P)).then_inc(z_in, 16)

            @block.vector
            def _(dve):
                v = Chain(dve, fv)
                for h in range(DH):
                    v(dve.tensor_tensor(flat(O, h), flat(O, h), flat(O, DH + h), ALU.add))
                v(dve.tensor_tensor(sq, o_rows, o_rows, ALU.mult))
                v(dve.tensor_reduce(ss[:, :], sq, AX.X, ALU.add))
                v(dve.tensor_scalar(ss[:, :], ss[:, :], 1.0 / DHD, EPS, ALU.mult, ALU.add))
                dve.wait_ge(fa, 1)
                v(dve.reciprocal(ss[:, :], ss[:, :]))
                v(dve.tensor_tensor(o_rows, o_rows, ss[:, :].unsqueeze(2).to_broadcast([P, DH * NT, DHD]), ALU.mult))
                dve.wait_ge(z_in, 32)
                v(dve.tensor_tensor(o_rows, o_rows, onorm[:, :].unsqueeze(1).to_broadcast([P, DH * NT, DHD]), ALU.mult))
                dve.wait_ge(fa, 2)
                v(dve.tensor_tensor(o_all, o_all, z_hm, ALU.mult))

            @block.scalar
            def _(act):
                a = Chain(act, fa)
                act.wait_ge(fv, 7)
                a(act.activation(ss[:, :], ss[:, :], ACT.Sqrt))
                act.wait_ge(z_in, 32)
                a(act.activation(z_tok, z_tok, ACT.Silu))
        turn_and_split(k, name, lambda h, m: O[:, h, m, :], *outT)


def delta_tables():
    i = np.arange(P)
    same = (i[:, None] // CH) == (i[None, :] // CH)
    tri = np.stack([same & (i[:, None] <= i[None, :]), same & (i[:, None] >= i[None, :])], 1)
    strict = np.stack([same & (i[:, None] < i[None, :]), same & (i[:, None] > i[None, :])], 1)
    level = np.zeros((P, 2, 6, P), bool)
    for l in range(6):
        pair = (i[:, None] >> (l + 1)) == (i[None, :] >> (l + 1))
        up, low = (i[:, None] >> l) & 1, (i[None, :] >> l) & 1
        level[:, 0, l] = pair & (up == 1) & (low == 0)
        level[:, 1, l] = pair & (up == 0) & (low == 1)
    f = lambda a: np.ascontiguousarray(a.astype(np.float32))
    return f(tri), f(strict), f(same), f(level)


SIDE = 64
ELEN = 384


def t5_bucket(rel):
    half, exact = BUCKETS // 2, BUCKETS // 4
    n = np.abs(rel)
    large = exact + (np.log(np.maximum(n, 1) / exact) / math.log(1024 / exact) * (half - exact)).astype(np.int64)
    large = np.minimum(large, half - 1)
    return np.where(rel > 0, half, 0) + np.where(n < exact, n, large)


def bias_tables():
    hot = np.zeros((BUCKETS + 1, NG, ELEN), np.float32)
    for g, (window, dil) in enumerate(GROUPS):
        rel = np.arange(ELEN) - (191 if g == 0 else 127)
        ok = np.abs(rel) <= window // (2 * dil)
        b = t5_bucket(rel * dil)
        for x in range(ELEN):
            if ok[x]:
                hot[b[x], g, x] = 1.0
            else:
                hot[BUCKETS, g, x] = NEG
    i = np.arange(P) // 32
    block = np.where(i[:, None] == i[None, :], 0.0, NEG).astype(np.float32)
    return hot, block


def dilated_attention(k, name, qk_dram, v_dram, table, hot_dram, block_dram, e_scratch, o_scratch, lse_scratch, outT):
    nc, ps = k.nc, k.ps
    es = ExitStack()
    with es:
        def sb(n, shape, dt=F32):
            return es.enter_context(nc.sbuf_tensor(name + "_" + n, shape, dt))

        bias0, bias12 = sb("bias0", [P, 3, AH, 2 * P]), sb("bias12", [P, 2, AH, P])
        with nc.sbuf_tensor(name + "_hot", [BUCKETS + 1, NG, ELEN], F32) as hot, \
                nc.sbuf_tensor(name + "_tab", [BUCKETS + 1, NG * AH], F32) as tab, \
                nc.sbuf_tensor(name + "_tabw", [BUCKETS + 1, NG * AH, P], F32) as tabw, \
                nc.sbuf_tensor(name + "_e", [P, NG * AH, ELEN], F32) as e, \
                nc.sbuf_tensor(name + "_blk", [P, P], F32) as blk, nc.Block() as block:
            landed, ones_row, wide, made, kept = (k.sem(name + "_b_landed"), k.sem(name + "_b_ones"),
                                                  k.sem(name + "_b_wide"), k.sem(name + "_b_made"), k.sem(name + "_b_kept"))
            out, back, fixed = k.sem(name + "_b_out"), k.sem(name + "_b_back"), k.sem(name + "_b_fixed")

            @block.sync
            def _(sp):
                sp.dma_start(hot[:, :, :], hot_dram).then_inc(landed, 16)
                sp.dma_start(tab[0:BUCKETS, :], table).then_inc(landed, 16)
                sp.dma_start(blk[:, :], block_dram).then_inc(landed, 16)
                sp.wait_ge(kept, NG * AH)
                sp.dma_start(e_scratch.rearrange("(n p) x -> p n x", p=P), e[:, :, :]).then_inc(out, 16)
                sp.wait_ge(out, 16)
                size = P * ELEN
                skew = lambda n0, w: bass.AP(e_scratch.tensor, e_scratch.offset + n0 * size + P - 1,
                                             [[ELEN - 1, P], [size, AH], [1, w]])
                for v in range(3):
                    sp.dma_start(bias0[:, v, :, :], skew(0, 2 * P)).then_inc(back, 16)
                for g in (1, 2):
                    sp.dma_start(bias12[:, g - 1, :, :], skew(g * AH, P)).then_inc(back, 16)

            @block.vector
            def _(dve):
                dve.memset(tab[BUCKETS:BUCKETS + 1, :], 1.0).then_inc(ones_row, 1)
                dve.wait_ge(ones_row, 1)
                dve.wait_ge(landed, 48)
                dve.tensor_copy(tabw[:, :, :], tab[:, :].unsqueeze(2).to_broadcast([BUCKETS + 1, NG * AH, P])).then_inc(wide, 1)
                for n in range(NG * AH):
                    dve.wait_ge(made, n + 1)
                    dve.tensor_copy(e[:, n, :], ps[:, n % 8, 0:ELEN]).then_inc(kept, 1)
                dve.wait_ge(back, 80)
                dve.memset(bias0[:, 0, :, 0:SIDE], NEG).then_inc(fixed, 1)
                dve.memset(bias0[:, 2, :, 2 * P - SIDE:2 * P], NEG).then_inc(fixed, 1)
                dve.tensor_tensor(bias12[:, 1, :, :], bias12[:, 1, :, :],
                                  blk[:, :].unsqueeze(1).to_broadcast([P, AH, P]), ALU.add).then_inc(fixed, 1)

            @block.tensor
            def _(pe):
                pe.wait_ge(wide, 1)
                for n in range(NG * AH):
                    if n >= 8:
                        pe.wait_ge(kept, n - 7)
                    pe.matmul(ps[:, n % 8, 0:ELEN], tabw[:, n, :], hot[:, n // AH, :], start=True, stop=True).then_inc(made, 1)

        o = sb("o", [P, NG, NT, AH * P])
        nmx, l_sum, rl = sb("nmx", [P, NG, NT, AH]), sb("l", [P, NG, NT, AH]), sb("rl", [P, NG, NT, AH])
        es2 = ExitStack()
        with es2:
            def sb2(n, shape, dt=F32):
                return es2.enter_context(nc.sbuf_tensor(name + "_" + n, shape, dt))
            q0, k0 = sb2("q0", [P, AH, T]), sb2("k0", [P, AH, T + 2 * SIDE])
            q12, k12 = sb2("q12", [P, 2, AH, T]), sb2("k12", [P, 2, AH, T])
            raw = sb2("raw", [P, 2, AH, T])
            v0, v12 = sb2("v0", [P, NT + 1, AH * P]), sb2("v12", [P, 2, NT, AH * P])
            logit, pT = sb2("logit", [P, 2, 2 * P]), sb2("pT", [P, 2, 2, P])
            q_in, r_in, v_in, zeroed, moved = (k.sem(name + "_q_in"), [k.sem(f"{name}_r_in{i}") for i in range(2)],
                                               k.sem(name + "_v_in"), k.sem(name + "_zeroed"), k.sem(name + "_moved"))
            s_done, s_read, p_done, t_done, t_read, pv_done, o_done = (
                k.sem(name + "_s_done"), k.sem(name + "_max_done"), k.sem(name + "_p_done"), k.sem(name + "_t_done"),
                k.sem(name + "_t_read"), k.sem(name + "_pv_done"), k.sem(name + "_o_done"))
            chain, stored, lse_a, lse_v = (k.sem(name + "_chain"), k.sem(name + "_stored"), k.sem(name + "_lse_a"),
                                           k.sem(name + "_lse_v"))
            units = [(g, m, h) for g in range(NG) for m in range(NT) for h in range(AH)]
            N = len(units)
            qk = lambda which, g: qk_dram[:, which * NG * AH + g * AH:which * NG * AH + (g + 1) * AH, :]
            vg = lambda g: v_dram[:, g * AH * P:(g + 1) * AH * P]

            with nc.Block() as block:
                @block.sync
                def _(sp):
                    sp.dma_start(q0[:, :, :], qk(0, 0)).then_inc(q_in, 16)
                    sp.dma_start(k0[:, :, SIDE:T + SIDE], qk(1, 0)).then_inc(q_in, 16)
                    sp.dma_start(v0[:, 1:NT, :], vg(0)[SIDE:T - SIDE, :].rearrange("(m p) c -> p m c", p=P)).then_inc(v_in, 16)
                    sp.dma_start(v0[SIDE:P, 0, :], vg(0)[0:SIDE, :]).then_inc(v_in, 16)
                    sp.dma_start(v0[0:SIDE, NT, :], vg(0)[T - SIDE:T, :]).then_inc(v_in, 16)
                    sp.dma_start(v12[:, 0, :, :], vg(1).rearrange("(l m) c -> l m c", m=4)).then_inc(v_in, 16)
                    for r in range(4):
                        sp.dma_start(v12[r * 32:(r + 1) * 32, 1, :, :],
                                     vg(2).rearrange("(l m r) c -> r l m c", m=4, r=4)[r]).then_inc(v_in, 16)
                    for i, (which, g) in enumerate([(0, 1), (1, 1), (0, 2), (1, 2)]):
                        if i >= 2:
                            sp.wait_ge(moved, AH * (i - 1))
                        sp.dma_start(raw[:, i % 2, :, :], qk(which, g)).then_inc(r_in[i % 2], 16)
                    for g in range(NG):
                        sp.wait_ge(o_done, NT * AH * (g + 1))
                        if g == 0:
                            sp.dma_start(o_scratch[0].rearrange("(m p) c -> p m c", p=P), o[:, 0, :, :]).then_inc(stored, 16)
                        elif g == 1:
                            sp.dma_start(o_scratch[1].rearrange("(l m) c -> l m c", m=4), o[:, 1, :, :]).then_inc(stored, 16)
                        else:
                            for r in range(4):
                                sp.dma_start(o_scratch[2].rearrange("(l m r) c -> r l m c", m=4, r=4)[r],
                                             o[r * 32:(r + 1) * 32, 2, :, :]).then_inc(stored, 16)
                    sp.wait_ge(lse_v, 1)
                    sp.dma_start(lse_scratch[0].rearrange("(m p) c -> p m c", p=P), l_sum[:, 0, :, :]).then_inc(stored, 16)
                    sp.dma_start(lse_scratch[1].rearrange("(l m) c -> l m c", m=4), l_sum[:, 1, :, :]).then_inc(stored, 16)
                    for r in range(4):
                        sp.dma_start(lse_scratch[2].rearrange("(l m r) c -> r l m c", m=4, r=4)[r],
                                     l_sum[r * 32:(r + 1) * 32, 2, :, :]).then_inc(stored, 16)
                    sp.wait_ge(stored, 16 * 12)

                @block.gpsimd
                def _(pool):
                    pool.memset(k0[:, :, 0:SIDE], 0.0).then_inc(zeroed, 1)
                    pool.memset(k0[:, :, T + SIDE:T + 2 * SIDE], 0.0).then_inc(zeroed, 1)
                    pool.wait_ge(zeroed, 2)
                    pool.memset(v0[0:SIDE, 0, :], 0.0).then_inc(zeroed, 1)
                    pool.wait_ge(zeroed, 3)
                    pool.memset(v0[SIDE:P, NT, :], 0.0).then_inc(zeroed, 1)
                    pool.wait_ge(zeroed, 4)
                    for i in range(4):
                        pool.wait_ge(r_in[i % 2], 16 * (i // 2 + 1))
                        dst = (q12, k12)[i % 2]
                        n = (4, 16)[i // 2]
                        for h in range(AH):
                            pool.tensor_copy(dst[:, i // 2, h, :].rearrange("p (n l) -> p n l", n=n),
                                             raw[:, i % 2, h, :].rearrange("p (l n) -> p n l", n=n)).then_inc(moved, 1)

                def keys(g):
                    return 2 * P if g == 0 else P

                @block.tensor
                def _(pe):
                    for i in range(N + 2):
                        if i < N:
                            g, m, h = units[i]
                            if i == 0:
                                pe.wait_ge(q_in, 32)
                                pe.wait_ge(zeroed, 4)
                            elif (m, h) == (0, 0):
                                pe.wait_ge(moved, 2 * AH * g)
                            if i >= 2:
                                pe.wait_ge(s_read, i - 1)
                            if g == 0:
                                pe.matmul(ps[:, i % 2, 0:2 * P], q0[:, h, m * P:(m + 1) * P], k0[:, h, m * P:(m + 2) * P],
                                          start=True, stop=True).then_inc(s_done, 1)
                            else:
                                tok = slice(m * P, (m + 1) * P)
                                pe.matmul(ps[:, i % 2, 0:P], q12[:, g - 1, h, tok], k12[:, g - 1, h, tok],
                                          start=True, stop=True).then_inc(s_done, 1)
                        if 1 <= i <= N:
                            j = i - 1
                            g = units[j][0]
                            pe.wait_ge(p_done, j + 1)
                            if j >= 2:
                                pe.wait_ge(t_read, j - 1)
                            for c in range(keys(g) // P):
                                last = pe.transpose(ps[:, 2 + j % 2, c * P:(c + 1) * P], logit[:, j % 2, c * P:(c + 1) * P],
                                                    k.ident[:, :])
                            last.then_inc(t_done, 1)
                        if i >= 2:
                            j = i - 2
                            g, m, h = units[j]
                            pe.wait_ge(t_read, j + 1)
                            if j == 0:
                                pe.wait_ge(v_in, 16 * 8)
                            if j >= 2:
                                pe.wait_ge(o_done, j - 1)
                            nk = keys(g) // P
                            for c in range(nk):
                                v = v0[:, m + c, h * P:(h + 1) * P] if g == 0 else v12[:, g - 1, m, h * P:(h + 1) * P]
                                last = pe.matmul(ps[:, 4 + j % 2, 0:P], pT[:, j % 2, c, :], v, start=(c == 0), stop=(c == nk - 1))
                            last.then_inc(pv_done, 1)

                @block.vector
                def _(dve):
                    n_chain = 0
                    for i in range(N + 2):
                        if i < N:
                            g, m, h = units[i]
                            w = keys(g)
                            dve.wait_ge(s_done, i + 1)
                            if i >= 2:
                                dve.wait_ge(t_done, i - 1)
                            b = bias0[:, (0 if m == 0 else 2 if m == NT - 1 else 1), h, :] if g == 0 else bias12[:, g - 1, h, :]
                            dve.scalar_tensor_tensor(logit[:, i % 2, 0:w], ps[:, i % 2, 0:w], P ** -0.5, b,
                                                     ALU.mult, ALU.add).then_inc(chain, 1)
                            n_chain += 1
                            dve.wait_ge(chain, n_chain)
                            dve.tensor_reduce(nmx[:, g, m, h:h + 1], logit[:, i % 2, 0:w], AX.X, ALU.max,
                                              negate=True).then_inc(s_read, 1)
                        if i >= 2:
                            j = i - 2
                            g, m, h = units[j]
                            dve.wait_ge(pv_done, j + 1)
                            dve.reciprocal(rl[:, g, m, h:h + 1], l_sum[:, g, m, h:h + 1]).then_inc(chain, 1)
                            n_chain += 1
                            dve.wait_ge(chain, n_chain)
                            dve.tensor_scalar(o[:, g, m, h * P:(h + 1) * P], ps[:, 4 + j % 2, 0:P], rl[:, g, m, h:h + 1],
                                              None, ALU.mult).then_inc(o_done, 1)
                    dve.wait_ge(lse_a, 1)
                    dve.tensor_tensor(l_sum[:, :, :, :], l_sum[:, :, :, :], nmx[:, :, :, :], ALU.subtract).then_inc(lse_v, 1)

                @block.scalar
                def _(act):
                    for i in range(N + 1):
                        if i < N:
                            g, m, h = units[i]
                            w = keys(g)
                            act.wait_ge(s_read, i + 1)
                            act.activation(logit[:, i % 2, 0:w], logit[:, i % 2, 0:w], ACT.Exp, bias=nmx[:, g, m, h:h + 1],
                                           accum_out=l_sum[:, g, m, h:h + 1]).then_inc(p_done, 1)
                        if i >= 1:
                            j = i - 1
                            w = keys(units[j][0])
                            act.wait_ge(t_done, j + 1)
                            if j >= 2:
                                act.wait_ge(pv_done, j - 1)
                            act.copy(pT[:, j % 2, :, :].rearrange("p c q -> p (c q)")[:, 0:w],
                                     ps[:, 2 + j % 2, 0:w]).then_inc(t_read, 1)
                    act.wait_ge(o_done, N)
                    act.activation(l_sum[:, :, :, :], l_sum[:, :, :, :], ACT.Ln).then_inc(lse_a, 1)

        lse, mx, tot = sb("lse", [P, NG, NT, AH]), sb("mx", [P, NT, AH]), sb("tot", [P, NT, AH])
        acc = sb("acc", [P, NT, AH * P])
        back, mv, ma = k.sem(name + "_m_in"), k.sem(name + "_m_dve"), k.sem(name + "_m_act")
        with nc.Block() as block:
            @block.sync
            def _(sp):
                for g in range(NG):
                    sp.dma_start(lse[:, g, :, :], lse_scratch[g].rearrange("(m p) c -> p m c", p=P)).then_inc(back, 16)
                    sp.dma_start(o[:, g, :, :], o_scratch[g].rearrange("(m p) c -> p m c", p=P)).then_inc(back, 16)

            @block.vector
            def _(dve):
                v = Chain(dve, mv)
                dve.wait_ge(back, 16 * 2 * NG)
                v(dve.tensor_tensor(mx[:, :, :], lse[:, 0, :, :], lse[:, 1, :, :], ALU.max))
                v(dve.tensor_tensor(mx[:, :, :], mx[:, :, :], lse[:, 2, :, :], ALU.max))
                v(dve.tensor_tensor(lse[:, :, :, :], lse[:, :, :, :], mx[:, :, :].unsqueeze(1).to_broadcast([P, NG, NT, AH]),
                                    ALU.subtract))
                dve.wait_ge(ma, 1)
                v(dve.tensor_tensor(tot[:, :, :], lse[:, 0, :, :], lse[:, 1, :, :], ALU.add))
                v(dve.tensor_tensor(tot[:, :, :], tot[:, :, :], lse[:, 2, :, :], ALU.add))
                v(dve.reciprocal(tot[:, :, :], tot[:, :, :]))
                v(dve.tensor_tensor(lse[:, :, :, :], lse[:, :, :, :], tot[:, :, :].unsqueeze(1).to_broadcast([P, NG, NT, AH]),
                                    ALU.mult))
                for g in range(NG):
                    og = o[:, g, :, :].rearrange("p m (h c) -> p (m h) c", h=AH)
                    w = lse[:, g, :, :].rearrange("p m h -> p (m h)").unsqueeze(2).to_broadcast([P, NT * AH, P])
                    v(dve.tensor_tensor(og, og, w, ALU.mult))
                v(dve.tensor_tensor(acc[:, :, :], o[:, 0, :, :], o[:, 1, :, :], ALU.add))
                v(dve.tensor_tensor(acc[:, :, :], acc[:, :, :], o[:, 2, :, :], ALU.add))

            @block.scalar
            def _(act):
                act.wait_ge(mv, 3)
                act.activation(lse[:, :, :, :], lse[:, :, :, :], ACT.Exp).then_inc(ma, 1)
        turn_and_split(k, name, lambda h, m: acc[:, m, h * P:(h + 1) * P], *outT)


SETS = 2 * PH
MHN = NT * PH


def peer_route(k, name, qh_dram, sub_keysT, iota_dram, keyT, gateT):
    nc, ps = k.nc, k.ps
    with ExitStack() as es:
        def sb(n, shape, dt=F32):
            return es.enter_context(nc.sbuf_tensor(name + "_" + n, shape, dt))
        sv, si = sb("sv", [P, NT, SETS, TOPK]), sb("si", [P, NT, SETS, TOPK], U32)
        sif = sb("sif", [P, NT, SETS, TOPK])
        landed, k_in = [k.sem(f"{name}_landed{m}") for m in range(NT)], k.sem(name + "_k_in")
        scored, val_a, idx_a, cut, val_b, top = (k.sem(name + "_scored"),
                                                         k.sem(name + "_val_a"), k.sem(name + "_idx_a"), k.sem(name + "_cut"),
                                                         k.sem(name + "_val_b"), k.sem(name + "_top"))
        with (nc.sbuf_tensor(name + "_qT", [P, SETS, T], F32) as qT, nc.sbuf_tensor(name + "_kT", [P, SETS, NKEY], F32) as kT,
              nc.sbuf_tensor(name + "_rest", [P, SETS, NKEY], F32) as rest, nc.Block() as block):
            @block.sync
            def _(sp):
                sp.dma_start(kT[:, :, :], sub_keysT).then_inc(k_in, 16)
                for m in range(NT):
                    sp.dma_start(qT[:, :, m * P:(m + 1) * P], qh_dram[:, :, m * P:(m + 1) * P]).then_inc(landed[m], 16)

            @block.tensor
            def _(pe):
                pe.wait_ge(k_in, 16)
                for m in range(NT):
                    pe.wait_ge(landed[m], 16)
                    if m >= 2:
                        pe.wait_ge(top, SETS * (m - 1))
                    for s in range(SETS):
                        last = pe.matmul(ps[:, 4 * (m % 2) + s // 4, (s % 4) * NKEY:(s % 4 + 1) * NKEY],
                                         qT[:, s, m * P:(m + 1) * P], kT[:, s, :], start=True, stop=True)
                    last.then_inc(scored, 1)

            @block.vector
            def _(dve):
                for m in range(NT):
                    dve.wait_ge(scored, m + 1)
                    S = lambda s: ps[:, 4 * (m % 2) + s // 4, (s % 4) * NKEY:(s % 4 + 1) * NKEY]
                    n = m * SETS
                    for s in range(SETS):
                        dve.max(sv[:, m, s, 0:8], S(s)).then_inc(val_a, 1)
                    for s in range(SETS):
                        dve.wait_ge(val_a, n + s + 1)
                        dve.max_index(si[:, m, s, 0:8], sv[:, m, s, 0:8], S(s)).then_inc(idx_a, 1)
                        if m:
                            dve.wait_ge(top, n)
                        dve.match_replace(rest[:, s, :], sv[:, m, s, 0:8], S(s), -3e38).then_inc(cut, 1)
                    for s in range(SETS):
                        dve.wait_ge(cut, n + s + 1)
                        dve.max(sv[:, m, s, 8:16], rest[:, s, :]).then_inc(val_b, 1)
                    for s in range(SETS):
                        dve.wait_ge(val_b, n + s + 1)
                        dve.max_index(si[:, m, s, 8:16], sv[:, m, s, 8:16], rest[:, s, :]).then_inc(top, 1)

        cand, rest2 = sb("cand", [P, MHN, TOPK, TOPK]), sb("rest2", [P, MHN, TOPK * TOPK])
        cv, ci = sb("cv", [P, MHN, TOPK]), sb("ci", [P, MHN, TOPK], U32)
        digit, digf, i12 = sb("digit", [P, MHN, TOPK], U32), sb("digf", [P, MHN, TOPK]), sb("i12", [P, 2, MHN, TOPK])
        ej, iota = sb("exp", [P, MHN, TOPK]), sb("iota", [P, TOPK])
        tot = sb("tot", [P, MHN])
        cd, i_in, a_done, turned = k.sem(name + "_c_dve"), k.sem(name + "_iota_in"), k.sem(name + "_exp_act"), k.sem(name + "_turned")
        val_a, cut, val_b, top, fin = (k.sem(name + "_c_val_a"), k.sem(name + "_c_cut"), k.sem(name + "_c_val_b"),
                                       k.sem(name + "_c_top"), k.sem(name + "_c_fin"))
        ready, hot, picked = k.sem(name + "_ready"), k.sem(name + "_hot"), k.sem(name + "_picked")
        with nc.Block() as block:
            four = [P, MHN, TOPK, TOPK]
            pair = lambda t, c: t[:, :, :, :].rearrange("p m (h c) i -> p (m h) c i", c=2)[:, :, c, :]

            @block.sync
            def _(sp):
                sp.dma_start(iota[:, :], iota_dram.partition_broadcast(P)).then_inc(i_in, 16)

            @block.vector
            def _(dve):
                v = Chain(dve, cd)
                v(dve.tensor_copy(sif[:, :, :, :], si[:, :, :, :]))
                v(dve.tensor_tensor(cand[:, :, :, :], pair(sv, 0).unsqueeze(3).to_broadcast(four),
                                    pair(sv, 1).unsqueeze(2).to_broadcast(four), ALU.add))
                C = lambda n: cand[:, n, :, :].rearrange("p a b -> p (a b)")
                for n in range(MHN):
                    dve.max(cv[:, n, 0:8], C(n)).then_inc(val_a, 1)
                for n in range(MHN):
                    dve.wait_ge(val_a, n + 1)
                    dve.max_index(ci[:, n, 0:8], cv[:, n, 0:8], C(n)).then_inc(top, 1)
                    dve.match_replace(rest2[:, n, :], cv[:, n, 0:8], C(n), -3e38).then_inc(cut, 1)
                for n in range(MHN):
                    dve.wait_ge(cut, n + 1)
                    dve.max(cv[:, n, 8:16], rest2[:, n, :]).then_inc(val_b, 1)
                for n in range(MHN):
                    dve.wait_ge(val_b, n + 1)
                    dve.max_index(ci[:, n, 8:16], cv[:, n, 8:16], rest2[:, n, :]).then_inc(top, 1)
                v(dve.tensor_tensor(ej[:, :, :], cv[:, :, :], cv[:, :, 0:1].to_broadcast([P, MHN, TOPK]), ALU.subtract))
                dve.wait_ge(top, 2 * MHN)
                dve.wait_ge(i_in, 16)
                hots = (rest2[:, :, :].rearrange("p n (a b) -> p n a b", a=TOPK), cand[:, :, :, :])
                for c in range(2):
                    if c == 0:
                        v(dve.tensor_scalar(digit[:, :, :], ci[:, :, :], 4, None, ALU.logical_shift_right))
                    else:
                        v(dve.tensor_scalar(digit[:, :, :], ci[:, :, :], 15, None, ALU.bitwise_and))
                    v(dve.tensor_copy(digf[:, :, :], digit[:, :, :]))
                    v(dve.tensor_tensor(hots[c], digf[:, :, :].unsqueeze(3).to_broadcast(four),
                                        iota[:, :].unsqueeze(1).unsqueeze(1).to_broadcast(four), ALU.is_equal))
                    if c == 0:
                        dve.sem_inc(hot, 1)
                v(dve.tensor_tensor(hots[1], hots[1], pair(sif, 1).unsqueeze(2).to_broadcast(four), ALU.mult))
                v(dve.tensor_reduce(i12[:, 1, :, :], hots[1], AX.X, ALU.add))
                dve.wait_ge(picked, 1)
                v(dve.tensor_reduce(i12[:, 0, :, :], hots[0], AX.X, ALU.add))
                dve.wait_ge(a_done, 1)
                v(dve.tensor_reduce(tot[:, :], ej[:, :, :], AX.X, ALU.add))
                v(dve.reciprocal(tot[:, :], tot[:, :]))
                v(dve.tensor_tensor(ej[:, :, :], ej[:, :, :], tot[:, :].unsqueeze(2).to_broadcast([P, MHN, TOPK]), ALU.mult))
                dve.sem_inc(ready, 1)
                dve.wait_ge(turned, 1)
                dve.tensor_copy(keyT[:, :, :], ps[:, 0:2, :]).then_inc(fin, 1)
                dve.tensor_copy(gateT[:, :], ps[:, 2, :]).then_inc(fin, 1)

            @block.gpsimd
            def _(pool):
                pool.wait_ge(hot, 1)
                h = rest2[:, :, :].rearrange("p n (a b) -> p n a b", a=TOPK)
                pool.tensor_tensor(h, h, pair(sif, 0).unsqueeze(2).to_broadcast(four), ALU.mult).then_inc(picked, 1)

            @block.scalar
            def _(act):
                act.wait_ge(cd, 3)
                act.activation(ej[:, :, :], ej[:, :, :], ACT.Exp).then_inc(a_done, 1)

            @block.tensor
            def _(pe):
                pe.wait_ge(ready, 1)
                for b, src in ((0, i12[:, 0, :, :]), (1, i12[:, 1, :, :]), (2, ej[:, :, :])):
                    for m in range(NT):
                        last = pe.transpose(ps[:, b, m * P:(m + 1) * P],
                                            src[:, m * PH:(m + 1) * PH, :].rearrange("p h j -> p (h j)"), k.ident[:, :])
                last.then_inc(turned, 1)


UNIT = 8
TB = P


def peer_gates(k, name, keyT, gateT, iota_dram, table):
    nc, ps = k.nc, k.ps
    sem = lambda n: k.sem(name + "_" + n)
    i_in, one_j, one_i, gated, used, kept = sem("iota_in"), sem("one_j"), sem("one_i"), sem("gated"), sem("used"), sem("kept")
    stored = [sem(f"stored{s}") for s in range(2)]
    with ExitStack() as es:
        def sb(n, shape, dt=F32):
            return es.enter_context(nc.sbuf_tensor(name + "_" + n, shape, dt))
        iota, J, I_ = sb("iota", [P, P]), sb("J", [P, 2, UNIT, P]), sb("I", [P, 2, UNIT, P])
        out = sb("out", [P, 2, NKEY, TB])
        tiles = table.rearrange("(i j) t -> j i t", j=P)

        with nc.Block() as block:
            @block.sync
            def _(sp):
                sp.dma_start(iota[:, :], iota_dram.partition_broadcast(P)).then_inc(i_in, 16)
                for b in range(T // TB):
                    sp.wait_ge(kept, (b + 1) * TB // UNIT + 2)
                    sp.dma_start(tiles[:, :, b * TB:(b + 1) * TB], out[:, b % 2, :, :]).then_inc(stored[b % 2], 16)
                for s in range(2):
                    sp.wait_ge(stored[s], 16 * (T // TB // 2))

            @block.vector
            def _(dve):
                dve.wait_ge(i_in, 16)
                full = [P, UNIT, P]
                with dve.Fori(0, T // UNIT // 2) as it:
                    for s in range(2):
                        dve.wait_ge(used, it * 2 + (s + 1))
                        for c, to, done in ((0, I_, one_i), (1, J, one_j)):
                            keys = keyT[:, c, bass.ds(it * (2 * UNIT) + s * UNIT, UNIT)]
                            dve.tensor_tensor(to[:, s, :, :], iota[:, :].unsqueeze(1).to_broadcast(full),
                                              keys.unsqueeze(2).to_broadcast(full), ALU.is_equal).then_inc(done, 1)

            @block.gpsimd
            def _(pool):
                with pool.Fori(0, T // UNIT // 2) as it:
                    for s in range(2):
                        pool.wait_ge(one_i, it * 2 + (s + 1))
                        for h in range(2):
                            g = gateT[:, bass.ds(it * (2 * UNIT) + (s * UNIT + h * UNIT // 2), UNIT // 2)]
                            o = I_[:, s, h * UNIT // 2:(h + 1) * UNIT // 2, :]
                            pool.tensor_tensor(o, o, g.unsqueeze(2).to_broadcast([P, UNIT // 2, P]), ALU.mult).then_inc(gated, 1)

            @block.tensor
            def _(pe):
                pe.sem_inc(used, 2)
                with pe.Fori(0, T // UNIT // 2) as it:
                    for s in range(2):
                        pe.wait_ge(one_j, it * 2 + (s + 1))
                        pe.wait_ge(kept, it * 2 + (s + 1))
                        for j in range(UNIT):
                            if j % (UNIT // 2) == 0:
                                pe.wait_ge(gated, it * 4 + (s * 2 + j // (UNIT // 2) + 1))
                            last = pe.matmul(ps[:, 2 * s + j // 4, (j % 4) * P:(j % 4 + 1) * P], J[:, s, j, :], I_[:, s, j, :],
                                             start=True, stop=True)
                        last.then_inc(used, 1)

            @block.scalar
            def _(act):
                act.sem_inc(kept, 2)
                for b in range(T // TB):
                    if b >= 2:
                        act.wait_ge(stored[b % 2], 16 * (b // 2))
                    with act.Fori(0, TB // UNIT // 2) as it:
                        for s in range(2):
                            act.wait_ge(used, it * 2 + (b * TB // UNIT + s + 3))
                            act.copy(out[:, b % 2, :, bass.ds(it * (2 * UNIT) + s * UNIT, UNIT)],
                                     ps[:, 2 * s:2 * s + 2, :].rearrange("p b c -> p (b c)").rearrange("p (t i) -> p i t", t=UNIT)
                                     ).then_inc(kept, 1)


QD = M_NOPE + M_ROPE


def block2_tables():
    f = lambda a: np.ascontiguousarray(np.asarray(a).astype(np.float32))
    i = np.arange(P)
    t = {}
    def rot(n, half, base):
        r = np.zeros((n, n), np.float32)
        for m in base:
            for j in range(half):
                r[m + half + j, m + j] = -1.0
                r[m + j, m + half + j] = 1.0
        return r
    t["rot_r"] = rot(P, RD // 2, (0, RD))
    t["rot_m"] = rot(QD, M_ROPE // 2, (M_NOPE,))
    inv = lambda dim: np.float32(10000.0) ** (-np.arange(0, dim, 2, dtype=np.float32) / np.float32(dim))
    t["inv_r"] = f(inv(RD)[i % (RD // 2)])[:, None]
    t["inv_m"] = f(inv(M_ROPE)[i % (M_ROPE // 2)])[:, None]
    cm = np.zeros((P, T), np.float32)
    cm[:, T - P:] = np.where(i[None, :] <= i[:, None], 0.0, NEG)
    t["causal"] = cm
    t["later"] = f(i[:, None] > i[None, :])
    t["before"] = f(i[:, None] < i[None, :])
    lg = np.log1p(-np.exp2(-5.0 - np.arange(RH, dtype=np.float64)))
    d = i[None, :] - i[:, None]
    t["decay"] = f(np.where(d[:, None, :] >= 0, np.exp(np.maximum(d, 0)[:, None, :] * lg[None, :, None]), 0.0) * RD ** -0.5)
    t["zeta"] = f(np.exp((P - 1 - i)[:, None] * lg[None, :]) * RD ** -0.5)
    t["xi"] = f(np.exp((i + 1.0)[:, None] * lg[None, :]))
    pairs = 2 * np.arange(RH // 2)[None, :] + (i // RD)[:, None]
    t["chunk_decay"] = f(np.exp(P * lg)[pairs])
    t["pair"] = f((i[:, None] // RD) == (i[None, :] // RD))
    return t


def rope_tables(k, name, pos, inv_r, inv_m, cos_r, sin_r, cos_m, sin_m):
    nc = k.nc
    c1 = 6.28125
    c2 = float(np.float32(np.floor((2 * math.pi - c1) * 2 ** 21) / 2 ** 21))
    c3 = float(2 * math.pi - c1 - c2)
    TOP = 3.1415925
    landed, step, done = k.sem(name + "_landed"), k.sem(name + "_step"), k.sem(name + "_done")
    with (nc.sbuf_tensor(name + "_pi", [P, T], I32) as pi, nc.sbuf_tensor(name + "_pf", [P, T], F32) as pf,
          nc.sbuf_tensor(name + "_n", [P, 2, T], F32) as n, nc.sbuf_tensor(name + "_r", [P, 2, T], F32) as r,
          nc.sbuf_tensor(name + "_c", [P, 2, T], F32) as c, nc.sbuf_tensor(name + "_iv", [P, 2], F32) as iv,
          nc.Block() as block):
        @block.sync
        def _(sp):
            sp.dma_start(pi[:, :], pos.partition_broadcast(P)).then_inc(landed, 16)
            sp.dma_start(iv[:, 0:1], inv_r).then_inc(landed, 16)
            sp.dma_start(iv[:, 1:2], inv_m).then_inc(landed, 16)

        @block.vector
        def _(dve):
            v = Chain(dve, step)
            dve.wait_ge(landed, 48)
            v(dve.tensor_copy(pf[:, :], pi[:, :]))
            for j in range(2):
                v(dve.tensor_scalar(r[:, j, :], pf[:, :], iv[:, j:j + 1], None, ALU.mult))
            v(dve.tensor_scalar(n[:, :, :], r[:, :, :], 1.0 / (2 * math.pi), 12582912.0, ALU.mult, ALU.add))
            v(dve.tensor_scalar(n[:, :, :], n[:, :, :], -12582912.0, None, ALU.add))
            for part in (c1, c2, c3):
                v(dve.scalar_tensor_tensor(r[:, :, :], n[:, :, :], -part, r[:, :, :], ALU.mult, ALU.add))
            v(dve.tensor_scalar(n[:, :, :], r[:, :, :], math.pi / 2, -2 * math.pi, ALU.is_gt, ALU.mult))
            v(dve.scalar_tensor_tensor(c[:, :, :], r[:, :, :], math.pi / 2, n[:, :, :], ALU.add, ALU.add))
            v(dve.tensor_scalar(c[:, :, :], c[:, :, :], TOP, -TOP, ALU.min, ALU.max))
            v(dve.tensor_scalar(r[:, :, :], r[:, :, :], TOP, -TOP, ALU.min, ALU.max))

        @block.scalar
        def _(act):
            act.wait_ge(step, 12)
            for dst, src in ((cos_r, c[:, 0, :]), (sin_r, r[:, 0, :]), (cos_m, c[:, 1, :]), (sin_m, r[:, 1, :])):
                act.activation(dst[:, :], src, ACT.Sin).then_inc(done, 1)


def project_latent(k, name, x, w_dram, cT):
    nc, ps = k.nc, k.ps
    n = (M_QR + M_KVR) // P
    landed = [k.sem(f"{name}_landed{s}") for s in range(2)]
    hi_done, lo_done, product, copied = (k.sem(name + "_hi"), k.sem(name + "_lo"), k.sem(name + "_product"),
                                         k.sem(name + "_copied"))
    xh, xl = x
    with (nc.sbuf_tensor(name + "_w", [P, 2, NC_D, P], F32) as w, nc.sbuf_tensor(name + "_w_high", [P, 2, NC_D, P], F32R) as hi,
          nc.sbuf_tensor(name + "_w_low", [P, 2, NC_D, P], F32R) as lo, nc.Block() as block):
        @block.sync
        def _(sp):
            for a in range(n):
                if a >= 2:
                    sp.wait_ge(product, a - 1)
                sp.dma_start(w[:, a % 2, :, :], w_dram[:, :, a * P:(a + 1) * P]).then_inc(landed[a % 2], 16)

        @block.scalar
        def _(act):
            for a in range(n):
                act.wait_ge(landed[a % 2], 16 * (a // 2 + 1))
                act.copy(hi[:, a % 2, :, :], w[:, a % 2, :, :]).then_inc(hi_done, 1)

        @block.tensor
        def _(pe):
            for a in range(n):
                pe.wait_ge(lo_done, a + 1)
                for c in range(NC_D):
                    for p, (wp, xp) in enumerate(((hi, xh), (lo, xh), (hi, xl))):
                        last = pe.matmul(ps[:, a, :], wp[:, a % 2, c, :], xp[:, c, :], start=(c == 0 and p == 0),
                                         stop=(c == NC_D - 1 and p == 2))
                last.then_inc(product, 1)

        @block.vector
        def _(dve):
            for a in range(n + 1):
                if a < n:
                    dve.wait_ge(hi_done, a + 1)
                    dve.tensor_tensor(lo[:, a % 2, :, :], w[:, a % 2, :, :], hi[:, a % 2, :, :].bitcast(F32),
                                      ALU.subtract).then_inc(lo_done, 1)
                if a >= 1:
                    dve.wait_ge(product, a)
                    dve.tensor_copy(cT[:, a - 1, :], ps[:, a - 1, :]).then_inc(copied, 1)


def load_early(k, name, block, pairs):
    landed = k.sem(name + "_early")

    @block.sync
    def _(sp):
        for dst, src in pairs:
            sp.dma_start(dst, src).then_inc(landed, 16)
        sp.wait_ge(landed, 16 * len(pairs))


def latent_attention(k, name, cT, peT, uq_dram, ukv_dram, rot_m, cos_m, sin_m, causal, outT, early):
    nc, ps = k.nc, k.ps
    rope = slice(M_NOPE, QD)
    with ExitStack() as es:
        def sb(n, shape, dt=F32):
            return es.enter_context(nc.sbuf_tensor(name + "_" + n, shape, dt))
        sem = lambda n: k.sem(name + "_" + n)
        qT, kT, v = sb("qT", [QD, MH, T]), sb("kT", [QD, MH, T]), sb("v", [P, NT, MH * M_V])
        y = sb("y", [P, NT, MH * M_V])
        with (nc.sbuf_tensor(name + "_wq", [P, 3, MH * QD], F32) as wq, nc.sbuf_tensor(name + "_wkv", [P, 2, MH, P], F32) as wkv,
              nc.sbuf_tensor(name + "_t", [QD, 2, T], F32) as t, nc.Block() as block):
            landed, prod, rot, kept, free, chain = sem("w_in"), sem("prod"), sem("rot"), sem("kept"), sem("bank_free"), sem("chain_r")

            @block.sync
            def _(sp):
                sp.dma_start(wq[:, :, :], uq_dram).then_inc(landed, 16)
                sp.dma_start(wkv[:, :, :, :], ukv_dram).then_inc(landed, 16)

            @block.tensor
            def _(pe):
                pe.wait_ge(landed, 32)
                for s in range(21):
                    if s >= 2:
                        pe.wait_ge(free, s - 1)
                    o = ps[:, s % 2, :]
                    if s < 8:
                        for c in range(3):
                            last = pe.matmul(o[0:QD, :], wq[:, c, s * QD:(s + 1) * QD], cT[:, c, :], start=(c == 0), stop=(c == 2))
                        last.then_inc(prod, 1)
                    elif 8 < s < 17:
                        for c in range(2):
                            last = pe.matmul(o[0:M_NOPE, :], wkv[:, c, s - 9, 0:M_NOPE], cT[:, 3 + c, :], start=(c == 0), stop=(c == 1))
                        last.then_inc(prod, 1)
                    elif s >= 17:
                        m = s - 17
                        for c in range(2):
                            last = pe.matmul(o, cT[:, 3 + c, m * P:(m + 1) * P], wkv[:, c, :, M_NOPE:P], start=(c == 0), stop=(c == 1))
                        last.then_inc(prod, 1)
                    if s <= 8:
                        if s < 8:
                            pe.wait_ge(kept, s + 1)
                        src = qT[:, s, :] if s < 8 else peT[:, :]
                        pe.matmul(ps[0:QD, 2 + s % 2, :], rot_m[:, :], src, start=True, stop=True).then_inc(rot, 1)

            @block.vector
            def _(dve):
                v_ = Chain(dve, chain)
                for s in range(21):
                    if s < 8:
                        dve.wait_ge(prod, s + 1)
                        dve.tensor_copy(qT[:, s, :], ps[0:QD, s % 2, :]).then_inc(kept, 1)
                        dve.wait_ge(kept, s + 1)
                    if s <= 8:
                        src = qT[rope, s, :] if s < 8 else peT[rope, :]
                        dve.wait_ge(rot, s + 1)
                        v_(dve.tensor_tensor(t[rope, 0, :], src, cos_m[rope, :], ALU.mult))
                        v_(dve.tensor_tensor(t[rope, 1, :], ps[rope, 2 + s % 2, :], sin_m[rope, :], ALU.mult))
                        v_(dve.tensor_tensor(src, t[rope, 0, :], t[rope, 1, :], ALU.add))
                        dve.sem_inc(free, 1)
                    elif s < 17:
                        h = s - 9
                        dve.wait_ge(prod, s)
                        dve.tensor_copy(kT[0:M_NOPE, h, :], ps[0:M_NOPE, s % 2, :]).then_inc(chain, 1)
                        dve.tensor_copy(kT[rope, h, :], peT[rope, :]).then_inc(free, 1)
                        v_.n += 1
                        dve.wait_ge(chain, v_.n)
                    else:
                        dve.wait_ge(prod, s)
                        dve.tensor_copy(v[:, s - 17, :], ps[:, s % 2, :]).then_inc(free, 1)

        units = [(m, h) for m in range(NT) for h in range(MH)]
        N = len(units)
        with (nc.sbuf_tensor(name + "_logit", [P, 2, T], F32) as logit, nc.sbuf_tensor(name + "_pT", [P, 2, T], F32) as pT,
              nc.sbuf_tensor(name + "_st", [P, 3, N], F32) as st, nc.Block() as block):
            nmx, ls, rl = st[:, 0, :], st[:, 1, :], st[:, 2, :]
            s_done, s_read, p_done, t_done, t_read, pv_done, o_done, chain = (
                sem("s_done"), sem("max_done"), sem("p_done"), sem("t_done"), sem("t_read"), sem("pv_done"), sem("o_done"),
                sem("chain"))
            load_early(k, name, block, early)

            @block.tensor
            def _(pe):
                for i in range(N + 2):
                    if i < N:
                        m, h = units[i]
                        if i >= 2:
                            pe.wait_ge(s_read, i - 1)
                        pe.matmul(ps[:, i % 2, 0:(m + 1) * P], qT[:, h, m * P:(m + 1) * P], kT[:, h, 0:(m + 1) * P],
                                  start=True, stop=True).then_inc(s_done, 1)
                    if 1 <= i <= N:
                        j = i - 1
                        m, h = units[j]
                        pe.wait_ge(p_done, j + 1)
                        if j >= 2:
                            pe.wait_ge(t_read, j - 1)
                        for c in range(m + 1):
                            last = pe.transpose(ps[:, 2 + j % 2, c * P:(c + 1) * P], logit[:, j % 2, c * P:(c + 1) * P], k.ident[:, :])
                        last.then_inc(t_done, 1)
                    if i >= 2:
                        j = i - 2
                        m, h = units[j]
                        pe.wait_ge(t_read, j + 1)
                        if j >= 2:
                            pe.wait_ge(o_done, j - 1)
                        for c in range(m + 1):
                            last = pe.matmul(ps[:, 4 + j % 2, 0:M_V], pT[:, j % 2, c * P:(c + 1) * P],
                                             v[:, c, h * M_V:(h + 1) * M_V], start=(c == 0), stop=(c == m))
                        last.then_inc(pv_done, 1)

            @block.vector
            def _(dve):
                v_ = Chain(dve, chain)
                for i in range(N + 2):
                    if i < N:
                        m, h = units[i]
                        w = (m + 1) * P
                        dve.wait_ge(s_done, i + 1)
                        if i >= 2:
                            dve.wait_ge(t_done, i - 1)
                        v_(dve.scalar_tensor_tensor(logit[:, i % 2, 0:w], ps[:, i % 2, 0:w], QD ** -0.5, causal[:, T - w:T],
                                                    ALU.mult, ALU.add))
                        dve.tensor_reduce(nmx[:, i:i + 1], logit[:, i % 2, 0:w], AX.X, ALU.max, negate=True).then_inc(s_read, 1)
                    if i >= 2:
                        j = i - 2
                        m, h = units[j]
                        dve.wait_ge(pv_done, j + 1)
                        v_(dve.reciprocal(rl[:, j:j + 1], ls[:, j:j + 1]))
                        dve.tensor_scalar(y[:, m, h * M_V:(h + 1) * M_V], ps[:, 4 + j % 2, 0:M_V], rl[:, j:j + 1], None,
                                          ALU.mult).then_inc(o_done, 1)

            @block.scalar
            def _(act):
                for i in range(N + 1):
                    if i < N:
                        w = (units[i][0] + 1) * P
                        act.wait_ge(s_read, i + 1)
                        act.activation(logit[:, i % 2, 0:w], logit[:, i % 2, 0:w], ACT.Exp, bias=nmx[:, i:i + 1],
                                       accum_out=ls[:, i:i + 1]).then_inc(p_done, 1)
                    if i >= 1:
                        j = i - 1
                        w = (units[j][0] + 1) * P
                        act.wait_ge(t_done, j + 1)
                        if j >= 2:
                            act.wait_ge(pv_done, j - 1)
                        act.copy(pT[:, j % 2, 0:w], ps[:, 2 + j % 2, 0:w]).then_inc(t_read, 1)
        turn_and_split(k, name, lambda j, m: y[:, m, j * P:(j + 1) * P], *outT)


def stick_breaking(k, name, qT, kT, v, later, before, outT):
    nc, ps = k.nc, k.ps
    W = sum(T - P * j for j in range(NT))
    off = [sum(T - P * j for j in range(kt)) for kt in range(NT)]
    bank = [(0, 0), (1, 0), (2, 0), (2, 2 * P)]
    wid = [T - P * kt for kt in range(NT)]
    with ExitStack() as es:
        def sb(n, shape, dt=F32):
            return es.enter_context(nc.sbuf_tensor(name + "_" + n, shape, dt))
        sem = lambda n: k.sem(name + "_" + n)
        z, t, sp_ = (sb(n, [P, 2, W]) for n in ("z", "t", "sp"))
        lb = sb("lb", [P, 3, W])
        z_done, z_kept, ln_done, sp_done, lb_done, sums, args, expd, masked, o_done, o_kept, chain = (
            sem("z_done"), sem("z_kept"), sem("ln_done"), sem("sp_done"), sem("lb_done"), sem("sums"), sem("args"),
            sem("exp"), sem("masked"), sem("o_done"), sem("o_kept"), sem("chain"))
        act_chain, y_hi, y_lo = sem("act_chain"), sem("y_hi"), sem("y_lo")
        yT = sb("yT", [P, 4, T])
        y_high, y_low = outT

        def two(b0):
            return ((ps[:, b0:b0 + 2, :].rearrange("p b c -> p (b c)")[:, 0:off[2]], slice(0, off[2])),
                    (ps[:, b0 + 2, 0:wid[2] + wid[3]], slice(off[2], W)))

        with nc.Block() as block:
            @block.tensor
            def _(pe):
                def scores(h):
                    if h >= 1:
                        pe.wait_ge(z_kept, h)
                    r = slice(SBD * (h % 2), SBD * (h % 2) + SBD)
                    for kt in range(NT):
                        b, c = bank[kt]
                        last = pe.matmul(ps[:, b, c:c + wid[kt]], kT[r, h // 2, kt * P:(kt + 1) * P], qT[r, h // 2, kt * P:T],
                                         start=True, stop=True)
                    last.then_inc(z_done, 1)

                def suffix_sums(h):
                    pe.wait_ge(sp_done, h + 1)
                    if h >= 1:
                        pe.wait_ge(args, h)
                    for kt in range(NT):
                        b, c = bank[kt]
                        for j in range(kt, NT):
                            o = ps[:, 3 + b, c + (j - kt) * P:c + wid[kt]]
                            last = pe.matmul(o, later[:, :] if j == kt else k.ones[:, :], sp_[:, h % 2, off[j]:off[j] + wid[j]],
                                             start=(j == kt), stop=(j == NT - 1))
                    last.then_inc(sums, 1)

                def outputs(h):
                    pe.wait_ge(masked, h + 1)
                    if h >= 1:
                        pe.wait_ge(o_kept, h)
                    for kt in range(NT):
                        last = pe.matmul(ps[0:SBD, 6, kt * P:T], v[:, kt, h * SBD:(h + 1) * SBD], lb[:, h % 3, off[kt]:off[kt] + wid[kt]],
                                         start=(kt == 0), stop=(kt == NT - 1))
                    last.then_inc(o_done, 1)

                scores(0)
                scores(1)
                for h in range(SBH):
                    suffix_sums(h)
                    if h >= 1:
                        outputs(h - 1)
                    if h + 2 < SBH:
                        scores(h + 2)
                outputs(SBH - 1)

            @block.vector
            def _(dve):
                v_ = Chain(dve, chain)

                def mask(buf):
                    for kt in range(NT):
                        d = buf[:, off[kt]:off[kt] + P]
                        ins = dve.tensor_tensor(d, d, before[:, :], ALU.mult)
                        ins.then_inc(chain, 1)
                        v_.n += 1
                    dve.wait_ge(chain, v_.n)

                def keep(h):
                    dve.wait_ge(z_done, h + 1)
                    for src, cols in two(0):
                        v_(dve.tensor_scalar(z[:, h % 2, cols], src, SBD ** -0.5, None, ALU.mult))
                    dve.sem_inc(z_kept, 1)

                def softplus(h):
                    zz, tt, ss = (b[:, h % 2, :] for b in (z, t, sp_))
                    dve.wait_ge(ln_done, h + 1)
                    v_(dve.scalar_tensor_tensor(ss, zz, 0.0, tt, ALU.max, ALU.add))
                    if h >= 3:
                        dve.wait_ge(o_done, h - 2)
                    v_(dve.tensor_tensor(lb[:, h % 3, :], zz, ss, ALU.subtract))
                    mask(ss)
                    dve.sem_inc(sp_done, 1)

                def weights(h):
                    dve.wait_ge(expd, h + 1)
                    mask(lb[:, h % 3, :])
                    dve.sem_inc(masked, 1)

                keep(0)
                keep(1)
                softplus(0)
                for h in range(SBH):
                    if h >= 1:
                        weights(h - 1)
                    if h + 1 < SBH:
                        softplus(h + 1)
                    dve.wait_ge(sums, h + 1)
                    for src, cols in two(3):
                        v_(dve.tensor_tensor(lb[:, h % 3, cols], lb[:, h % 3, cols], src, ALU.subtract))
                    dve.sem_inc(args, 1)
                    if h + 2 < SBH:
                        keep(h + 2)
                weights(SBH - 1)
                for j in range(4):
                    dve.wait_ge(y_hi, j + 1)
                    dve.tensor_tensor(y_low[:, j, :], yT[:, j, :], y_high[:, j, :].bitcast(F32), ALU.subtract).then_inc(y_lo, 1)

            @block.scalar
            def _(act):
                a = Chain(act, act_chain)

                def log1p(h):
                    zz, tt = z[:, h % 2, :], t[:, h % 2, :]
                    act.wait_ge(z_kept, h + 1)
                    a(act.activation(tt, zz, ACT.Abs))
                    a(act.activation(tt, tt, ACT.Exp, scale=-1.0))
                    act.activation(tt, tt, ACT.Ln, bias=1.0).then_inc(ln_done, 1)

                log1p(0)
                for h in range(SBH + 1):
                    if h >= 1:
                        act.wait_ge(args, h)
                        act.activation(lb[:, (h - 1) % 3, :], lb[:, (h - 1) % 3, :], ACT.Exp).then_inc(expd, 1)
                    if h + 1 < SBH:
                        log1p(h + 1)
                    if h >= 1:
                        g = h - 1
                        act.wait_ge(o_done, g + 1)
                        act.copy(yT[SBD * (g % 2):SBD * (g % 2) + SBD, g // 2, :], ps[0:SBD, 6, :]).then_inc(o_kept, 1)
                        if g % 2 == 1:
                            act.wait_ge(o_kept, g + 1)
                            act.copy(y_high[:, g // 2, :], yT[:, g // 2, :]).then_inc(y_hi, 1)


def retention(k, name, xT, v_dram, gate_dram, norm_dram, tab, cos_r, sin_r, outT):
    nc, ps = k.nc, k.ps
    NP_ = RH // 2
    with ExitStack() as es:
        def sb(n, shape, dt=F32):
            return es.enter_context(nc.sbuf_tensor(name + "_" + n, shape, dt))
        sem = lambda n: k.sem(name + "_" + n)
        rT = sb("rT", [P, 2, T])
        v, kz, y, z = (sb(n, [P, NT, RH * RD]) for n in ("v", "kz", "y", "z"))
        s = sb("s", [P, NT, RH, P])
        state = sb("state", [P, NT - 1, NP_, P])
        kv = sb("kv", [P, NP_, P])
        g = sb("g", [P, RH * RD])
        st = sb("st", [P, 2, NT * RH])
        tab_in = sem("tab_in")
        rot, roped, chain = sem("rot"), sem("roped"), sem("chain")
        with nc.Block() as block:
            @block.sync
            def _(sp):
                sp.dma_start(v[:, :, :], v_dram).then_inc(tab_in, 16)
                sp.dma_start(z[:, :, :], gate_dram).then_inc(tab_in, 16)
                sp.dma_start(g[:, :], norm_dram.partition_broadcast(P)).then_inc(tab_in, 16)

            @block.tensor
            def _(pe):
                for n in range(2 * NP_):
                    pe.matmul(ps[:, n, :], tab["rot_r"][:, :], xT[:, n // NP_, n % NP_, :], start=True, stop=True).then_inc(rot, 1)

            @block.vector
            def _(dve):
                v_ = Chain(dve, chain)
                for n in range(2 * NP_):
                    x = xT[:, n // NP_, n % NP_, :]
                    dve.wait_ge(rot, n + 1)
                    v_(dve.tensor_tensor(rT[:, 0, :], x, cos_r[:, :], ALU.mult))
                    v_(dve.tensor_tensor(rT[:, 1, :], ps[:, n, :], sin_r[:, :], ALU.mult))
                    v_(dve.tensor_tensor(x, rT[:, 0, :], rT[:, 1, :], ALU.add))

            @block.scalar
            def _(act):
                act.wait_ge(tab_in, 48)
                act.activation(z[:, :, :], z[:, :, :], ACT.Silu).then_inc(roped, 1)

        sc_done, s_kept, k_turned, k_kept, kv_done, st_done = (sem("sc_done"), sem("s_kept"), sem("k_turned"), sem("k_kept"),
                                                               sem("kv_done"), sem("st_done"))
        y_in, y_x, y_kept, chain2 = sem("y_in"), sem("y_x"), sem("y_kept"), sem("chain2")
        with nc.Block() as block:
            @block.tensor
            def _(pe):
                for m in range(NT):
                    tok = slice(m * P, (m + 1) * P)
                    if m >= 1:
                        pe.wait_ge(s_kept, 2 * m)
                        pe.wait_ge(k_kept, m)
                    for h in range(RH):
                        r = slice(RD * (h % 2), RD * (h % 2) + RD)
                        last = pe.matmul(ps[:, h % 2, (h // 2) * P:(h // 2 + 1) * P], xT[r, 1, h // 2, tok], xT[r, 0, h // 2, tok],
                                         start=True, stop=True)
                        if h >= RH - 2:
                            last.then_inc(sc_done, 1)
                    for j in range(NP_):
                        last = pe.transpose(ps[:, 2, j * P:(j + 1) * P], xT[:, 1, j, tok], k.ident[:, :])
                    last.then_inc(k_turned, 1)
                    if m < NT - 1:
                        pe.wait_ge(k_kept, m + 1)
                        if m >= 1:
                            pe.wait_ge(st_done, m)
                        for j in range(NP_):
                            last = pe.matmul(ps[:, 3, j * P:(j + 1) * P], kz[:, m, j * P:(j + 1) * P], v[:, m, j * P:(j + 1) * P],
                                             start=True, stop=True)
                        last.then_inc(kv_done, 1)
                for m in range(NT):
                    tok = slice(m * P, (m + 1) * P)
                    pe.wait_ge(s_kept, 2 * (m + 1))
                    if m >= 2:
                        pe.wait_ge(y_kept, m - 1)
                    for h in range(RH):
                        last = pe.matmul(ps[:, 4 + m % 2, h * RD:(h + 1) * RD], s[:, m, h, :], v[:, m, h * RD:(h + 1) * RD],
                                         start=True, stop=True)
                    if m >= 1:
                        pe.wait_ge(st_done, m)
                        for j in range(NP_):
                            last = pe.matmul(ps[:, 6 + m % 2, j * P:(j + 1) * P], xT[:, 0, j, tok], state[:, m - 1, j, :],
                                             start=True, stop=True)
                    last.then_inc(y_in, 1)

            @block.vector
            def _(dve):
                v_ = Chain(dve, chain2)
                pair = tab["pair"][:, :].unsqueeze(1).to_broadcast([P, NP_, P])
                for m in range(NT):
                    for half in range(2):
                        dve.wait_ge(sc_done, 2 * m + half + 1)
                        dve.tensor_tensor(s[:, m, half:RH:2, :], ps[:, half, :].rearrange("p (h q) -> p h q", h=4),
                                          tab["decay"][:, half:RH:2, :], ALU.mult).then_inc(s_kept, 1)
                    dve.wait_ge(k_turned, m + 1)
                    dve.tensor_tensor(kz[:, m, :].rearrange("p (h d) -> p h d", h=RH), ps[:, 2, :].rearrange("p (h d) -> p h d", h=RH),
                                      tab["zeta"][:, :].unsqueeze(2).to_broadcast([P, RH, RD]), ALU.mult).then_inc(k_kept, 1)
                    if m < NT - 1:
                        dve.wait_ge(kv_done, m + 1)
                        ks = ps[:, 3, :].rearrange("p (j c) -> p j c", j=NP_)
                        if m == 0:
                            v_(dve.tensor_tensor(state[:, 0, :, :], ks, pair, ALU.mult))
                        else:
                            v_(dve.tensor_tensor(kv[:, :, :], ks, pair, ALU.mult))
                            v_(dve.tensor_tensor(state[:, m, :, :], state[:, m - 1, :, :],
                                                 tab["chunk_decay"][:, :].unsqueeze(2).to_broadcast([P, NP_, P]), ALU.mult))
                            v_(dve.tensor_tensor(state[:, m, :, :], state[:, m, :, :], kv[:, :, :], ALU.add))
                        dve.sem_inc(st_done, 1)
                heads = lambda a: a.rearrange("p (h d) -> p h d", h=RH)
                for m in range(NT):
                    dve.wait_ge(y_in, m + 1)
                    if m == 0:
                        v_(dve.tensor_copy(y[:, m, :], ps[:, 4, :]))
                    else:
                        v_(dve.tensor_tensor(heads(y[:, m, :]), heads(ps[:, 6 + m % 2, :]),
                                             tab["xi"][:, :].unsqueeze(2).to_broadcast([P, RH, RD]), ALU.mult))
                        v_(dve.tensor_tensor(y[:, m, :], y[:, m, :], ps[:, 4 + m % 2, :], ALU.add))
                    dve.sem_inc(y_kept, 1)
                rows = y[:, :, :].rearrange("p m (h d) -> p (m h) d", h=RH)
                sq = kz[:, :, :].rearrange("p m (h d) -> p (m h) d", h=RH)
                bc = lambda a: a.unsqueeze(2).to_broadcast([P, NT * RH, RD])
                v_(dve.tensor_reduce(st[:, 0, :], rows, AX.X, ALU.add))
                v_(dve.tensor_scalar(st[:, 0, :], st[:, 0, :], 1.0 / RD, None, ALU.mult))
                v_(dve.tensor_tensor(rows, rows, bc(st[:, 0, :]), ALU.subtract))
                v_(dve.tensor_tensor(sq, rows, rows, ALU.mult))
                v_(dve.tensor_reduce(st[:, 1, :], sq, AX.X, ALU.add))
                v_(dve.tensor_scalar(st[:, 1, :], st[:, 1, :], 1.0 / RD, EPS, ALU.mult, ALU.add))
                dve.sem_inc(y_kept, 1)
                dve.wait_ge(y_x, 1)
                v_(dve.reciprocal(st[:, 1, :], st[:, 1, :]))
                v_(dve.tensor_tensor(rows, rows, bc(st[:, 1, :]), ALU.mult))
                v_(dve.tensor_tensor(y[:, :, :], y[:, :, :], g[:, :].unsqueeze(1).to_broadcast([P, NT, RH * RD]), ALU.mult))
                v_(dve.tensor_tensor(y[:, :, :], y[:, :, :], z[:, :, :], ALU.mult))

            @block.scalar
            def _(act):
                act.wait_ge(y_kept, NT + 1)
                act.activation(st[:, 1, :], st[:, 1, :], ACT.Sqrt).then_inc(y_x, 1)
        turn_and_split(k, name, lambda j, m: y[:, m, j * P:(j + 1) * P], *outT)


def build(nc, a, scratch, out):
    ctx = ExitStack()
    with ctx:
        k = Kernel(nc, ctx)

        def keep(stack, name, shape, dt=F32):
            return stack.enter_context(nc.sbuf_tensor(name, shape, dt))

        k.ps = ctx.enter_context(nc.psum_tensor("ps", [P, 8, T], F32))
        k.resid = keep(ctx, "resid", [P, NC_D, T])
        k.ident, k.ones = keep(ctx, "ident_sb", [P, P]), keep(ctx, "ones_sb", [P, P])
        load_constants(k, [(k.ident[:, :], a["c_ident"]), (k.ones[:, :], a["c_ones"])])
        load_residual(k, "in", a["x"])
        groups = lambda d: d.rearrange("(g q p) t -> g p q t", q=4, p=P)
        tokens = lambda d: d.rearrange("(m p) n -> p m n", p=P)
        tiles = lambda d: d.rearrange("(a p) t -> p a t", p=P)

        def pair(stack, name, n):
            return keep(stack, name + "_high", [P, n, T], F32R), keep(stack, name + "_low", [P, n, T], F32R)

        def chunks(x):
            return lambda j, i: tuple(h[:, i * UC:(i + 1) * UC, :] for h in x)

        def units(w, c0=0):
            return lambda j, i: w[:, i * UC:(i + 1) * UC, bass.ds(c0 + j * GW, GW)]

        C_Z, C_AB = 3 * T, 4 * T
        C_QK = C_AB + 4 * DH
        C_AV = C_QK + 2 * NG * AH * P
        C_G = C_AV + NG * AH * P
        pf1, pt1 = scratch("pf1", [3 * T + (C_AV - C_QK) + 2 * D, T]), scratch("pt1", [T, T + NG * AH * P])
        w_in = a["w_in"].rearrange("(c p) n -> p c n", p=P)
        with ExitStack() as s1:
            odn, oda = pair(s1, "odn", DH), pair(s1, "oda", AH)
            with ExitStack() as s2:
                ab = keep(s2, "ab", [P, NT, 4 * DH])
                with ExitStack() as s3:
                    xn = pair(s3, "xn1", NC_D)
                    raw, early = ahead(k, s3, "in1", units(w_in, 0))
                    with nc.sbuf_tensor("tmp1", [P, NC_D, T], F32) as tmp:
                        normalise(k, "mix", k.resid, a["norm_mix"][0], NC_D, tmp, *xn, early=early)
                    fm = lambda g0: lambda j: groups(pf1)[j + g0]
                    tm = lambda c0: lambda j: tokens(pt1)[:, :, bass.ds(c0 + j * GW, GW)]
                    project(k, "in1", [Run(3, units(w_in, 0), chunks(xn), FEATURE, fm(0)), Run(1, units(w_in, C_Z), chunks(xn), TOKEN, tm(0)),
                                       Run(6, units(w_in, C_QK), chunks(xn), FEATURE, fm(3)),
                                       Run(4, units(w_in, C_G), chunks(xn), FEATURE, fm(9)),
                                       Run(3, units(w_in, C_AV), chunks(xn), TOKEN, tm(GW))], raw)
                    narrow(k, "ab", xn, a["w_ab"], slice(0, 4 * DH), ab, turned=True)
                    k.recycle()
                tri, strict = keep(s2, "tri_sb", [P, 2, P]), keep(s2, "strict_sb", [P, 2, P])
                same, level = keep(s2, "same_sb", [P, P]), keep(s2, "level_sb", [P, 2, 6, P])
                load_constants(k, [(tri[:, :, :], a["c_tri"]), (strict[:, :, :], a["c_strict"]), (same[:, :], a["c_same"]),
                                   (level[:, :, :, :], a["c_level"])], "delta_tables")
                qT, kT = keep(s2, "dn_qT", [P, DH, T]), keep(s2, "dn_kT", [P, DH, T])
                v_tok, k_tok = keep(s2, "dn_v", [P, NT, DH, P]), keep(s2, "dn_k", [P, NT, DH, P])
                delta_features(k, "dnf", tiles(pf1)[:, 0:3 * DH, :], a["dn_conv"], a["c_to_row"], a["c_from_row"], qT, kT, v_tok, k_tok)
                delta_rule(k, "dn", ab, a["dn_a_log"], a["dn_dt_bias"], qT, kT, k_tok, v_tok, (tri, strict, same, level),
                           tokens(pt1)[:, :, 0:T], a["dn_out_norm"], odn)
                k.recycle()
            n_qk = 3 * DH
            dilated_attention(k, "da", tiles(pf1)[:, n_qk:n_qk + 2 * NG * AH, :], pt1[:, T:T + NG * AH * P], a["rel_bias"],
                              a["c_hot"], a["c_block"], scratch("bias_rows", [NG * AH * P, ELEN]),
                              scratch("da_o", [NG, T, AH * P]), scratch("da_lse", [NG, T, AH]), oda)
            k.recycle()
            n_g = n_qk + 2 * NG * AH
            w_b1 = [a[n].rearrange("(j p) n -> p j n", p=P) for n in ("w_branch_dn", "w_branch_da")]
            with ExitStack() as s2:
                merged = pair(s2, "merged1", NC_D)
                with nc.sbuf_tensor("merged1_sum", [P, NC_D, T], F32) as total:
                    merge_branches(k, "mg1", [odn, oda], lambda b, g: w_b1[b][:, :, g * GW:(g + 1) * GW],
                                   lambda b, g: tiles(pf1)[:, n_g + b * NC_D + OUTS * g:n_g + b * NC_D + OUTS * (g + 1), :],
                                   total, *merged)
                w_out = units(a["w_out"].rearrange("(c p) n -> p c n", p=P))
                add_product(k, "wo1", merged, lambda b, g: w_out(g, b), NC_D)
                k.recycle()

        with ExitStack() as s1:
            xn = pair(s1, "xn_p", NC_D)
            keyT, gateT = keep(s1, "key_T", [P, 2, T]), keep(s1, "gate_T", [P, T])
            qh, gate_table = scratch("peer_q", [SETS * P, T]), scratch("peer_gates", [NKEY * NKEY, T])
            with ExitStack() as s2:
                wq = units(a["peer_wq"].rearrange("(c p) n -> p c n", p=P))
                raw, early = ahead(k, s2, "pq", wq)
                with nc.sbuf_tensor("tmp_p", [P, NC_D, T], F32) as tmp:
                    normalise(k, "ffn", k.resid, a["norm_ffn"][0], NC_D, tmp, *xn, early=early)
                project(k, "pq", [Run(4, wq, chunks(xn), FEATURE, lambda j: groups(qh)[j])], raw)
            k.recycle()
            peer_route(k, "pr", tiles(qh), a["peer_sub_keys"], a["c_iota"][0:TOPK], keyT, gateT)
            k.recycle()
            peer_gates(k, "pg", keyT, gateT, a["c_iota"], gate_table)
            k.recycle()
            u, v = (d.rearrange("(c p) n -> p c n", p=P) for d in (a["peer_uT"], a["peer_v"]))
            feed_forward(k, "pe", xn, units(u), lambda b, g, i: v[:, bass.ds(b * 8 + i * UC, UC), g * GW:(g + 1) * GW],
                         NKEY * NKEY // D, ACT.Gelu_apprx_tanh, lambda j: tiles(gate_table)[:, bass.ds(j * OUTS, OUTS), :],
                         rolled=True)
            k.recycle()
        with ExitStack() as s1:
            tab = {n: keep(s1, n + "_sb", list(a["c_" + n].shape)) for n in
                   ("rot_r", "rot_m", "causal", "later", "before", "decay", "zeta", "xi", "chunk_decay", "pair")}
            full = lambda t: t[tuple([slice(None)] * len(t.shape))]
            norm_out(k, nc, "nf", a["norm_final"][0], [(full(t), a["c_" + n]) for n, t in tab.items()])
            cos_r, sin_r, cos_m, sin_m = (keep(s1, n, [P, T]) for n in ("cos_r", "sin_r", "cos_m", "sin_m"))
            rope_tables(k, "rope", a["positions_2"], a["c_inv_r"], a["c_inv_m"], cos_r, sin_r, cos_m, sin_m)
            pf2, pt2 = scratch("pf2", [(4 + 6) * GW, T]), scratch("pt2", [T, 3 * GW])
            w_in2 = a["w_in_2"].rearrange("l (c p) n -> l p c n", p=P)
            uq = a["mla_w_uq_2"].rearrange("l (c p) n -> l p c n", p=P)
            ukv = a["mla_w_ukv_2"].rearrange("l (c p) (h x) -> l p c h x", p=P, x=P)
            w_br = a["w_branch_2"].rearrange("l b (j p) n -> l b p j n", p=P)
            w_o2 = a["w_out_2"].rearrange("l (c p) n -> l p c n", p=P)
            w_up = a["w_up_2"].rearrange("l (c p) n -> l p c n", p=P)
            w_dn = a["w_down_2"].rearrange("l (c p) n -> l p c n", p=P)
            C_PE = M_QR + M_KVR
            C_SB = C_PE + M_ROPE
            C_RET = C_SB + 3 * GW
            C_G2 = C_RET + 4 * GW
            k.recycle()
            with nc.Fori(0, 2) as l, ExitStack() as s2:
                ya, yb, yc = (pair(s2, n, 4) for n in ("ya", "yb", "yc"))
                with ExitStack() as s3:
                    cT, peT = keep(s3, "c_T", [P, 5, T]), keep(s3, "pe_T", [QD, T])
                    with ExitStack() as s4:
                        xn = pair(s4, "xn2", NC_D)
                        w_l = w_in2[l]
                        raw, early = ahead(k, s4, "in2", units(w_l, C_SB))
                        with nc.sbuf_tensor("tmp2", [P, NC_D, T], F32) as tmp:
                            normalise(k, "mix2", k.resid, a["norm_mix_g_2"][l], NC_D, tmp, *xn, early=early)
                        fm = lambda g0: lambda j: groups(pf2)[j + g0]
                        tm = lambda c0: lambda j: tokens(pt2)[:, :, bass.ds(c0 + j * GW, GW)]
                        project(k, "in2", [Run(2, units(w_l, C_SB), chunks(xn), FEATURE, fm(0)),
                                           Run(6, units(w_l, C_G2), chunks(xn), FEATURE, fm(4)),
                                           Run(2, units(w_l, C_RET), chunks(xn), FEATURE, fm(2)),
                                           Run(2, units(w_l, C_RET + 2 * GW), chunks(xn), TOKEN, tm(GW)),
                                           Run(1, units(w_l, C_SB + 2 * GW), chunks(xn), TOKEN, tm(0))], raw)
                        project_latent(k, "lat", xn, w_l[:, :, 0:C_PE], cT)
                        narrow(k, "kpe", xn, w_l[:, :, C_PE:C_SB], slice(M_NOPE, QD), peT)
                        k.recycle()
                    with nc.sbuf_tensor("sq3", [P, 3, T], F32) as sq:
                        normalise(k, "nq", cT[:, 0:3, :], a["mla_q_norm_g_2"][l], 3, sq, dst=cT[:, 0:3, :])
                        normalise(k, "nkv", cT[:, 3:5, :], a["mla_kv_norm_g_2"][l], 2, sq, dst=cT[:, 3:5, :])
                    p2 = tiles(pf2)
                    ret_x = keep(s3, "ret_x", [P, 2, RH // 2, T])
                    with ExitStack() as s4:
                        sb_q, sb_k, sb_v = (keep(s4, n, [P, 4, T]) for n in ("sb_q", "sb_k", "sb_v"))
                        latent_attention(k, "mla", cT, peT, uq[l], ukv[l], tab["rot_m"], cos_m, sin_m, tab["causal"], ya,
                                         [(sb_q[:, :, :], p2[:, 0:4, :]), (sb_k[:, :, :], p2[:, 4:8, :]),
                                          (sb_v[:, :, :], tokens(pt2)[:, :, 0:GW]), (ret_x[:, 0, :, :], p2[:, 8:12, :]),
                                          (ret_x[:, 1, :, :], p2[:, 12:16, :])])
                        k.recycle()
                        stick_breaking(k, "sb", sb_q, sb_k, sb_v, tab["later"], tab["before"], yb)
                        k.recycle()
                    retention(k, "ret", ret_x, tokens(pt2)[:, :, GW:2 * GW], tokens(pt2)[:, :, 2 * GW:3 * GW],
                              a["ret_norm_g_2"][l], tab, cos_r, sin_r, yc)
                    k.recycle()
                with ExitStack() as s3:
                    merged = pair(s3, "merged2", NC_D)
                    with nc.sbuf_tensor("merged2_sum", [P, NC_D, T], F32) as total:
                        merge_branches(k, "mg2", [ya, yb, yc], lambda b, g: w_br[l, b][:, :, g * GW:(g + 1) * GW],
                                       lambda b, g: p2[:, 16 + b * NC_D + OUTS * g:16 + b * NC_D + OUTS * (g + 1), :],
                                       total, *merged)
                    w_o = units(w_o2[l])
                    add_product(k, "wo2", merged, lambda b, g: w_o(g, b), NC_D)
                k.recycle()
                s2.close()
                with ExitStack() as s3:
                    xn = pair(s3, "xn3", NC_D)
                    raw, early = ahead(k, s3, "mlp", units(w_up[l]))
                    with nc.sbuf_tensor("tmp3", [P, NC_D, T], F32) as tmp:
                        normalise(k, "nm", k.resid, a["norm_mlp_g_2"][l], NC_D, tmp, *xn, early=early)
                    feed_forward(k, "mlp", xn, units(w_up[l]),
                                 lambda b, g, i: w_dn[l][:, b * 8 + i * UC:b * 8 + (i + 1) * UC, g * GW:(g + 1) * GW],
                                 FF // D, ACT.Relu, raw=raw)
                k.recycle()
        norm_out(k, nc, "ng", a["final_norm_g_2"][0])
        store_final(k, "fin", k.resid, out)


def norm_out(k, nc, name, gain, early=()):
    with nc.sbuf_tensor(name + "_sq", [P, NC_D, T], F32) as sq:
        normalise(k, name, k.resid, gain, NC_D, sq, dst=k.resid, early=early)


def constants():
    hot, blk = bias_tables()
    tri, strict, same, level = delta_tables()
    c = {"ident": np.eye(P, dtype=np.float32), "ones": np.ones((P, P), np.float32), "hot": hot, "block": blk, "tri": tri,
         "strict": strict, "same": same, "level": level, "iota": np.arange(NKEY, dtype=np.float32)}
    rows = np.eye(2 * DH, dtype=np.float32)
    c["to_row"], c["from_row"] = np.tile(rows, (P, 1, 1)), np.repeat(rows[:, :, None], P, axis=2)
    c.update(block2_tables())
    return {"c_" + n: v for n, v in c.items()}


def layout(x, norm_mix, w_in, dn_conv, dn_a_log, dn_dt_bias, dn_out_norm, rel_bias, w_branch_dn, w_branch_da, w_out,
           norm_ffn, peer_wq, peer_sub_keys, peer_u, peer_v, norm_final, positions_2, norm_mix_g_2, w_in_2,
           mla_q_norm_g_2, mla_w_uq_2, mla_kv_norm_g_2, mla_w_ukv_2, ret_norm_g_2, w_branch_2, w_out_2, norm_mlp_g_2,
           w_up_2, w_down_2, final_norm_g_2):
    def gains(g):
        g = np.asarray(g)
        return np.ascontiguousarray(g.reshape(-1, g.shape[-1] // P, P).transpose(0, 2, 1))
    f = lambda v: np.ascontiguousarray(np.asarray(v))
    a = {
        "x": f(x)[0], "norm_mix": gains(norm_mix), "w_in": f(w_in)[0],
        "w_ab": f(f(w_in)[0][:, 4 * T:4 * T + 4 * DH].reshape(NC_D, P, 4 * DH).transpose(1, 0, 2)),
        "dn_conv": f(f(dn_conv)[0].T.reshape(3 * DH, P, 4).transpose(1, 0, 2)),
        "dn_a_log": f(dn_a_log).reshape(2 * DH), "dn_dt_bias": f(dn_dt_bias).reshape(2 * DH),
        "dn_out_norm": f(dn_out_norm)[0], "rel_bias": f(rel_bias), "w_branch_dn": f(w_branch_dn)[0],
        "w_branch_da": f(w_branch_da)[0], "w_out": f(w_out)[0], "norm_ffn": gains(norm_ffn), "peer_wq": f(peer_wq)[0],
        "peer_sub_keys": f(f(peer_sub_keys).reshape(SETS, NKEY, P).transpose(2, 0, 1)),
        "peer_uT": f(f(peer_u)[0].T), "peer_v": f(peer_v)[0], "norm_final": gains(norm_final),
        "positions_2": f(positions_2)[0], "norm_mix_g_2": gains(norm_mix_g_2), "w_in_2": f(w_in_2),
        "mla_q_norm_g_2": gains(mla_q_norm_g_2), "mla_w_uq_2": f(mla_w_uq_2), "mla_kv_norm_g_2": gains(mla_kv_norm_g_2),
        "mla_w_ukv_2": f(mla_w_ukv_2), "ret_norm_g_2": f(ret_norm_g_2), "w_branch_2": f(w_branch_2), "w_out_2": f(w_out_2),
        "norm_mlp_g_2": gains(norm_mlp_g_2), "w_up_2": f(w_up_2), "w_down_2": f(w_down_2), "final_norm_g_2": gains(final_norm_g_2),
    }
    return a


def kernel(**inputs):
    import concourse.bacc as _bacc
    from concourse.bass_utils import run_bass_kernel_spmd as _run

    nc = _bacc.Bacc("TRN2", target_bir_lowering=False, num_devices=1)
    arrays, aps = {}, {}
    for name, v in {**layout(**inputs), **constants()}.items():
        arrays[f"in_{name}"] = v
        aps[name] = nc.dram_tensor(f"in_{name}", v.shape, mybir.dt.from_np(v.dtype), kind="ExternalInput").ap()
    out = nc.dram_tensor("out_0_dram", (T, D), F32, kind="ExternalOutput").ap()
    build(nc, aps, lambda name, shape: nc.dram_tensor("dram_" + name, shape, F32).ap(), out)
    r = _run(nc, [arrays], core_ids=[0])
    return r.results[0]["out_0_dram"].reshape(1, T, D)
```
